# Optimizing a Trainium2 kernel written in Bass

```python
import math
import jax, jax.numpy as jnp
from jax import lax
import numpy as np

D_MODEL = 1024
BATCH = 1
SEQ = 512
DEPTH = 1

CHUNK = 64
D_MIX = D_MODEL
GDN_HEADS = 4
GDN_HEAD_DIM = 128
GDN_WIDTH = GDN_HEADS * GDN_HEAD_DIM
SC_WIDTH = D_MIX - GDN_WIDTH
SC_GROUPS = 8
GDN_CONV = 4
SC_CONV = 3
D_FF = -(-8 * D_MODEL // (3 * 256)) * 256
RMS_EPS = 1e-6
L2_EPS = 1e-6

Q_OFF = 0
K_OFF = GDN_WIDTH
V_OFF = 2 * GDN_WIDTH
Z_OFF = 3 * GDN_WIDTH
A_OFF = 4 * GDN_WIDTH
BETA_OFF = A_OFF + GDN_HEADS
SCB_OFF = BETA_OFF + GDN_HEADS
SCC_OFF = SCB_OFF + SC_WIDTH
SCH_OFF = SCC_OFF + SC_WIDTH
D_IN = SCH_OFF + SC_WIDTH


def rms_norm(x, w):
    x32 = x.astype(jnp.float32)
    y = x32 * lax.rsqrt(jnp.mean(x32 * x32, axis=-1, keepdims=True) + RMS_EPS)
    return (y * w.astype(jnp.float32)).astype(x.dtype)

def l2_normalize(x):
    x32 = x.astype(jnp.float32)
    return x32 * lax.rsqrt(jnp.sum(x32 * x32, axis=-1, keepdims=True) + L2_EPS)

def causal_depthwise_conv(x, w):
    k_width = w.shape[0]
    s = x.shape[1]
    xp = jnp.pad(x, ((0, 0), (k_width - 1, 0), (0, 0)))
    out = xp[:, 0:s] * w[0]
    for j in range(1, k_width):
        out = out + xp[:, j:j + s] * w[j]
    return out

def gated_delta_rule_chunked(q, k, v, g, beta):
    bsz, s, h, dk = q.shape
    dv = v.shape[-1]
    n = s // CHUNK
    f32 = jnp.float32

    def to_chunks(t):
        return t.astype(f32).reshape(bsz, n, CHUNK, h, -1).transpose(0, 3, 1, 2, 4)

    q = to_chunks(q) * (dk ** -0.5)
    k = to_chunks(k)
    v = to_chunks(v)
    g = g.astype(f32).reshape(bsz, n, CHUNK, h).transpose(0, 3, 1, 2)
    beta = beta.astype(f32).reshape(bsz, n, CHUNK, h).transpose(0, 3, 1, 2)
    g = jnp.cumsum(g, axis=-1)

    k_beta = k * beta[..., None]
    v_beta = v * beta[..., None]
    tril = jnp.tril(jnp.ones((CHUNK, CHUNK), dtype=bool))
    strict = jnp.tril(jnp.ones((CHUNK, CHUNK), dtype=bool), -1)
    decay = jnp.exp(jnp.where(tril, g[..., :, None] - g[..., None, :], -jnp.inf))

    lmat = jnp.where(strict, jnp.einsum('bhncd,bhnmd->bhncm', k_beta, k) * decay, 0.0)
    eye = jnp.broadcast_to(jnp.eye(CHUNK, dtype=f32), lmat.shape)
    tmat = lax.linalg.triangular_solve(lmat, eye, left_side=True, lower=True, unit_diagonal=True)

    u = jnp.einsum('bhncm,bhnme->bhnce', tmat, v_beta)
    w = jnp.einsum('bhncm,bhnmd->bhncd', tmat, k_beta * jnp.exp(g)[..., None])
    attn = jnp.where(tril, jnp.einsum('bhncd,bhnmd->bhncm', q, k) * decay, 0.0)
    g_last = g[..., -1]
    k_dec = k * jnp.exp(g_last[..., None] - g)[..., None]
    q_dec = q * jnp.exp(g)[..., None]

    def step(state, inp):
        qd, wi, ui, ai, kd, gl = inp
        v_new = ui - jnp.einsum('bhcd,bhde->bhce', wi, state)
        out = jnp.einsum('bhcd,bhde->bhce', qd, state) + jnp.einsum('bhcm,bhme->bhce', ai, v_new)
        state = state * jnp.exp(gl)[..., None, None] + jnp.einsum('bhcd,bhce->bhde', kd, v_new)
        return state, out

    xs = tuple(jnp.moveaxis(t, 2, 0) for t in (q_dec, w, u, attn, k_dec, g_last))
    state0 = jnp.zeros((bsz, h, dk, dv), dtype=f32)
    _, outs = lax.scan(step, state0, xs)
    return outs.transpose(1, 0, 3, 2, 4).reshape(bsz, s, h, dv)

def hybrid_mixer(h, w_in, conv_qkv_w, a_log, dt_bias, gdn_norm_w, conv_short_w, w_out):
    bsz, s, _ = h.shape
    p = h @ w_in
    qkv = jax.nn.silu(causal_depthwise_conv(p[..., Q_OFF:Z_OFF], conv_qkv_w))
    q = qkv[..., 0:GDN_WIDTH].reshape(bsz, s, GDN_HEADS, GDN_HEAD_DIM)
    k = qkv[..., GDN_WIDTH:2 * GDN_WIDTH].reshape(bsz, s, GDN_HEADS, GDN_HEAD_DIM)
    v = qkv[..., 2 * GDN_WIDTH:3 * GDN_WIDTH].reshape(bsz, s, GDN_HEADS, GDN_HEAD_DIM)
    z = p[..., Z_OFF:A_OFF].reshape(bsz, s, GDN_HEADS, GDN_HEAD_DIM)
    a = p[..., A_OFF:BETA_OFF].astype(jnp.float32)
    b = p[..., BETA_OFF:SCB_OFF].astype(jnp.float32)
    g = -jnp.exp(a_log.astype(jnp.float32)) * jax.nn.softplus(a + dt_bias.astype(jnp.float32))
    beta = jax.nn.sigmoid(b)
    o = gated_delta_rule_chunked(l2_normalize(q), l2_normalize(k), v, g, beta)
    o = rms_norm(o, gdn_norm_w) * jax.nn.silu(z.astype(jnp.float32))
    y_gdn = o.reshape(bsz, s, GDN_WIDTH).astype(h.dtype)
    sc_b = p[..., SCB_OFF:SCC_OFF]
    sc_c = p[..., SCC_OFF:SCH_OFF]
    sc_h = p[..., SCH_OFF:D_IN]
    y_sc = sc_b * causal_depthwise_conv(sc_c * sc_h, conv_short_w)
    return jnp.concatenate([y_gdn, y_sc], axis=-1) @ w_out

def swiglu(h, w_gate, w_up, w_down):
    return (jax.nn.silu(h @ w_gate) * (h @ w_up)) @ w_down

def first_inputs(seed: int = 0) -> dict:
    key = jax.random.key(seed)
    ks = jax.random.split(key, 20)
    f32 = jnp.float32
    nrm = lambda k, shape, scale: jax.random.normal(k, shape, f32) * scale
    dt = jnp.exp(jax.random.uniform(ks[8], (DEPTH, GDN_HEADS), f32, math.log(1e-3), math.log(1e-1)))
    return {
        "x": nrm(ks[0], (BATCH, SEQ, D_MODEL), 1.0),
        "c": nrm(ks[1], (BATCH, D_MODEL), 1.0),
        "w_ada": nrm(ks[2], (DEPTH, D_MODEL, 6 * D_MODEL), 0.5 * D_MODEL ** -0.5),
        "b_ada": nrm(ks[3], (DEPTH, 6 * D_MODEL), 0.02),
        "norm1_w": 1.0 + nrm(ks[4], (DEPTH, D_MODEL), 0.02),
        "w_in": nrm(ks[5], (DEPTH, D_MODEL, D_IN), D_MODEL ** -0.5),
        "conv_qkv_w": nrm(ks[6], (DEPTH, GDN_CONV, 3 * GDN_WIDTH), GDN_CONV ** -0.5),
        "A_log": jnp.log(jax.random.uniform(ks[7], (DEPTH, GDN_HEADS), f32, 1.0, 16.0)),
        "dt_bias": dt + jnp.log(-jnp.expm1(-dt)),
        "gdn_norm_w": 1.0 + nrm(ks[9], (DEPTH, GDN_HEAD_DIM), 0.02),
        "conv_short_w": nrm(ks[10], (DEPTH, SC_CONV, SC_WIDTH), SC_CONV ** -0.5),
        "w_out": nrm(ks[11], (DEPTH, D_MIX, D_MODEL), D_MIX ** -0.5),
        "norm2_w": 1.0 + nrm(ks[12], (DEPTH, D_MODEL), 0.02),
        "w_gate": nrm(ks[13], (DEPTH, D_MODEL, D_FF), D_MODEL ** -0.5),
        "w_up": nrm(ks[14], (DEPTH, D_MODEL, D_FF), D_MODEL ** -0.5),
        "w_down": nrm(ks[15], (DEPTH, D_FF, D_MODEL), D_FF ** -0.5),
        "norm_f_w": 1.0 + nrm(ks[16], (D_MODEL,), 0.02),
    }

def first_block(x, c, w_ada, b_ada, norm1_w, w_in, conv_qkv_w, A_log, dt_bias, gdn_norm_w,
              conv_short_w, w_out, norm2_w, w_gate, w_up, w_down, norm_f_w):
    c_act = jax.nn.silu(c)
    for l in range(DEPTH):
        mod = (c_act @ w_ada[l] + b_ada[l])[:, None, :]
        shift1, scale1, gate1, shift2, scale2, gate2 = jnp.split(mod, 6, axis=-1)
        h = rms_norm(x, norm1_w[l]) * (1.0 + scale1) + shift1
        x = x + gate1 * hybrid_mixer(h, w_in[l], conv_qkv_w[l], A_log[l], dt_bias[l],
                                     gdn_norm_w[l], conv_short_w[l], w_out[l])
        h = rms_norm(x, norm2_w[l]) * (1.0 + scale2) + shift2
        x = x + gate2 * swiglu(h, w_gate[l], w_up[l], w_down[l])
    return rms_norm(x, norm_f_w)


N_META = 16
BLOCK = 128
META_PAD = BLOCK - N_META
HEAD_DIM = 64
SB_HEADS = (D_MODEL // 2) // HEAD_DIM
RWKV_HEADS = (D_MODEL // 2) // HEAD_DIM
SB_WIDTH = SB_HEADS * HEAD_DIM
RWKV_WIDTH = RWKV_HEADS * HEAD_DIM
MIX_WIDTH = SB_WIDTH + RWKV_WIDTH
D_FF_2 = 2816
W_LORA = 32
A_LORA = 32
G_LORA = 96
N_RWKV_COLS = 3 * RWKV_WIDTH + W_LORA + A_LORA + G_LORA
IN_COLS = 3 * SB_WIDTH + N_RWKV_COLS
LNX_EPS = 64e-5


def rms_norm_2(x, g):
    xf = x.astype(jnp.float32)
    y = xf * lax.rsqrt(jnp.mean(xf * xf, axis=-1, keepdims=True) + RMS_EPS)
    return (y * g.astype(jnp.float32)).astype(x.dtype)

def swiglu_2(h, w_gate, w_up, w_down):
    return (jax.nn.silu(h @ w_gate) * (h @ w_up)) @ w_down

def stick_breaking_attention(q, k, v):
    B, L, H, Dh = q.shape
    pad = ((0, 0), (META_PAD, 0), (0, 0), (0, 0))
    q, k, v = [jnp.pad(t, pad).transpose(0, 2, 1, 3) for t in (q, k, v)]
    Lp = L + META_PAD
    nblk = Lp // BLOCK
    key_pos = jnp.arange(Lp)
    scale = Dh ** -0.5
    qb = q.reshape(B, H, nblk, BLOCK, Dh).transpose(2, 0, 1, 3, 4)

    def block(args):
        q_blk, i = args
        q_pos = i * BLOCK + jnp.arange(BLOCK)
        z = jnp.einsum('bhqd,bhkd->bhqk', q_blk, k).astype(jnp.float32) * scale
        valid = (key_pos[None, :] < q_pos[:, None]) & (key_pos[None, :] >= META_PAD)
        log_keep = jnp.where(valid, -jax.nn.softplus(z), 0.0)
        log_rest = lax.cumsum(log_keep, axis=3, reverse=True) - log_keep
        attn = jnp.where(valid, jnp.exp(jax.nn.log_sigmoid(z) + log_rest), 0.0)
        return jnp.einsum('bhqk,bhkd->bhqd', attn.astype(v.dtype), v)

    out = lax.map(block, (qb, jnp.arange(nblk)))
    out = out.transpose(1, 0, 3, 2, 4).reshape(B, Lp, H * Dh)
    return out[:, META_PAD:]

def rwkv7_time_mix(p, mu, w0, w_up, a0, a_up, g_up, k_k, k_a, r_k, lnx_w, lnx_b):
    B, L, _ = p.shape
    C, H, N = RWKV_WIDTH, RWKV_HEADS, HEAD_DIM
    p_prev = jnp.pad(p, ((0, 0), (1, 0), (0, 0)))[:, :-1]
    p = p + (p_prev - p) * mu
    r = p[..., :C]
    k = p[..., C:2 * C]
    v = p[..., 2 * C:3 * C]
    xw = p[..., 3 * C:3 * C + W_LORA]
    xa = p[..., 3 * C + W_LORA:3 * C + W_LORA + A_LORA]
    xg = p[..., 3 * C + W_LORA + A_LORA:]
    w = -jax.nn.softplus(-(w0 + jnp.tanh(xw) @ w_up)) - 0.5
    decay = jnp.exp(-jnp.exp(w.astype(jnp.float32)))
    a = jax.nn.sigmoid(a0 + xa @ a_up)
    g = jax.nn.sigmoid(xg) @ g_up
    kk = (k * k_k).astype(jnp.float32).reshape(B, L, H, N)
    kk = kk / jnp.maximum(jnp.sqrt(jnp.sum(kk * kk, axis=-1, keepdims=True)), 1e-12)
    k = k * (1.0 + (a - 1.0) * k_a)

    rh, kh, vh, ah, dh = [t.astype(jnp.float32).reshape(B, L, H, N) for t in (r, k, v, a, decay)]

    def step(S, inp):
        r_t, w_t, k_t, v_t, kk_t, a_t = inp
        sa = jnp.einsum('bhij,bhj->bhi', S, -kk_t)
        S = (S * w_t[:, :, None, :] + sa[..., None] * (kk_t * a_t)[:, :, None, :]
             + v_t[..., None] * k_t[:, :, None, :])
        return S, jnp.einsum('bhij,bhj->bhi', S, r_t)

    xs = tuple(t.transpose(1, 0, 2, 3) for t in (rh, dh, kh, vh, kk, ah))
    S0 = jnp.zeros((B, H, N, N), jnp.float32)
    _, ys = lax.scan(step, S0, xs)
    y = ys.transpose(1, 0, 2, 3)
    mean = jnp.mean(y, axis=-1, keepdims=True)
    var = jnp.mean(jnp.square(y - mean), axis=-1, keepdims=True)
    y = ((y - mean) * lax.rsqrt(var + LNX_EPS)).reshape(B, L, C)
    y = y * lnx_w.astype(jnp.float32) + lnx_b.astype(jnp.float32)
    bonus = jnp.sum(rh * kh * r_k.astype(jnp.float32), axis=-1, keepdims=True) * vh
    y = y + bonus.reshape(B, L, C)
    return (y * g.astype(jnp.float32)).astype(p.dtype)

def second_inputs(seed: int = 0) -> dict:
    key = jax.random.key(seed)
    ks = jax.random.split(key, 32)
    nrm = lambda k, s: jax.random.normal(k, s, jnp.float32)
    gain = lambda k, s: 1.0 + 0.02 * nrm(k, s)
    Dd = DEPTH
    return {
        "x": nrm(ks[0], (BATCH, SEQ, D_MODEL)),
        "meta_tokens": nrm(ks[1], (N_META, D_MODEL)),
        "ffn1_norm": gain(ks[2], (Dd, D_MODEL)),
        "ffn1_w_gate": nrm(ks[3], (Dd, D_MODEL, D_FF_2)) * D_MODEL ** -0.5,
        "ffn1_w_up": nrm(ks[4], (Dd, D_MODEL, D_FF_2)) * D_MODEL ** -0.5,
        "ffn1_w_down": nrm(ks[5], (Dd, D_FF_2, D_MODEL)) * D_FF_2 ** -0.5,
        "mix_norm": gain(ks[6], (Dd, D_MODEL)),
        "w_in": nrm(ks[7], (Dd, D_MODEL, IN_COLS)) * D_MODEL ** -0.5,
        "rwkv_mu": jax.random.uniform(ks[8], (Dd, N_RWKV_COLS), jnp.float32),
        "rwkv_w0": jax.random.uniform(ks[9], (Dd, RWKV_WIDTH), jnp.float32, -4.0, 1.0),
        "rwkv_w_up": nrm(ks[10], (Dd, W_LORA, RWKV_WIDTH)) * 0.5 * W_LORA ** -0.5,
        "rwkv_a0": 0.5 * nrm(ks[11], (Dd, RWKV_WIDTH)),
        "rwkv_a_up": nrm(ks[12], (Dd, A_LORA, RWKV_WIDTH)) * 0.5 * A_LORA ** -0.5,
        "rwkv_g_up": nrm(ks[13], (Dd, G_LORA, RWKV_WIDTH)) * G_LORA ** -0.5,
        "rwkv_k_k": 0.85 + 0.05 * nrm(ks[14], (Dd, RWKV_WIDTH)),
        "rwkv_k_a": 1.0 + 0.05 * nrm(ks[15], (Dd, RWKV_WIDTH)),
        "rwkv_r_k": 0.1 * nrm(ks[16], (Dd, RWKV_HEADS, HEAD_DIM)),
        "rwkv_lnx_w": gain(ks[17], (Dd, RWKV_WIDTH)),
        "rwkv_lnx_b": 0.02 * nrm(ks[18], (Dd, RWKV_WIDTH)),
        "w_out": nrm(ks[19], (Dd, MIX_WIDTH, D_MODEL)) * MIX_WIDTH ** -0.5,
        "ffn2_norm": gain(ks[20], (Dd, D_MODEL)),
        "ffn2_w_gate": nrm(ks[21], (Dd, D_MODEL, D_FF_2)) * D_MODEL ** -0.5,
        "ffn2_w_up": nrm(ks[22], (Dd, D_MODEL, D_FF_2)) * D_MODEL ** -0.5,
        "ffn2_w_down": nrm(ks[23], (Dd, D_FF_2, D_MODEL)) * D_FF_2 ** -0.5,
        "final_norm": gain(ks[24], (D_MODEL,)),
    }

def second_block(x, meta_tokens, ffn1_norm, ffn1_w_gate, ffn1_w_up, ffn1_w_down, mix_norm, w_in,
              rwkv_mu, rwkv_w0, rwkv_w_up, rwkv_a0, rwkv_a_up, rwkv_g_up, rwkv_k_k, rwkv_k_a,
              rwkv_r_k, rwkv_lnx_w, rwkv_lnx_b, w_out, ffn2_norm, ffn2_w_gate, ffn2_w_up,
              ffn2_w_down, final_norm):
    B = x.shape[0]
    meta = jnp.broadcast_to(meta_tokens[None].astype(x.dtype), (B, N_META, D_MODEL))
    h = jnp.concatenate([meta, x], axis=1)
    for l in range(DEPTH):
        n = rms_norm_2(h, ffn1_norm[l])
        h = h + 0.5 * swiglu_2(n, ffn1_w_gate[l], ffn1_w_up[l], ffn1_w_down[l])
        n = rms_norm_2(h, mix_norm[l])
        proj = n @ w_in[l]
        Bn, L, _ = proj.shape
        q = proj[..., :SB_WIDTH].reshape(Bn, L, SB_HEADS, HEAD_DIM)
        k = proj[..., SB_WIDTH:2 * SB_WIDTH].reshape(Bn, L, SB_HEADS, HEAD_DIM)
        v = proj[..., 2 * SB_WIDTH:3 * SB_WIDTH].reshape(Bn, L, SB_HEADS, HEAD_DIM)
        sb_out = stick_breaking_attention(q, k, v)
        rw_out = rwkv7_time_mix(proj[..., 3 * SB_WIDTH:], rwkv_mu[l], rwkv_w0[l], rwkv_w_up[l],
                                rwkv_a0[l], rwkv_a_up[l], rwkv_g_up[l], rwkv_k_k[l], rwkv_k_a[l],
                                rwkv_r_k[l], rwkv_lnx_w[l], rwkv_lnx_b[l])
        h = h + jnp.concatenate([sb_out, rw_out], axis=-1) @ w_out[l]
        n = rms_norm_2(h, ffn2_norm[l])
        h = h + 0.5 * swiglu_2(n, ffn2_w_gate[l], ffn2_w_up[l], ffn2_w_down[l])
    return rms_norm_2(h, final_norm)[:, N_META:]


def setup_inputs(seed=0):
    out = dict(first_inputs(seed))
    for name, value in second_inputs(seed + 1).items():
        if name != "x":
            out[name + "_2"] = value
    return out


def reference(
    x, c, w_ada, b_ada, norm1_w, w_in, conv_qkv_w, A_log, dt_bias, gdn_norm_w, conv_short_w,
    w_out, norm2_w, w_gate, w_up, w_down, norm_f_w, meta_tokens_2, ffn1_norm_2, ffn1_w_gate_2,
    ffn1_w_up_2, ffn1_w_down_2, mix_norm_2, w_in_2, rwkv_mu_2, rwkv_w0_2, rwkv_w_up_2,
    rwkv_a0_2, rwkv_a_up_2, rwkv_g_up_2, rwkv_k_k_2, rwkv_k_a_2, rwkv_r_k_2, rwkv_lnx_w_2,
    rwkv_lnx_b_2, w_out_2, ffn2_norm_2, ffn2_w_gate_2, ffn2_w_up_2, ffn2_w_down_2, final_norm_2,
):
    x = first_block(
        x, c, w_ada, b_ada, norm1_w, w_in, conv_qkv_w, A_log, dt_bias, gdn_norm_w, conv_short_w,
        w_out, norm2_w, w_gate, w_up, w_down, norm_f_w,
    )
    return second_block(
        x, meta_tokens_2, ffn1_norm_2, ffn1_w_gate_2, ffn1_w_up_2, ffn1_w_down_2, mix_norm_2,
        w_in_2, rwkv_mu_2, rwkv_w0_2, rwkv_w_up_2, rwkv_a0_2, rwkv_a_up_2, rwkv_g_up_2,
        rwkv_k_k_2, rwkv_k_a_2, rwkv_r_k_2, rwkv_lnx_w_2, rwkv_lnx_b_2, w_out_2, ffn2_norm_2,
        ffn2_w_gate_2, ffn2_w_up_2, ffn2_w_down_2, final_norm_2,
    )


_drawn_inputs = setup_inputs


def setup_inputs(seed=0):
    import zlib

    import numpy as np

    out = dict(_drawn_inputs(seed))
    spreads = {}
    factors = {'norm1_w': 4.65,
     'gdn_norm_w': 24.492,
     'norm2_w': 8.0,
     'ffn1_norm_2': 5.991,
     'mix_norm_2': 3.909,
     'rwkv_w_up_2': 4.222,
     'rwkv_k_k_2': 196.776,
     'rwkv_k_a_2': 3.345,
     'rwkv_lnx_w_2': 190.497,
     'rwkv_lnx_b_2': 189.27,
     'ffn2_norm_2': 28.269,
     'final_norm_2': 22.672}
    for name, (base, spread) in spreads.items():
        noise = np.random.default_rng([zlib.crc32(name.encode()), seed]).standard_normal(out[name].shape)
        drawn = base * np.exp(spread * noise) if base else spread * noise
        out[name] = __import__('jax').numpy.asarray(drawn.astype(out[name].dtype))
    for name, factor in factors.items():
        out[name] = (out[name] * factor).astype(out[name].dtype)
    return out
```

```python
import concourse.bass as bass
from concourse import mybir
from contextlib import ExitStack

D = 1024
T1 = 512
NM = 16
T2 = T1 + NM
KT = 8
FT = 22
SLAB = 1024
EPS = 1e-6
KAPPA = 0.6065306597126334
PAD = 48
TP = T2 + PAD
NCH = 9

COLS = {}
_at = 0
for _n, _k in (("c", 8), ("b_ada", 48), ("norm1", 8), ("convq", 48), ("convs", 12), ("gdn", 1), ("norm2", 8),
               ("normf", 8), ("ffn1", 8), ("mix", 8), ("mu", 14), ("w0", 4), ("a0", 4), ("kk", 4), ("ka", 4),
               ("rk", 4), ("lnw", 4), ("lnb", 4), ("ffn2", 8), ("final", 8), ("alog", 1), ("dtb", 1)):
    COLS[_n] = _at
    _at += _k
NCOL = _at

CON = {}
NCON = [0, 0, 0]
for _g, _n, _k in ((0, "ident", 128), (0, "ones", 128), (0, "bones", 128), (0, "b16", 64), (0, "c32", 64), (0, "c64", 64),
                   (1, "madd", 64), (1, "nstrict", 64), (1, "reset1", 512), (1, "sel", 1024),
                   (2, "tri", 128), (2, "m4", 128), (2, "reset2", TP)):
    CON[_n] = (_g, NCON[_g], _k)
    NCON[_g] += _k



class Engine:

    def __init__(self, eng, sem):
        self.eng, self.sem, self.n, self.seen = eng, sem, 0, {}

    def wait(self, marks):
        for sem, n in marks:
            if self.seen.get(sem.name, 0) < n:
                self.eng.wait_ge(sem, n)
                self.seen[sem.name] = n

    def op(self, f, *a, after=(), **k):
        self.wait(after)
        f(*a, **k).then_inc(self.sem, 1)
        self.n += 1
        return (self.sem, self.n)

    def quiet(self, f, *a, after=(), **k):
        self.wait(after)
        f(*a, **k)


class Bank:
    def __init__(self, ap):
        self.ap, self.free = ap, []


def program(nc, xT, metaT, cols, consts, slabs, lup, gup, out):
    f32, f32r = mybir.dt.float32, mybir.dt.float32r
    ALU, ACT = mybir.AluOpType, mybir.ActivationFunctionType
    ve, ae, ge, te, se = nc.vector, nc.scalar, nc.gpsimd, nc.tensor, nc.sync
    top = ExitStack()

    def sem(name):
        return top.enter_context(nc.semaphore(name))

    def sbuf(name, shape, dt=f32, st=top):
        return st.enter_context(nc.sbuf_tensor(name, shape, dt))

    V, A, G, T = Engine(ve, sem("s_v")), Engine(ae, sem("s_a")), Engine(ge, sem("s_g")), Engine(te, sem("s_t"))
    S = Engine(se, sem("s_s"))
    PS = top.enter_context(nc.psum_tensor("PS", [128, 8, 512], f32))
    banks = [Bank(PS[:, i, :]) for i in range(8)]
    pairs = [Bank(PS[:, 2 * i:2 * i + 2, 0:264]) for i in range(4)]
    turn = [0]

    def bank():
        b = banks[turn[0] % 8]
        turn[0] += 1
        after = b.free
        b.free = None
        assert after is not None
        return b, after

    def pair():
        turn[0] += turn[0] % 2
        i = turn[0] % 8
        turn[0] += 2
        after = banks[i].free + banks[i + 1].free
        banks[i].free = banks[i + 1].free = None
        return (i, pairs[i // 2].ap), after

    def free_pair(p, marks):
        banks[p[0]].free = list(marks)
        banks[p[0] + 1].free = list(marks)

    X = sbuf("X", [128, KT, T2])
    HH = sbuf("HH", [128, KT, T2], f32r)
    HL = sbuf("HL", [128, KT, T2], f32r)
    CV = sbuf("CV", [128, NCOL])
    NCV = sbuf("NCV", [128, 8])
    KC = [sbuf("KC", [128, NCON[0]]), None, None]
    MOD = sbuf("MOD", [128, 48])
    SC = sbuf("SC", [128, 16])
    CA = sbuf("CA", [128, 8])
    TRIR = sbuf("TRIR", [128, 128], f32r)
    ONER = sbuf("ONER", [128, 128], f32r)
    RSTD = sbuf("RSTD", [128, T2])
    TMP = [sbuf(f"TMP{i}", [128, T2]) for i in range(3)]

    def col(name, i=0, p0=0, p1=128):
        return CV[p0:p1, COLS[name] + i:COLS[name] + i + 1]

    def con(name, p1=128):
        g, a, k = CON[name]
        return KC[g][0:p1, a:a + k]

    s_in = sem("s_in")
    se.dma_start(CV[:, :], cols).then_inc(s_in, 16)
    loaded = [(s_in, 48)]

    NR, NS = 4, 3
    RAW = [sbuf(f"RAW{i}", [128, SLAB]) for i in range(NR)]
    WH = [sbuf(f"WH{i}", [128, SLAB], f32r) for i in range(NS)]
    WL = [sbuf(f"WL{i}", [128, SLAB], f32r) for i in range(NS)]
    s_raw = [sem(f"s_raw{i}") for i in range(NR)]
    order = []

    def whole(which, n):
        order.extend((which, i, SLAB, which != "ada") for i in range(n))

    order += [("ada", i, SLAB, False) for i in range(16)]
    later = [("ada", i, SLAB, False) for i in range(16, 48)]
    order.append(("ab", 0, 512, True))
    for i in range(28):
        order.append(("w_in", i, SLAB, True))
        order.append(later.pop(0))
    order += later
    whole("w_out", 8)
    for w in ("f0", "f1", "f2"):
        if w == "f2":
            order.append(("lora", 0, SLAB, True))
            order.append(("lora", 1, SLAB, True))
            whole("w_in2", 24)
            whole("w_out2", 8)
        for j in range(FT):
            order.append((w + "g", j, SLAB, True))
            order.append((w + "u", j, SLAB, True))
        for m in range(8):
            for t in range(3):
                order.append((w + "d", 3 * m + t, SLAB if t < 2 else 768, True))
    raw_used = [[] for _ in range(NR)]
    split_used = [[] for _ in range(NS)]
    at = {"load": 0, "split": 0, "use": 0, "nsplit": 0}
    loads = {}
    splits = {}

    def load_next():
        i = at["load"]
        if i >= len(order) or raw_used[i % NR] is None:
            return
        which, j, n, _ = order[i]
        r = i % NR
        S.wait(raw_used[r])
        raw_used[r] = None
        se.dma_start(RAW[r][:, 0:n], slabs[which][j, :, 0:n]).then_inc(s_raw[r], 16)
        loads[i] = (s_raw[r], 16 * (i // NR + 1))
        at["load"] += 1

    def split_next():
        i = at["split"]
        if i >= len(order):
            return
        which, j, n, cut = order[i]
        r = i % NR
        at["split"] += 1
        if not cut:
            return
        s = at["nsplit"] % NS
        at["nsplit"] += 1
        used = split_used[s]
        assert used is not None
        split_used[s] = None
        hi = A.op(ae.activation, WH[s][:, 0:n], RAW[r][:, 0:n], ACT.Copy, after=[loads[i]] + used)
        lo = V.op(ve.tensor_tensor, WL[s][:, 0:n], RAW[r][:, 0:n], WH[s][:, 0:n].bitcast(f32), ALU.subtract,
                  after=[loads[i], hi] + used)
        splits[i] = (s, [hi, lo])
        raw_used[r] = [hi, lo]
        load_next()

    def slab(which, j):
        i = at["use"]
        assert order[i][:2] == (which, j), (order[i], which, j)
        at["use"] += 1
        while at["split"] < min(i + 3, at["load"]) and at["nsplit"] - cut_before(i) < NS:
            split_next()
        return i

    cuts = [0]
    for o in order:
        cuts.append(cuts[-1] + o[3])

    def cut_before(i):
        return cuts[i]

    def gemm(which, j, ps, after, xh, xl, nk, halves, xmarks, m=128, first=True, last=True, k0=0):
        i = slab(which, j)
        s, marks = splits[i]
        T.wait(list(after) + marks + list(xmarks))
        for k in range(nk):
            for w, x, e in ((WH[s], xh, 0), (WH[s], xl, 1), (WL[s], xh, 2)):
                for q, (o, a, b) in enumerate(halves):
                    stop = last and k == nk - 1 and e == 2
                    ins = te.matmul(ps[0:m, q, o:o + b - a] if len(halves) > 1 else ps[0:m, o:o + b - a],
                                    w[:, k * m:k * m + m], x[:, k0 + k, a:b],
                                    start=first and k == 0 and e == 0, stop=stop)
        ins.then_inc(T.sem, 1)
        T.n += 1
        done = (T.sem, T.n)
        split_used[s] = [done]
        return done

    H1 = [(0, NM, T2)]
    H2 = [(0, 0, 264), (0, 264, T2)]

    def two(ap):
        return ap.rearrange("p (a b) -> p a b", a=2)

    def rms(x, wcols, shift, t0, xmarks, free, dst=None):
        n = T2 - t0
        if n == 528:
            p, after = pair()
            pv = p[1]
            views = [(p[1][:, 0, :], 0, 264), (p[1][:, 1, :], 264, 528)]
        else:
            p, after = bank()
            views = [(p.ap[:, 0:n], 0, n)]
            pv = p.ap
        used = [[], [], []]
        for k in range(KT):
            sq = A.op(ae.activation, TMP[k % 3][:, 0:n], x[:, k, t0:T2], ACT.Square, after=xmarks[k] + used[k % 3] + (free if k < 3 else []))
            T.wait([sq] + (after if k == 0 else []))
            for q, (o, a, b) in enumerate(views):
                ins = te.matmul(o, con("ones"), TMP[k % 3][:, a:b], start=(k == 0), stop=(k == KT - 1))
            ins.then_inc(T.sem, 1)
            T.n += 1
            used[k % 3] = [(T.sem, T.n)]
        rv = two(RSTD[:, 0:n]) if n == 528 else RSTD[:, 0:n]
        r1 = A.op(ae.activation, rv, pv, ACT.Sqrt, bias=EPSC[:, 0:1], scale=1.0 / D, after=[(T.sem, T.n), epc] + free)
        if n == 528:
            free_pair(p, [r1])
        else:
            p.free = [r1]
        r2 = V.op(ve.reciprocal, RSTD[:, 0:n], RSTD[:, 0:n], after=[r1])
        res = []
        for k in range(KT):
            if dst is not None:
                res.append([V.op(ve.scalar_tensor_tensor, dst[:, k, t0:T2], x[:, k, t0:T2], wcols[:, k:k + 1],
                                 RSTD[:, 0:n], ALU.mult, ALU.mult, after=[r2] + xmarks[k])])
                continue
            h = V.op(ve.scalar_tensor_tensor, TMP[k % 3][:, 0:n], x[:, k, t0:T2], wcols[:, k:k + 1], RSTD[:, 0:n],
                     ALU.mult, ALU.mult, after=[r2] + used[k % 3])
            if shift is None:
                hi = A.op(ae.activation, HH[:, k, t0:T2], TMP[k % 3][:, 0:n], ACT.Copy, after=[h])
                lo = V.op(ve.tensor_tensor, HL[:, k, t0:T2], TMP[k % 3][:, 0:n], HH[:, k, t0:T2].bitcast(f32),
                          ALU.subtract, after=[hi])
            else:
                hi = A.op(ae.activation, HH[:, k, t0:T2], TMP[k % 3][:, 0:n], ACT.Identity,
                          bias=shift[:, k:k + 1], after=[h])
                lo = V.op(ve.scalar_tensor_tensor, HL[:, k, t0:T2], TMP[k % 3][:, 0:n], shift[:, k:k + 1],
                          HH[:, k, t0:T2].bitcast(f32), ALU.add, ALU.subtract, after=[hi])
            used[k % 3] = [lo]
            res.append([hi, lo])
        return res

    def flat(marks):
        return [x for m in marks for x in m]

    def ffn(name, hm, t0, finish):
        st = ExitStack()
        n = T2 - t0
        IH = sbuf("IH" + name, [128, FT, n], f32r, st)
        IL = sbuf("IL" + name, [128, FT, n], f32r, st)
        halves = H2 if t0 == 0 else H1
        im = []
        used = [[], [], []]
        for j in range(FT):
            ps = []
            for w in "gu":
                if t0 == 0:
                    p, after = pair()
                    d = gemm(name + w, j, p[1], after, HH, HL, KT, halves, flat(hm))
                    ps.append((p, p[1], d))
                else:
                    p, after = bank()
                    d = gemm(name + w, j, p.ap, after, HH, HL, KT, halves, flat(hm))
                    ps.append((p, p.ap, d))
            (pg, g, dg), (pu, u, du) = ps
            b = j % 3
            tv = two(TMP[b][:, 0:n]) if t0 == 0 else TMP[b][:, 0:n]
            a = A.op(ae.activation, tv, g, ACT.Silu, after=[dg] + used[b])
            m = V.op(ve.tensor_tensor, tv, tv, u, ALU.mult, after=[a, du])
            if t0 == 0:
                free_pair(pg, [a])
                free_pair(pu, [m])
            else:
                pg.free, pu.free = [a], [m]
            hi = A.op(ae.activation, IH[:, j, :], TMP[b][:, 0:n], ACT.Copy, after=[m])
            lo = V.op(ve.tensor_tensor, IL[:, j, :], TMP[b][:, 0:n], IH[:, j, :].bitcast(f32), ALU.subtract,
                      after=[hi])
            used[b] = [lo]
            im.append([hi, lo])
        out_marks = []
        hv = [(0, 0, n)] if t0 else H2
        for m in range(8):
            if t0 == 0:
                p, after = pair()
                ps = p[1]
            else:
                p, after = bank()
                ps = p.ap
            for t in range(3):
                nk = 8 if t < 2 else 6
                d = gemm(name + "d", 3 * m + t, ps, after, IH, IL, nk, hv, flat(im[8 * t:8 * t + nk]) if m == 0 else [],
                         first=(t == 0), last=(t == 2), k0=8 * t)
                after = []
            mk = finish(m, ps, d)
            if t0 == 0:
                free_pair(p, [mk])
            else:
                p.free = [mk]
            out_marks.append([mk])
        st.close()
        return out_marks, d

    se.dma_start(KC[0][:, :], consts[:, 0:NCON[0]]).then_inc(s_in, 16)
    se.dma_start(X[:, :, 0:NM], metaT.rearrange("(k p) t -> p k t", p=128)).then_inc(s_in, 16)
    s_x = sem("s_x")
    for _ in range(NR):
        load_next()
    se.dma_start(X[:, :, NM:T2], xT.rearrange("(k p) t -> p k t", p=128)).then_inc(s_x, 16)

    ca = A.op(ae.activation, CA[:, :], CV[:, COLS["c"]:COLS["c"] + 8], ACT.Silu, after=loaded)
    EPSC = sbuf("EPSC", [128, 1])
    epc = G.op(ge.memset, EPSC[:, :], EPS)
    c2 = A.op(ae.activation, ONER[:, :], con("ones"), ACT.Copy)

    ada_bank = [None]

    def ada(j, j0, after):
        i = slab("ada", j)
        r = i % NR
        b = ada_bank[0]
        T.wait([loads[i], ca] + after)
        for k in range(KT):
            ins = te.matmul(b.ap[:, j - j0:j - j0 + 1], RAW[r][:, k * 128:k * 128 + 128], CA[:, k:k + 1],
                            start=(k == 0), stop=(k == KT - 1))
        ins.then_inc(T.sem, 1)
        T.n += 1
        raw_used[r] = [(T.sem, T.n)]
        load_next()
        return (T.sem, T.n)

    ada_bank[0], after = bank()
    for j in range(16):
        d = ada(j, 0, after)
    mod1 = V.op(ve.tensor_tensor, MOD[:, 0:16], ada_bank[0].ap[:, 0:16], CV[:, COLS["b_ada"]:COLS["b_ada"] + 16],
                ALU.add, after=[d] + loaded)
    ada_bank[0].free = [mod1]
    sc1 = V.op(ve.scalar_tensor_tensor, SC[:, 0:8], MOD[:, 8:16], 1.0, CV[:, COLS["norm1"]:COLS["norm1"] + 8],
               ALU.add, ALU.mult, after=[mod1])
    A.wait([sc1])
    T.wait(loaded + [c2])
    V.wait(loaded)
    G.wait(loaded)
    A.wait(loaded)
    hm = rms(X, SC[:, 0:8], MOD[:, 0:8], NM, [[(s_x, 16)]] * KT, [sc1])

    mx = ExitStack()
    KC[1] = sbuf("KC1", [128, NCON[1]], st=mx)
    s_k1 = sem("s_k1")
    se.dma_start(KC[1][:, :], consts[:, NCON[0]:NCON[0] + NCON[1]]).then_inc(s_k1, 16)
    k1 = [(s_k1, 16)]
    QKV = sbuf("QKV", [128, 12, 512], st=mx)
    Z = sbuf("Z", [128, 4, 512], st=mx)
    YS = sbuf("YS", [128, 4, 512], st=mx)
    ROW = sbuf("ROW", [64, 512], st=mx)
    NEA = sbuf("NEA", [4, 1], st=mx)
    stg = ExitStack()
    STG = [sbuf(f"STG{i}", [128, 3 + 512], st=stg) for i in range(2)]
    RT = [sbuf(f"RT{i}", [64, 512], st=stg) for i in range(2)]
    z0 = G.op(ge.memset, STG[0][:, 0:3], 0.0)
    z1 = G.op(ge.memset, STG[1][:, 0:3], 0.0)
    z2 = G.op(ge.memset, ROW[:, :], 0.0)
    hall = flat(hm)

    ada_bank[0] = Bank(None)
    ada_b, ada_after = bank()
    ada_bank[0] = ada_b
    skip = banks.index(ada_b)
    ada_next = [16]

    def more_ada():
        if ada_next[0] < 48:
            d = ada(ada_next[0], 16, ada_after)
            ada_next[0] += 1
            return d

    def bank_in():
        if turn[0] % 8 == skip:
            turn[0] += 1
        return bank()

    p, after = bank_in()
    d = gemm("ab", 0, p.ap, after, HH, HL, KT, H1, hall, m=64)
    tx = V.op(ve.tensor_scalar, RT[0][0:4, :], p.ap[0:4, :], col("dtb", 0, 0, 4), None, ALU.add, after=[d])
    rb = A.op(ae.activation, ROW[32:36, :], p.ap[32:36, :], ACT.Sigmoid, after=[d, z2])
    p.free = [tx, rb]
    ab = A.op(ae.activation, RT[1][0:4, :], RT[0][0:4, :], ACT.Abs, after=[tx])
    ex = A.op(ae.activation, RT[1][0:4, :], RT[1][0:4, :], ACT.Exp, scale=-1.0, after=[ab])
    ln = A.op(ae.activation, RT[1][0:4, :], RT[1][0:4, :], ACT.Ln, bias=1.0, after=[ex])
    nea = A.op(ae.activation, NEA[:, :], col("alog", 0, 0, 4), ACT.Exp)
    sp = V.op(ve.scalar_tensor_tensor, RT[0][0:4, :], RT[0][0:4, :], 0.0, RT[1][0:4, :], ALU.max, ALU.add, after=[ln])
    gg = V.op(ve.tensor_scalar, RT[0][0:4, :], RT[0][0:4, :], NEA[:, 0:1], -1.0, ALU.mult, ALU.mult, after=[sp, nea])
    rg = V.op(ve.tensor_tensor_scan, ROW[0:4, :], con("reset1", 4), RT[0][0:4, :], 0.0, ALU.mult, ALU.add,
              after=[gg, z2] + k1)
    rows = [rb, rg]

    used = [[z0], [z1]]
    tused = [[], [], []]
    qkv = []
    for j in range(12):
        p, after = bank_in()
        d = gemm("w_in", j, p.ap, after, HH, HL, KT, H1, hall)
        more_ada()
        s = STG[j % 2]
        ev = A.op(ae.activation, s[:, 3:515], p.ap, ACT.Copy, after=[d] + used[j % 2])
        p.free = [ev]
        a = TMP[j % 3][:, 0:512]
        m = V.op(ve.tensor_scalar, a, s[:, 0:512], col("convq", j), None, ALU.mult, after=[ev] + tused[j % 3] + used[j % 2])
        for t in range(1, 4):
            m = V.op(ve.scalar_tensor_tensor, a, s[:, t:t + 512], col("convq", 12 * t + j), a, ALU.mult, ALU.add,
                     after=[m])
        si = A.op(ae.activation, QKV[:, j, :], a, ACT.Silu, after=[m])
        used[j % 2] = [m]
        tused[j % 3] = [si]
        qkv.append(si)
    zm = []
    for j in range(4):
        p, after = bank_in()
        d = gemm("w_in", 12 + j, p.ap, after, HH, HL, KT, H1, hall)
        more_ada()
        zm.append(A.op(ae.activation, Z[:, j, :], p.ap, ACT.Silu, after=[d]))
        p.free = [zm[-1]]
    ys = []
    for j in range(4):
        s = STG[j % 2]
        p, after = bank_in()
        d = gemm("w_in", 16 + 3 * j, p.ap, after, HH, HL, KT, H1, hall)
        more_ada()
        c = TMP[j % 3][:, 0:512]
        ev = A.op(ae.activation, c, p.ap, ACT.Copy, after=[d] + tused[j % 3])
        p.free = [ev]
        p, after = bank_in()
        d = gemm("w_in", 17 + 3 * j, p.ap, after, HH, HL, KT, H1, hall)
        more_ada()
        m = V.op(ve.tensor_tensor, s[:, 3:515], c, p.ap, ALU.mult, after=[d, ev] + used[j % 2])
        p.free = [m]
        y = YS[:, j, :]
        m = V.op(ve.tensor_scalar, y, s[:, 1:513], col("convs", j), None, ALU.mult, after=[m])
        for t in (1, 2):
            m = V.op(ve.scalar_tensor_tensor, y, s[:, 1 + t:513 + t], col("convs", 4 * t + j), y, ALU.mult, ALU.add,
                     after=[m])
        used[j % 2] = [m]
        tused[j % 3] = [m]
        p, after = bank_in()
        d = gemm("w_in", 18 + 3 * j, p.ap, after, HH, HL, KT, H1, hall)
        more_ada()
        m = V.op(ve.tensor_tensor, y, y, p.ap, ALU.mult, after=[d, m])
        p.free = [m]
        ys.append(m)
    proj_done = d
    stg.close()
    d = None
    while ada_next[0] < 48:
        d = more_ada()
    mod2 = V.op(ve.tensor_tensor, MOD[:, 16:48], ada_b.ap[:, 0:32], CV[:, COLS["b_ada"] + 16:COLS["b_ada"] + 48],
                ALU.add, after=[d])
    ada_b.free = [mod2]
    sc2 = V.op(ve.scalar_tensor_tensor, SC[:, 8:16], MOD[:, 32:40], 1.0, CV[:, COLS["norm2"]:COLS["norm2"] + 8],
               ALU.add, ALU.mult, after=[mod2])
    cat = [None] * 8
    for j in range(4):
        hi = A.op(ae.activation, HH[:, 4 + j, NM:T2], YS[:, j, :], ACT.Copy, after=[ys[j], proj_done])
        lo = V.op(ve.tensor_tensor, HL[:, 4 + j, NM:T2], YS[:, j, :], HH[:, 4 + j, NM:T2].bitcast(f32), ALU.subtract,
                  after=[hi, proj_done])
        cat[4 + j] = [hi, lo]

    def bc(ap, n):
        return ap.unsqueeze(1).broadcast_to([ap.shape[0], n, ap.shape[1]])

    class Inverse:
        def __init__(self, st, name):
            t = [sbuf(f"{name}{x}", [64, 8, 64], st=st) for x in ("L", "UD", "LD", "U2", "L2", "U4", "L4", "XA", "XB")]
            self.L, self.UD, self.LD, self.U2, self.L2, self.U4, self.L4, self.XA, self.XB = t
            self.done = []

    def products(lhs, rhs, marks, transpose=False):
        p, after = bank()
        T.wait(after + marks)
        o = p.ap[0:64, :].rearrange("p (u t) -> p u t", u=8)
        for u in range(8):
            if transpose:
                ins = te.transpose(o[:, u, :], lhs[:, u, :], con("ident")[0:64, 0:64])
            else:
                ins = te.matmul(o[:, u, :], lhs[:, u, :], rhs[:, u, :], start=True, stop=True)
        ins.then_inc(T.sem, 1)
        T.n += 1
        return p, o, (T.sem, T.n)

    def copied(dst, lhs, rhs, marks, e, transpose=False):
        p, o, d = products(lhs, rhs, marks, transpose)
        if e is A:
            m = A.op(ae.activation, dst, o, ACT.Copy, after=[d])
        else:
            m = V.op(ve.tensor_copy, dst, o, after=[d])
        p.free = [m]
        return m

    def added(dst, base, lhs, rhs, marks):
        p, o, d = products(lhs, rhs, marks)
        m = V.op(ve.tensor_tensor, dst, o, base, ALU.add, after=[d])
        p.free = [m]
        return m

    def invert(w, U, um, X, free):
        i64 = con("ident", 64)[:, 0:64]
        L, UD, LD, U2, L2, U4, L4, XA, XB = w.L, w.UD, w.LD, w.U2, w.L2, w.U4, w.L4, w.XA, w.XB
        l = copied(L[:, :, :], U, None, um + w.done, A, transpose=True)
        ud = V.op(ve.tensor_tensor, UD[:, :, :], U, bc(con("b16", 64), 8), ALU.mult, after=um + w.done)
        ld = V.op(ve.tensor_tensor, LD[:, :, :], L[:, :, :], bc(con("b16", 64), 8), ALU.mult, after=[l])
        xa = V.op(ve.tensor_tensor, XA[:, :, :], UD[:, :, :], bc(i64, 8), ALU.add, after=[ud])
        l2 = copied(L2[:, :, :], UD, LD, [ud, ld], A)
        u2 = copied(U2[:, :, :], LD, UD, [], V)
        xb = added(XB[:, :, :], XA[:, :, :], L2, XA, [l2, xa])
        l4 = copied(L4[:, :, :], U2, L2, [u2, l2], A)
        u4 = copied(U4[:, :, :], L2, U2, [], V)
        xa = added(XA[:, :, :], XB[:, :, :], L4, XB, [l4, xb])
        l8 = copied(L2[:, :, :], U4, L4, [u4, l4], A)
        xb = added(XB[:, :, :], XA[:, :, :], L2, XA, [l8, xa])
        c1 = V.op(ve.tensor_tensor, LD[:, :, :], L[:, :, :], bc(con("c32", 64), 8), ALU.mult, after=[l2, u2])
        y = copied(U2[:, :, :], XB, None, [xb, l4], A, transpose=True)
        z = copied(U4[:, :, :], LD, XB, [c1], V)
        xa = added(XA[:, :, :], XB[:, :, :], U2, U4, [y, z])
        yy = added(L4[:, :, :], U2[:, :, :], U4, U2, [])
        c2 = V.op(ve.tensor_tensor, LD[:, :, :], L[:, :, :], bc(con("c64", 64), 8), ALU.mult, after=[z])
        z = copied(U2[:, :, :], LD, XA, [c2, xa, yy], A)
        p, o, d = products(L4, U2, [z])
        m = V.op(ve.tensor_tensor, X, o, XA[:, :, :], ALU.add, after=[d] + free)
        p.free = [m]
        w.done = [m]
        return m

    KB = sbuf("KB", [128, 4, 128], st=mx)
    QD = YS
    DC = sbuf("DC", [64, 8, 4, 64], st=mx)
    COLT = sbuf("COLT", [64, 8, 64], st=mx)
    EGC = sbuf("EGC", [64, 8, 4], st=mx)
    BEG = sbuf("BEG", [64, 8, 4], st=mx)
    KDC = sbuf("KDC", [64, 8, 4], st=mx)
    GL = sbuf("GL", [128, 8, 4], st=mx)
    EGL = sbuf("EGL", [128, 8, 4], st=mx)
    p, after = bank()
    T.wait(after + rows)
    o = p.ap[0:64, :].rearrange("p (u t) -> p u t", u=8)
    for n in range(8):
        ins = te.transpose(o[:, n, :], ROW[:, 64 * n:64 * n + 64], con("ident")[0:64, 0:64])
    ins.then_inc(T.sem, 1)
    T.n += 1
    ct = V.op(ve.tensor_copy, COLT[:, :, :], o, after=[(T.sem, T.n)])
    p.free = [ct]
    eg = A.op(ae.activation, EGC[:, :, :], COLT[:, :, 0:4], ACT.Exp, after=[ct])
    bg = V.op(ve.tensor_tensor, BEG[:, :, :], EGC[:, :, :], COLT[:, :, 32:36], ALU.mult, after=[eg])
    for j in range(8):
        t = TMP[j % 3][:, 0:512]
        sq = A.op(ae.activation, t, QKV[:, j, :], ACT.Square, after=[qkv[j]] + tused[j % 3])
        p, after = bank()
        mm = T.op(te.matmul, p.ap, con("ones"), t, start=True, stop=True, after=after + [sq])
        r = A.op(ae.activation, t, p.ap, ACT.Sqrt, bias=EPSC[:, 0:1], after=[mm])
        p.free = [r]
        r = V.op(ve.reciprocal, t, t, after=[r])
        qkv[j] = V.op(ve.scalar_tensor_tensor, QKV[:, j, :], QKV[:, j, :], 128.0 ** -0.5 if j < 4 else 1.0, t,
                      ALU.mult, ALU.mult, after=[r])
        tused[j % 3] = [qkv[j]]
    qd, dm = [], []
    DH = DC[:, :, :, :]
    for h in range(4):
        p, after = bank()
        mm = T.op(te.matmul, p.ap, con("sel", 64)[:, 128 * h:128 * h + 128], ROW[:, :], start=True, stop=True,
                  after=after + rows + k1)
        gv = p.ap.rearrange("p (n t) -> p n t", n=8)
        m1 = V.op(ve.tensor_tensor, DH[:, :, h, :], gv[0:64],
                  COLT[:, :, h:h + 1].broadcast_to([64, 8, 64]), ALU.subtract, after=[mm, ct])
        m2 = V.op(ve.tensor_tensor, DH[:, :, h, :], DH[:, :, h, :], bc(con("madd", 64), 8), ALU.add, after=[m1] + k1)
        gl = V.op(ve.tensor_copy, GL[:, :, h:h + 1], gv[:, :, 63:64], after=[mm])
        dm.append(A.op(ae.activation, DH[:, :, h, :], DH[:, :, h, :], ACT.Exp, after=[m2]))
        t = TMP[h % 3][:, 0:512]
        eg2 = A.op(ae.activation, t, p.ap, ACT.Exp, after=[m1, gl] + tused[h % 3])
        p.free = [m1, gl, eg2]
        qd.append(V.op(ve.tensor_tensor, QD[:, h, :], QKV[:, h, :], t, ALU.mult, after=[eg2, qkv[h]] + cat[4 + h]))
        tused[h % 3] = [qd[-1]]
    egl = A.op(ae.activation, EGL[:, :, :], GL[:, :, :], ACT.Exp, after=[gl])
    kd0 = V.op(ve.tensor_tensor, KDC[:, :, :], GL[0:64, :, :], COLT[:, :, 0:4], ALU.subtract, after=[gl, ct])
    kdc = A.op(ae.activation, KDC[:, :, :], KDC[:, :, :], ACT.Exp, after=[kd0])

    inv = Inverse(mx, "iv")
    UU = sbuf("UU", [64, 8, 64], st=mx)
    AT = sbuf("AT", [64, 8, 64], st=mx)
    XX = sbuf("XX", [64, 8, 64], st=mx)
    KBT = sbuf("KBT", [64, 8, 128], st=mx)
    KDT = sbuf("KDT", [64, 8, 128], st=mx)
    VBT = sbuf("VBT", [64, 8, 128], st=mx)
    UT = VBT
    WT = sbuf("WT", [128, 8, 64], st=mx)
    VN = sbuf("VN", [64, 4, 128], st=mx)
    ST = sbuf("ST", [128, 4, 128], st=mx)
    OG = QKV
    sm = [G.op(ge.memset, ST[:, :, :], 0.0)]
    prev_scan = []
    kbused = []
    og = []
    qkvT = list(qkv)
    for b in range(4):
        p, after = bank()
        T.wait(after + rows + k1)
        for h in range(4):
            ins = te.matmul(p.ap[:, 128 * h:128 * h + 128], con("sel", 64)[:, 128 * (4 + h):128 * (4 + h) + 128],
                            ROW[:, 128 * b:128 * b + 128], start=True, stop=True)
        ins.then_inc(T.sem, 1)
        T.n += 1
        kb = V.op(ve.tensor_tensor, KB[:, :, :], QKV[:, 4:8, 128 * b:128 * b + 128],
                  p.ap.rearrange("p (h t) -> p h t", h=4), ALU.mult, after=[(T.sem, T.n)] + qkvT + kbused)
        p.free = [kb]
        pk, after1 = bank()
        pq, after2 = bank()
        T.wait(after1 + after2 + qkvT + [kb])
        for u in range(8):
            c, h = divmod(u, 4)
            t0 = 64 * (2 * b + c)
            te.matmul(pk.ap[0:64, 64 * u:64 * u + 64], QKV[:, 4 + h, t0:t0 + 64], KB[:, h, 64 * c:64 * c + 64],
                      start=True, stop=True)
            ins = te.matmul(pq.ap[0:64, 64 * u:64 * u + 64], QKV[:, 4 + h, t0:t0 + 64], QKV[:, h, t0:t0 + 64],
                            start=True, stop=True)
        ins.then_inc(T.sem, 1)
        T.n += 1
        d = (T.sem, T.n)
        kbused = [d]
        db = DC[:, 2 * b:2 * b + 2, :, :].rearrange("p c h t -> p (c h) t")
        v8 = lambda ap: ap[0:64, :].rearrange("p (u t) -> p u t", u=8)
        u1 = V.op(ve.tensor_tensor, UU[:, :, :], v8(pk.ap), db, ALU.mult, after=[d] + dm + inv.done)
        um = V.op(ve.tensor_tensor, UU[:, :, :], UU[:, :, :], bc(con("nstrict", 64), 8), ALU.mult, after=[u1])
        atm = V.op(ve.tensor_tensor, AT[:, :, :], v8(pq.ap), db, ALU.mult, after=[d] + prev_scan)
        pk.free, pq.free = [u1], [atm]
        tk = []
        for c in range(2):
            n = 2 * b + c
            pk, after1 = bank()
            pv, after2 = bank()
            T.wait(after1 + after2)
            for h in range(4):
                te.transpose(pk.ap[0:64, 128 * h:128 * h + 128], QKV[:, 4 + h, 64 * n:64 * n + 64], con("ident"))
                ins = te.transpose(pv.ap[0:64, 128 * h:128 * h + 128], QKV[:, 8 + h, 64 * n:64 * n + 64], con("ident"))
            ins.then_inc(T.sem, 1)
            T.n += 1
            d = (T.sem, T.n)
            k4 = pk.ap[0:64, :].rearrange("p (h t) -> p h t", h=4)
            v4 = pv.ap[0:64, :].rearrange("p (h t) -> p h t", h=4)

            def cb(ap):
                return ap.unsqueeze(2).broadcast_to([64, 4, 128])

            m1 = V.op(ve.tensor_tensor, KBT[:, 4 * c:4 * c + 4, :], k4, cb(BEG[:, n, :]), ALU.mult, after=[d, bg] + prev_scan)
            m2 = V.op(ve.tensor_tensor, KDT[:, 4 * c:4 * c + 4, :], k4, cb(KDC[:, n, :]), ALU.mult, after=[d, kdc] + prev_scan)
            m3 = V.op(ve.tensor_tensor, VBT[:, 4 * c:4 * c + 4, :], v4, cb(COLT[:, n, 32:36]), ALU.mult, after=[d] + prev_scan)
            pk.free, pv.free = [m1, m2], [m3]
            tk += [m1, m2, m3]
        xm = invert(inv, UU[:, :, :], [um], XX[:, :, :], prev_scan)
        ums = []
        for c in range(2):
            p, after = bank()
            T.wait(after + tk + [xm])
            for h in range(4):
                ins = te.matmul(p.ap[0:64, 128 * h:128 * h + 128], XX[:, 4 * c + h, :], VBT[:, 4 * c + h, :],
                                start=True, stop=True)
            ins.then_inc(T.sem, 1)
            T.n += 1
            ums.append(A.op(ae.activation, UT[:, 4 * c:4 * c + 4, :], p.ap[0:64, :].rearrange("p (h t) -> p h t", h=4),
                            ACT.Copy, after=[(T.sem, T.n)] + prev_scan))
            p.free = [ums[-1]]
        p, after = bank()
        T.wait(after)
        for u in range(8):
            ins = te.matmul(p.ap[:, 64 * u:64 * u + 64], KBT[:, u, :], XX[:, u, :], start=True, stop=True)
        ins.then_inc(T.sem, 1)
        T.n += 1
        wt = V.op(ve.tensor_copy, WT[:, :, :], p.ap.rearrange("p (u t) -> p u t", u=8), after=[(T.sem, T.n)])
        p.free = [wt]
        for c in range(2):
            n = 2 * b + c
            p, after = bank()
            T.wait(after + [wt] + sm)
            for h in range(4):
                ins = te.matmul(p.ap[0:64, 128 * h:128 * h + 128], WT[:, 4 * c + h, :], ST[:, h, :], start=True, stop=True)
            ins.then_inc(T.sem, 1)
            T.n += 1
            vn = V.op(ve.tensor_tensor, VN[:, :, :], UT[:, 4 * c:4 * c + 4, :],
                      p.ap[0:64, :].rearrange("p (h t) -> p h t", h=4), ALU.subtract, after=[(T.sem, T.n), ums[c]] + prev_scan)
            p.free = [vn]
            p, after = bank()
            T.wait(after + qd + [atm])
            for h in range(4):
                te.matmul(p.ap[:, 64 * h:64 * h + 64], ST[:, h, :], QD[:, h, 64 * n:64 * n + 64], start=True, stop=False)
                T.wait([vn])
                ins = te.matmul(p.ap[:, 64 * h:64 * h + 64], VN[:, h, :], AT[:, 4 * c + h, :], start=False, stop=True)
            ins.then_inc(T.sem, 1)
            T.n += 1
            od = (T.sem, T.n)
            om = A.op(ae.activation, OG[:, 0:4, 64 * n:64 * n + 64], p.ap[:, 0:256].rearrange("p (h t) -> p h t", h=4),
                      ACT.Copy, after=[od])
            p.free = [om]
            og.append(om)
            p, after = bank()
            T.wait(after)
            for h in range(4):
                ins = te.matmul(p.ap[:, 128 * h:128 * h + 128], KDT[:, 4 * c + h, :], VN[:, h, :], start=True, stop=True)
            ins.then_inc(T.sem, 1)
            T.n += 1
            sd = (T.sem, T.n)
            sm = []
            for h in range(4):
                sm.append(V.op(ve.scalar_tensor_tensor, ST[:, h, :], ST[:, h, :], EGL[:, n, h:h + 1],
                               p.ap[:, 128 * h:128 * h + 128], ALU.mult, ALU.add, after=[sd, od, egl]))
            p.free = [sm[-1]]
            prev_scan = [sd]
    for h in range(4):
        t = TMP[h % 3][:, 0:512]
        sq = A.op(ae.activation, t, OG[:, h, :], ACT.Square, after=[og[-1]] + tused[h % 3])
        p, after = bank()
        mm = T.op(te.matmul, p.ap, con("ones"), t, start=True, stop=True, after=after + [sq])
        r = A.op(ae.activation, t, p.ap, ACT.Sqrt, bias=EPSC[:, 0:1], scale=1.0 / 128, after=[mm])
        p.free = [r]
        r = V.op(ve.reciprocal, t, t, after=[r])
        y = V.op(ve.scalar_tensor_tensor, t, OG[:, h, :], col("gdn"), t, ALU.mult, ALU.mult, after=[r])
        y = V.op(ve.tensor_tensor, t, t, Z[:, h, :], ALU.mult, after=[y, zm[h]])
        hi = A.op(ae.activation, HH[:, h, NM:T2], t, ACT.Copy, after=[y, proj_done])
        lo = V.op(ve.tensor_tensor, HL[:, h, NM:T2], t, HH[:, h, NM:T2].bitcast(f32), ALU.subtract, after=[hi])
        tused[h % 3] = [lo]
        cat[h] = [hi, lo]
    xm = []
    for m in range(8):
        p, after = bank()
        d = gemm("w_out", m, p.ap, after, HH, HL, KT, H1, flat(cat))
        xm.append([V.op(ve.scalar_tensor_tensor, X[:, m, NM:T2], p.ap, MOD[:, 16 + m:17 + m], X[:, m, NM:T2], ALU.mult,
                        ALU.add, after=[d, mod2])])
        p.free = [xm[-1][0]]
    mx.close()

    hm = rms(X, SC[:, 8:16], MOD[:, 24:32], NM, xm, [sc2, d] + flat(cat))

    def fin1(m, ps, d):
        return V.op(ve.scalar_tensor_tensor, X[:, m, NM:T2], ps, MOD[:, 40 + m:41 + m], X[:, m, NM:T2],
                    ALU.mult, ALU.add, after=[d])

    xm, d = ffn("f0", hm, NM, fin1)
    xm = rms(X, CV[:, COLS["normf"]:COLS["normf"] + 8], None, NM, xm, [d], dst=X)

    xm = [m + loaded for m in xm]

    def fin2(t0):
        def f(m, ps, d):
            n = T2 - t0
            xv = two(X[:, m, 0:n]) if t0 == 0 else X[:, m, t0:T2]
            return V.op(ve.scalar_tensor_tensor, xv, ps, 0.5, xv, ALU.mult, ALU.add, after=[d])
        return f

    hm = rms(X, CV[:, COLS["ffn1"]:COLS["ffn1"] + 8], None, 0, xm, [d])
    xm, d = ffn("f1", hm, 0, fin2(0))
    hm = rms(X, CV[:, COLS["mix"]:COLS["mix"] + 8], None, 0, xm, [d])
    hall = flat(hm)

    rw = ExitStack()
    BON = sbuf("BON", [128, 4, 512], st=rw)
    rk = ExitStack()
    KC[2] = sbuf("KC2", [128, NCON[2]], st=rk)
    LUP = sbuf("LUP", [64, 512], st=rk)
    GUP = sbuf("GUP", [96, 512], st=rk)
    s_k2 = sem("s_k2")
    S.wait(hall)
    a2 = NCON[0] + NCON[1]
    se.dma_start(KC[2][:, :], consts[:, a2:a2 + NCON[2]]).then_inc(s_k2, 16)
    se.dma_start(LUP[:, :], lup).then_inc(s_k2, 16)
    se.dma_start(GUP[:, :], gup).then_inc(s_k2, 16)
    k2 = [(s_k2, 48)]
    XG = sbuf("XG", [96, T2], st=rk)
    VB = sbuf("VB", [128, 4, 64 + TP], st=rk)
    AR = sbuf("AR", [128, 4, NCH, 2, 64], st=rk)
    BK = sbuf("BK", [128, 4, NCH, 2, 64], st=rk)
    WCC = sbuf("WCC", [128, 4, NCH], st=rk)
    KAM = sbuf("KAM", [128, 4], st=rk)
    el = ExitStack()
    LX = sbuf("LX", [64, T2], st=el)
    SG = [sbuf(f"SG{i}", [128, 1 + TP], st=el) for i in range(2)]
    R1, K1, SW, SA, CS, KK, EX = (sbuf(n, [128, TP], st=el) for n in ("R1", "K1", "SW", "SA", "CS", "KK", "EX"))
    zr = [G.op(ge.memset, t[:, 0:PAD + 1], 0.0, after=hall) for t in SG]
    zr += [G.op(ge.memset, t[:, 0:PAD], 0.0) for t in (SW, SA)]
    zr.append(G.op(ge.memset, VB[:, :, 0:64], 0.0))
    V.wait(zr)
    A.wait(zr)
    c1 = A.op(ae.activation, TRIR[:, :], con("tri"), ACT.Copy, after=k2)
    kam = V.op(ve.tensor_scalar, KAM[:, :], CV[:, COLS["ka"]:COLS["ka"] + 4], -1.0, 1.0, ALU.mult, ALU.add)

    sgused = [[], []]
    nst = [0]

    def shifted(which, j, dst, mucol, rows, dused):
        b = nst[0] % 2
        nst[0] += 1
        s = SG[b]
        p, after = pair()
        d = gemm(which, j, p[1], after, HH, HL, KT, H2, hall)
        ev = A.op(ae.activation, two(s[:, 1 + PAD:1 + TP]), p[1], ACT.Copy, after=[d] + sgused[b])
        free_pair(p, [ev])
        df = V.op(ve.tensor_tensor, dst[0:rows], s[0:rows, 0:TP], s[0:rows, 1:1 + TP], ALU.subtract,
                  after=[ev] + dused)
        m = V.op(ve.scalar_tensor_tensor, dst[0:rows], dst[0:rows], col("mu", mucol, 0, rows), s[0:rows, 1:1 + TP],
                 ALU.mult, ALU.add, after=[df])
        sgused[b] = [m]
        return m

    m = shifted("lora", 0, R1[:, :], 12, 64, [])
    lx1 = A.op(ae.activation, LX[0:32, :], R1[0:32, PAD:TP], ACT.Tanh, after=[m])
    lx2 = A.op(ae.activation, LX[32:64, :], R1[32:64, PAD:TP], ACT.Copy, after=[m])
    m = shifted("lora", 1, K1[:, :], 13, 96, [])
    xg = A.op(ae.activation, XG[:, :], K1[0:96, PAD:TP], ACT.Sigmoid, after=[m])
    used = {x: [] for x in ("R1", "K1", "SW", "SA", "CS", "KK", "EX")}
    used["R1"], used["K1"] = [lx1, lx2], [xg]
    feats, vmarks, bonm, wcm = [], [], [], []

    def ch(ap):
        return ap.rearrange("p (n t) -> p n t", t=64)

    for i in range(4):
        for dst, r0, bias, nm in ((SW, 0, "w0", "SW"), (SA, 32, "a0", "SA")):
            p, after = pair()
            T.wait(after + [lx1, lx2] + k2)
            for q in range(2):
                ins = te.matmul(p[1][:, q, :], LUP[r0:r0 + 32, 128 * i:128 * i + 128],
                                LX[r0:r0 + 32, 264 * q:264 * q + 264], start=True, stop=True)
            ins.then_inc(T.sem, 1)
            T.n += 1
            sg = A.op(ae.activation, two(dst[:, PAD:TP]), p[1], ACT.Sigmoid, bias=col(bias, i),
                      after=[(T.sem, T.n)] + used[nm])
            free_pair(p, [sg])
            if nm == "SW":
                sw = sg
            else:
                sa = sg
        r1 = shifted("w_in2", 3 * i, R1[:, :], i, 128, used["R1"])
        k1m = shifted("w_in2", 3 * i + 1, K1[:, :], 4 + i, 128, used["K1"])
        vm = shifted("w_in2", 3 * i + 2, VB[:, i, 64:64 + TP], 8 + i, 128, [])
        vmarks.append(vm)
        cs = V.op(ve.tensor_tensor_scan, CS[:, :], con("reset2"), SW[:, :], 0.0, ALU.mult, ALU.add,
                  after=[sw] + k2 + used["CS"])
        e1 = A.op(ae.activation, EX[:, :], CS[:, :], ACT.Exp, scale=-KAPPA, after=[cs] + used["EX"])
        f1 = V.op(ve.tensor_tensor, AR[:, i, :, 1, :], ch(R1[:, :]), ch(EX[:, :]), ALU.mult, after=[e1, r1])
        wc = V.op(ve.tensor_copy, WCC[:, i, :], ch(EX[:, :])[:, :, 63], after=[e1])
        wcm.append(wc)
        dcs = V.op(ve.tensor_tensor, SW[:, :], CS[:, :], SW[:, :], ALU.subtract, after=[cs])
        e1p = A.op(ae.activation, SW[:, :], SW[:, :], ACT.Exp, scale=-KAPPA, after=[dcs])
        kk = V.op(ve.tensor_scalar, KK[:, :], K1[:, :], col("kk", i), None, ALU.mult, after=[k1m] + used["KK"])
        sq = A.op(ae.activation, EX[:, :], KK[:, :], ACT.Square, after=[kk, f1, wc])
        p, after = pair()
        T.wait(after + [sq])
        pv = PS[:, p[0]:p[0] + 2, 0:288]
        for q in range(2):
            ins = te.matmul(pv[:, q, :], con("bones"), EX[:, 288 * q:288 * q + 288], start=True, stop=True)
        ins.then_inc(T.sem, 1)
        T.n += 1
        mxm = V.op(ve.tensor_scalar, two(EX[:, :]), pv, 1e-24, None, ALU.max, after=[(T.sem, T.n)])
        free_pair(p, [mxm])
        sr = A.op(ae.activation, EX[:, :], EX[:, :], ACT.Sqrt, after=[mxm])
        rc = V.op(ve.reciprocal, EX[:, :], EX[:, :], after=[sr])
        kn = V.op(ve.tensor_tensor, KK[:, :], KK[:, :], EX[:, :], ALU.mult, after=[rc])
        e2 = A.op(ae.activation, EX[:, :], CS[:, :], ACT.Exp, scale=KAPPA, after=[kn])
        f2 = V.op(ve.scalar_tensor_tensor, AR[:, i, :, 0, :], ch(KK[:, :]), -1.0, ch(SW[:, :]), ALU.mult,
                  ALU.mult, after=[kn, e1p])
        bm = V.op(ve.tensor_tensor, KK[:, :], KK[:, :], SA[:, :], ALU.mult, after=[f2, sa])
        f3 = V.op(ve.tensor_tensor, BK[:, i, :, 0, :], ch(KK[:, :]), ch(EX[:, :]), ALU.mult, after=[bm, e2])
        tm = V.op(ve.tensor_scalar, SA[:, :], SA[:, :], col("ka", i), KAM[:, i:i + 1], ALU.mult, ALU.add,
                  after=[bm, kam])
        kf = V.op(ve.tensor_tensor, K1[:, :], K1[:, :], SA[:, :], ALU.mult, after=[tm, kk])
        f4 = V.op(ve.tensor_tensor, BK[:, i, :, 1, :], ch(K1[:, :]), ch(EX[:, :]), ALU.mult, after=[kf, e2])
        bo = V.op(ve.scalar_tensor_tensor, K1[:, 64:TP], R1[:, 64:TP], col("rk", i), K1[:, 64:TP], ALU.mult,
                  ALU.mult, after=[kf, r1, f4])
        p, after = bank()
        mm = T.op(te.matmul, p.ap, con("bones"), K1[:, 64:TP], start=True, stop=True, after=after + [bo])
        bonm.append(V.op(ve.tensor_tensor, BON[:, i, :], VB[:, i, 128:64 + TP], p.ap, ALU.mult, after=[mm, vm]))
        p.free = [bonm[-1]]
        used = {"R1": [f1, bo], "K1": [f4, mm], "SW": [f2], "SA": [kf], "CS": [e2, dcs], "KK": [f3], "EX": [f4]}
        feats.append([f1, f2, f3, f4])
    el.close()

    ck = ExitStack()
    inv = Inverse(ck, "rv")
    MM = sbuf("MM", [128, 8, 128], st=ck)
    XX = sbuf("RX", [64, 8, 64], st=ck)
    V0 = sbuf("V0", [128, 8, 64], st=ck)
    SV = sbuf("SV", [128, 8, 64], st=ck)
    BKT = sbuf("BKT", [128, 8, 64], st=ck)
    RH = sbuf("RH", [64, 8, 64], st=ck)
    SB = sbuf("SB", [128, 4, 2, 64], st=ck)
    z1 = G.op(ge.memset, V0[0:64, :, :], 0.0, after=flat(feats) + bonm)
    sm = [G.op(ge.memset, SB[:, :, :, :], 0.0)]
    scan = []
    mmused = []
    y_marks = []
    for n in range(NCH):
        banks2 = [bank() for _ in range(2)]
        T.wait(banks2[0][1] + banks2[1][1] + flat(feats) + [z1])
        for h in range(8):
            i, par = divmod(h, 2)
            pb = 64 * par
            ins = te.matmul(banks2[par][0].ap[:, 128 * i:128 * i + 128],
                            BK[pb:pb + 64, i, n, :, :].rearrange("p a t -> p (a t)"),
                            AR[pb:pb + 64, i, n, :, :].rearrange("p a t -> p (a t)"), start=True, stop=True)
        ins.then_inc(T.sem, 1)
        T.n += 1
        d = (T.sem, T.n)
        M2 = MM[:, :, :].rearrange("p (i a) t -> p i a t", a=2)
        mms = []
        for par in range(2):
            p = banks2[par][0]
            m = V.op(ve.tensor_tensor, M2[:, :, par, :], p.ap.rearrange("p (i t) -> p i t", i=4),
                     con("m4").unsqueeze(1).broadcast_to([128, 4, 128]), ALU.mult, after=[d] + scan)
            p.free = [m]
            mms.append(m)
        pk, after1 = bank()
        pv, after2 = bank()
        T.wait(after1 + after2 + vmarks)
        for i in range(4):
            te.transpose(pk.ap[:, 128 * i:128 * i + 128], BK[:, i, n, :, :].rearrange("p a t -> p (a t)"),
                         con("ident"))
            ins = te.transpose(pv.ap[:, 128 * i:128 * i + 128], VB[:, i, 64 * n:64 * n + 128], con("ident"))
        ins.then_inc(T.sem, 1)
        T.n += 1
        d = (T.sem, T.n)
        v8 = pv.ap[64:128, :].rearrange("p (h t) -> p h t", h=8)
        bt = A.op(ae.activation, BKT[:, :, :], pk.ap.rearrange("p (h t) -> p h t", h=8), ACT.Copy, after=[d] + scan)
        v0 = A.op(ae.activation, V0[64:128, :, :], v8, ACT.Copy, after=[d] + scan)
        v1 = A.op(ae.activation, SV[64:128, :, :], v8, ACT.Copy, after=scan)
        pk.free, pv.free = [bt], [v1]
        xi = invert(inv, MM[0:64, :, 0:64], mms, XX[:, :, :], scan)
        p, after = bank()
        T.wait(after + sm + [v0] + mms)
        for i in range(4):
            te.matmul(p.ap[0:64, 128 * i:128 * i + 128], AR[:, i, n, 0, :],
                      SB[:, i, :, :].rearrange("p a t -> p (a t)"), start=True, stop=True)
            for par in range(2):
                h = 2 * i + par
                ins = te.matmul(p.ap[0:64, 64 * h:64 * h + 64], MM[:, h, 0:64], V0[:, h, :], start=False,
                                stop=True, skip_group_check=True)
        ins.then_inc(T.sem, 1)
        T.n += 1
        d = (T.sem, T.n)
        rh = V.op(ve.tensor_copy, RH[:, :, :], p.ap[0:64, :].rearrange("p (h t) -> p h t", h=8), after=[d] + scan)
        p.free = [rh]
        p, o, d = products(XX, RH, [rh, xi])
        sv = V.op(ve.tensor_copy, SV[0:64, :, :], o, after=[d] + scan)
        p.free = [sv]
        if n:
            p, after = bank()
            T.wait(after + [sv, v1])
            for i in range(4):
                te.matmul(p.ap[:, 64 * i:64 * i + 64], SB[:, i, :, :].rearrange("p a t -> p (a t)"),
                          AR[:, i, n, 1, :], start=True, stop=True)
                for par in range(2):
                    h = 2 * i + par
                    ins = te.matmul(p.ap[64 * par:64 * par + 64, 64 * i:64 * i + 64], SV[:, h, :], MM[:, h, 64:128],
                                    start=False, stop=True, skip_group_check=True)
            ins.then_inc(T.sem, 1)
            T.n += 1
            yd = (T.sem, T.n)
            ym = A.op(ae.activation, AR[:, :, n, 1, :], p.ap[:, 0:256].rearrange("p (i t) -> p i t", i=4),
                      ACT.Copy, after=[yd])
            p.free = [ym]
            y_marks.append(ym)
        p, after = bank()
        T.wait(after + [bt, sv, v1])
        for h in range(8):
            i, par = divmod(h, 2)
            ins = te.matmul(p.ap[64 * par:64 * par + 64, 64 * i:64 * i + 64], BKT[:, h, :], SV[:, h, :],
                            start=True, stop=True)
        ins.then_inc(T.sem, 1)
        T.n += 1
        sd = (T.sem, T.n)
        sm = []
        for par in range(2):
            q = slice(64 * par, 64 * par + 64)
            pp = p.ap[q, 0:256].rearrange("p (i t) -> p i t", i=4)
            s1 = V.op(ve.tensor_tensor, SB[q, :, par, :], pp, SB[q, :, par, :], ALU.add, after=[sd])
            sm.append(V.op(ve.tensor_tensor, SB[q, :, par, :], SB[q, :, par, :],
                           WCC[q, :, n:n + 1].broadcast_to([64, 4, 64]), ALU.mult, after=[s1] + wcm))
        p.free = [s1]
        scan = [sd]
    ck.close()
    lnx = ExitStack()
    TT = [sbuf(f"TT{i}", [128, 512], st=lnx) for i in range(2)]
    EPL = sbuf("EPL", [128, 1], st=lnx)
    epl = G.op(ge.memset, EPL[:, :], 64e-5, after=[sd])
    rwm = []
    for i in range(4):
        y3 = AR[:, i, 1:NCH, 1, :]
        pp, after = bank()
        T.wait(after + y_marks)
        mm = T.op(te.matmul, pp.ap, con("bones"), y3, start=True, stop=True)
        t, sq = TT[0], TT[1]
        c = V.op(ve.scalar_tensor_tensor, ch(t[:, :]), ch(pp.ap), -1.0 / 64, y3, ALU.mult, ALU.add,
                 after=[mm] + ([rwm[-1]] if rwm else [sd]))
        pp.free = [c]
        s2 = A.op(ae.activation, sq[:, :], t[:, :], ACT.Square, after=[c])
        pp, after = bank()
        mm = T.op(te.matmul, pp.ap, con("bones"), sq[:, :], start=True, stop=True, after=after + [s2])
        r = A.op(ae.activation, sq[:, :], pp.ap, ACT.Sqrt, bias=EPL[:, 0:1], scale=1.0 / 64, after=[mm, epl])
        pp.free = [r]
        r = V.op(ve.reciprocal, sq[:, :], sq[:, :], after=[r])
        m = V.op(ve.tensor_tensor, t[:, :], t[:, :], sq[:, :], ALU.mult, after=[r])
        m = V.op(ve.tensor_scalar, t[:, :], t[:, :], col("lnw", i), col("lnb", i), ALU.mult, ALU.add, after=[m])
        m = V.op(ve.tensor_tensor, BON[:, i, :], BON[:, i, :], t[:, :], ALU.add, after=[m, bonm[i]])
        pp, after = bank()
        mm = T.op(te.matmul, pp.ap, GUP[0:96, 128 * i:128 * i + 128], XG[0:96, NM:T2], start=True, stop=True,
                  after=after + [xg])
        m = V.op(ve.tensor_tensor, BON[:, i, :], BON[:, i, :], pp.ap, ALU.mult, after=[mm, m])
        pp.free = [m]
        rwm.append(m)
    lnx.close()
    rk.close()

    at_ = ExitStack()
    QA = sbuf("QA", [128, 4, 512], st=at_)
    KA = sbuf("KA", [128, 4, 640], st=at_)
    VT = sbuf("VT", [128, 5, 512], st=at_)
    VS = [sbuf(f"VS{i}", [128, 640], st=at_) for i in range(2)]
    PM = sbuf("PM", [128, 1], st=at_)
    zk = G.op(ge.memset, KA[:, :, 0:112], 0.0, after=rwm)
    zv = [G.op(ge.memset, VS[i][:, 0:112], 0.0) for i in range(2)]
    pm0 = G.op(ge.memset, PM[:, :], 1.0)
    pmk = G.op(ge.affine_select, out=PM[:, :], in_=PM[:, :], pattern=[[0, 1]], compare_op=ALU.is_ge, fill=0.0,
               base=-112, channel_multiplier=1, after=[pm0])
    qm, km, vtm = [], [], []
    for i in range(4):
        p, after = pair()
        d = gemm("w_in2", 12 + i, p[1], after, HH, HL, KT, H2, hall)
        m1 = A.op(ae.activation, QA[:, i, 0:248], p[1][:, 0, 16:264], ACT.Copy, scale=0.125, after=[d] + rwm)
        m2 = A.op(ae.activation, QA[:, i, 248:512], p[1][:, 1, :], ACT.Copy, scale=0.125)
        free_pair(p, [m2])
        qm.append(m2)
    for i in range(4):
        p, after = pair()
        d = gemm("w_in2", 16 + i, p[1], after, HH, HL, KT, H2, hall)
        m = A.op(ae.activation, two(KA[:, i, 112:640]), p[1], ACT.Copy, after=[d])
        free_pair(p, [m])
        km.append(m)
    vu = [list(zv), list(zv)]
    for i in range(4):
        p, after = pair()
        d = gemm("w_in2", 20 + i, p[1], after, HH, HL, KT, H2, hall)
        m = A.op(ae.activation, two(VS[i % 2][:, 112:640]), p[1], ACT.Copy, after=[d] + vu[i % 2])
        free_pair(p, [m])
        p, after = bank()
        q, after2 = bank()
        T.wait(after + after2 + [m])
        for j in range(5):
            o = p.ap[:, 128 * j:128 * j + 128] if j < 4 else q.ap[:, 0:128]
            ins = te.transpose(o, VS[i % 2][:, 128 * j:128 * j + 128], con("ident"))
        ins.then_inc(T.sem, 1)
        T.n += 1
        d = (T.sem, T.n)
        vu[i % 2] = [d]
        m1 = V.op(ve.tensor_copy, VT[:, 0:4, 128 * i:128 * i + 128], p.ap.rearrange("p (j t) -> p j t", j=4),
                  after=[d])
        m2 = V.op(ve.tensor_copy, VT[:, 4, 128 * i:128 * i + 128], q.ap[:, 0:128])
        p.free, q.free = [m1], [m2]
        vtm += [m1, m2]
    proj_done = d
    cat = [None] * 8
    for j in range(4):
        hi = A.op(ae.activation, HH[:, 4 + j, NM:T2], BON[:, j, :], ACT.Copy, after=[proj_done])
        lo = V.op(ve.tensor_tensor, HL[:, 4 + j, NM:T2], BON[:, j, :], HH[:, 4 + j, NM:T2].bitcast(f32),
                  ALU.subtract, after=[hi])
        cat[4 + j] = [hi, lo]

    OFF = [0, 512, 1024, 1408, 1664]
    LEN = [512, 512, 384, 256, 128]
    SP = [sbuf(f"SP{i}", [128, 512], st=at_) for i in range(3)]
    KHI = [sbuf(f"KHI{i}", [128, 1792], f32r, at_) for i in range(2)]
    KLO = [sbuf(f"KLO{i}", [128, 1792], f32r, at_) for i in range(2)]
    ATT = [sbuf(f"ATT{i}", [128, 1792], st=at_) for i in range(2)]
    spu = [[], [], []]
    khu = [[], []]
    atu = [[], []]
    nsp = 0
    avp = [None]

    def attend(h, am):
        i, par = divmod(h, 2)
        if par == 0:
            avp[0] = bank()
        p, after = avp[0]
        T.wait(after + am + vtm)
        for j in range(5):
            ins = te.matmul(p.ap[64 * par:64 * par + 64, 512 - LEN[j]:512], VT[:, j, 64 * h:64 * h + 64],
                            ATT[h % 2][:, OFF[j]:OFF[j] + LEN[j]], start=(j == 0), stop=(j == 4))
        ins.then_inc(T.sem, 1)
        T.n += 1
        d = (T.sem, T.n)
        atu[h % 2] = [d]
        if par:
            hi = A.op(ae.activation, HH[:, i, NM:T2], p.ap, ACT.Copy, after=[d])
            lo = V.op(ve.tensor_tensor, HL[:, i, NM:T2], p.ap, HH[:, i, NM:T2].bitcast(f32), ALU.subtract,
                      after=[hi])
            p.free = [lo]
            cat[i] = [hi, lo]

    pending = None
    for h in range(8):
        i, par = divmod(h, 2)
        pb = 64 * par
        b = h % 2
        lk = {}
        am = []
        for j in (4, 3, 2, 1, 0):
            n = LEN[j]
            p, after = bank()
            T.wait(after + qm + km + [zk])
            z = T.op(te.matmul, p.ap[:, 0:n], KA[pb:pb + 64, i, 128 * j:128 * j + 128], QA[pb:pb + 64, i, 512 - n:512],
                     start=True, stop=True)
            s = SP[nsp % 3]
            t = TMP[nsp % 3]
            su = spu[nsp % 3]
            a1 = A.op(ae.activation, t[:, 0:n], p.ap[:, 0:n], ACT.Abs, after=[z] + su)
            a2 = A.op(ae.activation, t[:, 0:n], t[:, 0:n], ACT.Exp, scale=-1.0, after=[a1])
            a3 = A.op(ae.activation, t[:, 0:n], t[:, 0:n], ACT.Ln, bias=1.0, after=[a2])
            m = V.op(ve.scalar_tensor_tensor, s[:, 0:n], p.ap[:, 0:n], 0.0, t[:, 0:n], ALU.max, ALU.add,
                     after=[a3] + su)
            if j:
                m = G.op(ge.affine_select, out=s[:, 0:128], in_=s[:, 0:128], pattern=[[1, 128]],
                         compare_op=ALU.is_gt, fill=0.0, base=0, channel_multiplier=-1, after=[m])
            else:
                m = V.op(ve.tensor_scalar, s[:, 0:n], s[:, 0:n], PM[:, 0:1], None, ALU.mult, after=[m, pmk])
            o = slice(OFF[j], OFF[j] + n)
            hi = A.op(ae.activation, KHI[b][:, o], s[:, 0:n], ACT.Copy, scale=-1.0, after=[m] + khu[b])
            lo = V.op(ve.scalar_tensor_tensor, KLO[b][:, o], s[:, 0:n], -1.0, KHI[b][:, o].bitcast(f32), ALU.mult,
                      ALU.subtract, after=[hi, m] + khu[b])
            spu[nsp % 3] = [lo, hi]
            nsp += 1
            lk[j] = [hi, lo]
            T.wait([hi, lo])
            for q in range(4, j - 1, -1):
                w = TRIR if q == j else ONER
                for part in (KHI[b], KLO[b]):
                    ins = te.matmul(p.ap[:, n - LEN[q]:n], w[:, :], part[:, OFF[q]:OFF[q] + LEN[q]], start=False,
                                    stop=True, skip_group_check=True)
            ins.then_inc(T.sem, 1)
            T.n += 1
            d = (T.sem, T.n)
            e = A.op(ae.activation, ATT[b][:, o], p.ap[:, 0:n], ACT.Exp, after=[d] + atu[b])
            p.free = [e]
            if j:
                e = G.op(ge.affine_select, out=ATT[b][:, OFF[j]:OFF[j] + 128], in_=ATT[b][:, OFF[j]:OFF[j] + 128],
                         pattern=[[1, 128]], compare_op=ALU.is_gt, fill=0.0, base=0, channel_multiplier=-1,
                         after=[e])
            am.append(e)
        khu[b] = [d]
        if pending:
            attend(*pending)
        pending = (h, am)
    attend(*pending)
    xn = []
    for m in range(8):
        p, after = bank()
        d = gemm("w_out2", m, p.ap, after, HH, HL, KT, H1, flat(cat))
        xn.append([V.op(ve.tensor_tensor, X[:, m, NM:T2], p.ap, X[:, m, NM:T2], ALU.add, after=[d])])
        p.free = [xn[-1][0]]
    at_.close()
    rw.close()
    hm = rms(X, CV[:, COLS["ffn2"]:COLS["ffn2"] + 8], None, NM, xn, [d] + flat(cat))
    xm, d = ffn("f2", hm, NM, fin2(NM))
    xm = rms(X, CV[:, COLS["final"]:COLS["final"] + 8], None, NM, xm, [d], dst=X)

    s_out = sem("s_out")
    S.wait(flat(xm))
    se.dma_start(out.rearrange("(k p) t -> p k t", p=128), X[:, :, NM:T2]).then_inc(s_out, 16)
    se.wait_ge(s_out, 16)
    top.close()


def host(inputs):
    import numpy as np
    g = {k: np.asarray(v) for k, v in inputs.items()}
    z = lambda *s: np.zeros(s, np.float32)

    def cv(v):
        v = v.reshape(-1)
        n = -(-v.size // 128)
        o = z(n * 128)
        o[:v.size] = v
        return o.reshape(n, 128).T

    mu = g["rwkv_mu_2"][0]
    cat = [g["c"], g["b_ada"], g["norm1_w"], g["conv_qkv_w"], g["conv_short_w"], g["gdn_norm_w"], g["norm2_w"],
           g["norm_f_w"], g["ffn1_norm_2"], g["mix_norm_2"], (mu[:1536], mu[1536:1600], mu[1600:]), g["rwkv_w0_2"],
           g["rwkv_a0_2"], g["rwkv_k_k_2"], g["rwkv_k_a_2"], g["rwkv_r_k_2"], g["rwkv_lnx_w_2"], g["rwkv_lnx_b_2"],
           g["ffn2_norm_2"], g["final_norm_2"], g["A_log"], g["dt_bias"]]
    cols = np.concatenate([np.concatenate([cv(x) for x in v], 1) if isinstance(v, tuple) else cv(v) for v in cat], 1)
    assert cols.shape[1] == NCOL, cols.shape

    con = z(128, sum(NCON))

    def put(n, v):
        g_, a, k = CON[n]
        a += sum(NCON[:g_])
        con[:v.shape[0], a:a + k] = v

    i = np.arange(128)
    s, t = i[:, None], i[None, :]
    put("ident", (s == t) * np.float32(1))
    put("ones", np.ones((128, 128), np.float32))
    put("bones", (s // 64 == t // 64) * np.float32(1))
    put("tri", (s >= t) * np.float32(1))
    put("m4", np.where(t < 64, s % 64 < t % 64, s % 64 <= t % 64) * np.float32(1))
    s, t = s[:64], t[:, :64]
    put("b16", (s // 16 == t // 16) * np.float32(1))
    c32 = ((s // 32 == t // 32) & (s // 16 != t // 16)) * np.float32(1)
    c64 = (s // 32 != t // 32) * np.float32(1)
    put("c32", c32)
    put("c64", c64)
    put("madd", np.where(s <= t, 0, -1e30).astype(np.float32))
    put("nstrict", np.where(s < t, -1, 0).astype(np.float32))
    put("reset1", np.broadcast_to((np.arange(512) % 64 != 0) * np.float32(1), (128, 512)))
    put("reset2", np.broadcast_to((np.arange(TP) % 64 != 0) * np.float32(1), (128, TP)))
    sel = z(64, 8, 128)
    for h in range(4):
        sel[h, h] = 1
        sel[32 + h, 4 + h] = 1
    put("sel", sel.reshape(64, 1024))

    def tiles(w):
        K, M = w.shape
        return np.ascontiguousarray(w.reshape(K // 128, 128, M // 128, 128).transpose(2, 1, 0, 3)).reshape(M // 128, 128, -1)

    def down(w):
        o = z(24, 128, 1024)
        a = tiles(w)
        for m in range(8):
            o[3 * m] = a[m][:, :1024]
            o[3 * m + 1] = a[m][:, 1024:2048]
            o[3 * m + 2, :, :768] = a[m][:, 2048:]
        return o

    w_in = g["w_in"][0]
    ab = z(1024, 64)
    ab[:, 0:4] = w_in[:, 2048:2052]
    ab[:, 32:36] = w_in[:, 2052:2056]
    sb, sc, sh = (tiles(w_in[:, 2056 + 512 * i:2568 + 512 * i]) for i in range(3))
    w = {"ada": tiles(g["w_ada"][0]),
         "ab": np.ascontiguousarray(ab.reshape(8, 128, 64).transpose(1, 0, 2)).reshape(1, 128, 512),
         "w_in": np.concatenate([tiles(w_in[:, :2048]), np.stack([sc, sh, sb], 1).reshape(12, 128, 1024)], 0),
         "w_out": tiles(g["w_out"][0])}
    v = g["w_in_2"][0]
    lo = z(1024, 256)
    lo[:, 0:64] = v[:, 3072:3136]
    lo[:, 128:224] = v[:, 3136:3232]
    r, k, vv = (tiles(v[:, 1536 + 512 * i:2048 + 512 * i]) for i in range(3))
    w["lora"] = tiles(lo)
    w["w_in2"] = np.concatenate([np.stack([r, k, vv], 1).reshape(12, 128, 1024), tiles(v[:, :1536])], 0)
    w["w_out2"] = tiles(g["w_out_2"][0])
    for f, pre in (("f0", ""), ("f1", "ffn1_"), ("f2", "ffn2_")):
        post = "_2" if pre else ""
        w[f + "g"] = tiles(g[pre + "w_gate" + post][0])
        w[f + "u"] = tiles(g[pre + "w_up" + post][0])
        w[f + "d"] = down(g[pre + "w_down" + post][0])
    arrays = {"xT": np.ascontiguousarray(g["x"][0].T), "metaT": np.ascontiguousarray(g["meta_tokens_2"].T),
              "cols": np.ascontiguousarray(cols), "consts": con}
    arrays["lup"] = np.ascontiguousarray(np.concatenate([g["rwkv_w_up_2"][0], g["rwkv_a_up_2"][0]], 0))
    arrays["gup"] = np.ascontiguousarray(g["rwkv_g_up_2"][0])
    for n, a in w.items():
        arrays["w_" + n] = a
    return arrays


def kernel(**inputs):
    import numpy as _np
    import concourse.bacc as _bacc
    from concourse import mybir as _mybir
    from concourse.bass_utils import run_bass_kernel_spmd as _run

    arrays = host(inputs)
    nc = _bacc.Bacc("TRN2", target_bir_lowering=False, num_devices=1)
    f32 = _mybir.dt.float32
    ap = {n: nc.dram_tensor(n, a.shape, f32, kind="ExternalInput").ap() for n, a in arrays.items()}
    out = nc.dram_tensor("out", (D, T1), f32, kind="ExternalOutput").ap()
    slabs = {n[2:]: a for n, a in ap.items() if n.startswith("w_")}
    program(nc, ap["xT"], ap["metaT"], ap["cols"], ap["consts"], slabs, ap["lup"], ap["gup"], out)
    r = _run(nc, [arrays], core_ids=[0])
    return _np.ascontiguousarray(r.results[0]["out"].T)[None]
```

```python
import concourse.bass as bass
from concourse import mybir
from contextlib import ExitStack

D = 1024
T1 = 512
NM = 16
T2 = T1 + NM
KT = 8
FT = 22
SLAB = 1024
EPS = 1e-6
KAPPA = 0.6065306597126334
PAD = 48
TP = T2 + PAD
NCH = 9

COLS = {}
_at = 0
for _n, _k in (("c", 8), ("b_ada", 48), ("norm1", 8), ("convq", 48), ("convs", 12), ("gdn", 1), ("norm2", 8),
               ("normf", 8), ("ffn1", 8), ("mix", 8), ("mu", 14), ("w0", 4), ("a0", 4), ("kk", 4), ("ka", 4),
               ("rk", 4), ("lnw", 4), ("lnb", 4), ("ffn2", 8), ("final", 8), ("alog", 1), ("dtb", 1)):
    COLS[_n] = _at
    _at += _k
NCOL = _at

CON = {}
NCON = [0, 0, 0]
for _g, _n, _k in ((0, "ident", 128), (0, "ones", 128), (0, "bones", 128), (0, "b16", 64), (0, "c32", 64), (0, "c64", 64),
                   (1, "madd", 64), (1, "nstrict", 64), (1, "sel", 1024), (2, "reset1", 512),
                   (2, "tri", 128), (2, "m4", 128), (2, "reset2", TP)):
    CON[_n] = (_g, NCON[_g], _k)
    NCON[_g] += _k



class Engine:

    def __init__(self, eng, sem):
        self.eng, self.sem, self.n, self.seen = eng, sem, 0, {}

    def wait(self, marks):
        for sem, n in marks:
            if self.seen.get(sem.name, 0) < n:
                self.eng.wait_ge(sem, n)
                self.seen[sem.name] = n

    def op(self, f, *a, after=(), **k):
        self.wait(after)
        f(*a, **k).then_inc(self.sem, 1)
        self.n += 1
        return (self.sem, self.n)

    def quiet(self, f, *a, after=(), **k):
        self.wait(after)
        f(*a, **k)


class Bank:
    def __init__(self, ap):
        self.ap, self.free = ap, []


def program(nc, xT, metaT, cols, consts, slabs, lup, gup, out):
    f32, f32r = mybir.dt.float32, mybir.dt.float32r
    ALU, ACT = mybir.AluOpType, mybir.ActivationFunctionType
    ve, ae, ge, te, se = nc.vector, nc.scalar, nc.gpsimd, nc.tensor, nc.sync
    top = ExitStack()

    def sem(name):
        return top.enter_context(nc.semaphore(name))

    def sbuf(name, shape, dt=f32, st=top):
        return st.enter_context(nc.sbuf_tensor(name, shape, dt))

    V, A, G, T = Engine(ve, sem("s_v")), Engine(ae, sem("s_a")), Engine(ge, sem("s_g")), Engine(te, sem("s_t"))
    S = Engine(se, sem("s_s"))
    PS = top.enter_context(nc.psum_tensor("PS", [128, 8, 512], f32))
    banks = [Bank(PS[:, i, :]) for i in range(8)]
    pairs = [Bank(PS[:, 2 * i:2 * i + 2, 0:264]) for i in range(4)]
    turn = [0]

    def bank():
        for _ in range(8):
            b = banks[turn[0] % 8]
            turn[0] += 1
            if b.free is not None:
                break
        after = b.free
        b.free = None
        assert after is not None
        return b, after

    def pair():
        turn[0] += turn[0] % 2
        for _ in range(4):
            i = turn[0] % 8
            turn[0] += 2
            if banks[i].free is not None and banks[i + 1].free is not None:
                break
        after = banks[i].free + banks[i + 1].free
        banks[i].free = banks[i + 1].free = None
        return (i, pairs[i // 2].ap), after

    def free_pair(p, marks):
        banks[p[0]].free = list(marks)
        banks[p[0] + 1].free = list(marks)

    X = sbuf("X", [128, KT, T2])
    HH = sbuf("HH", [128, KT, T2], f32r)
    HL = sbuf("HL", [128, KT, T2], f32r)
    CV = sbuf("CV", [128, NCOL])
    NCV = sbuf("NCV", [128, 8])
    KC = [sbuf("KC", [128, NCON[0]]), None, None]
    MOD = sbuf("MOD", [128, 48])
    SC = sbuf("SC", [128, 16])
    CA = sbuf("CA", [128, 8])
    TRIR = sbuf("TRIR", [128, 128], f32r)
    ONER = sbuf("ONER", [128, 128], f32r)
    RSTD = sbuf("RSTD", [128, T2])
    TMP = [sbuf(f"TMP{i}", [128, T2]) for i in range(3)]

    def col(name, i=0, p0=0, p1=128):
        return CV[p0:p1, COLS[name] + i:COLS[name] + i + 1]

    def con(name, p1=128):
        g, a, k = CON[name]
        return KC[g][0:p1, a:a + k]

    s_in = sem("s_in")
    se.dma_start(CV[:, :], cols).then_inc(s_in, 16)
    loaded = [(s_in, 48)]

    NR, NS = 4, 3
    RAWS = sbuf("RAWS", [128, NR * SLAB])
    RAW = [RAWS[:, SLAB * i:SLAB * i + SLAB] for i in range(NR)]
    WH = [sbuf(f"WH{i}", [128, SLAB], f32r) for i in range(NS)]
    WL = [sbuf(f"WL{i}", [128, SLAB], f32r) for i in range(NS)]
    s_raw = [sem(f"s_raw{i}") for i in range(NR)]
    order = []

    def whole(which, n):
        order.extend((which, i, SLAB, which != "ada") for i in range(n))

    order += [("ada", i, SLAB, False) for i in range(16)]
    later = [("ada", i, SLAB, False) for i in range(16, 48)]
    order.append(("ab", 0, 512, True))
    for i in range(28):
        order.append(("w_in", i, SLAB, True))
        order.append(later.pop(0))
    order += later
    whole("w_out", 8)
    for w in ("f0", "f1", "f2"):
        if w == "f2":
            order.append(("lora", 0, SLAB, True))
            order.append(("lora", 1, SLAB, True))
            for i in range(4):
                order.extend(("w_in2", t, SLAB, True) for t in (3 * i, 3 * i + 1, 3 * i + 2, 12 + i, 16 + i, 20 + i))
            order.append(("pause", 0, 0, False))
            whole("w_out2", 8)
        for j in range(FT):
            order.append((w + "g", j, SLAB, True))
            order.append((w + "u", j, SLAB, True))
        for m in range(8):
            for t in range(3):
                order.append((w + "d", 3 * m + t, SLAB if t < 2 else 768, True))
    raw_used = [[] for _ in range(NR)]
    split_used = [[] for _ in range(NS)]
    at = {"load": 0, "split": 0, "use": 0, "nsplit": 0}
    loads = {}
    splits = {}

    def load_next():
        i = at["load"]
        if i >= len(order) or raw_used[i % NR] is None:
            return
        which, j, n, _ = order[i]
        if which == "pause":
            return
        r = i % NR
        S.wait(raw_used[r])
        raw_used[r] = None
        se.dma_start(RAW[r][:, 0:n], slabs[which][j, :, 0:n]).then_inc(s_raw[r], 16)
        loads[i] = (s_raw[r], 16 * (i // NR + 1))
        at["load"] += 1

    def split_next():
        i = at["split"]
        if i >= len(order):
            return
        which, j, n, cut = order[i]
        r = i % NR
        at["split"] += 1
        if not cut:
            return
        s = at["nsplit"] % NS
        at["nsplit"] += 1
        used = split_used[s]
        assert used is not None
        split_used[s] = None
        hi = A.op(ae.activation, WH[s][:, 0:n], RAW[r][:, 0:n], ACT.Copy, after=[loads[i]] + used)
        lo = G.op(ge.tensor_tensor, WL[s][:, 0:n], RAW[r][:, 0:n], WH[s][:, 0:n].bitcast(f32), ALU.subtract,
                  after=[loads[i], hi] + used)
        splits[i] = (s, [hi, lo])
        raw_used[r] = [hi, lo]
        load_next()

    def slab(which, j):
        i = at["use"]
        assert order[i][:2] == (which, j), (order[i], which, j)
        at["use"] += 1
        while at["split"] < min(i + 3, at["load"]) and at["nsplit"] - cut_before(i) < NS:
            split_next()
        return i

    def resume():
        i = at["load"]
        assert order[i][0] == "pause" and at["use"] == i
        del order[i]
        del cuts[i]
        marks = [(e.sem, e.n) for e in (V, A, G, T)]
        for r in range(NR):
            assert raw_used[r] is not None
            raw_used[r] = raw_used[r] + marks
        for _ in range(NR):
            load_next()

    cuts = [0]
    for o in order:
        cuts.append(cuts[-1] + o[3])

    def cut_before(i):
        return cuts[i]

    def run(*gens):
        live = list(gens)
        while live:
            for g in list(live):
                if next(g, run) is run:
                    live.remove(g)

    def gemm(*a, **k):
        g = gemm_steps(*a, **k)
        while True:
            try:
                next(g)
            except StopIteration as e:
                return e.value

    def gemm_steps(which, j, ps, after, xh, xl, nk, halves, xmarks, m=128, first=True, last=True, k0=0):
        i = slab(which, j)
        s, marks = splits[i]
        T.wait(list(after) + marks)
        for k in range(nk):
            if k:
                yield
            T.wait(xmarks[k0 + k] if xmarks else [])
            for w, x, e in ((WH[s], xh, 0), (WH[s], xl, 1), (WL[s], xh, 2)):
                for q, (o, a, b) in enumerate(halves):
                    stop = last and k == nk - 1 and e == 2
                    ins = te.matmul(ps[0:m, q, o:o + b - a] if len(halves) > 1 else ps[0:m, o:o + b - a],
                                    w[:, k * m:k * m + m], x[:, k0 + k, a:b],
                                    start=first and k == 0 and e == 0, stop=stop)
        ins.then_inc(T.sem, 1)
        T.n += 1
        done = (T.sem, T.n)
        split_used[s] = [done]
        return done

    H1 = [(0, NM, T2)]
    H2 = [(0, 0, 264), (0, 264, T2)]

    def two(ap):
        return ap.rearrange("p (a b) -> p a b", a=2)

    class Stats:

        def __init__(self, t0, free):
            self.t0, self.n, self.sq = t0, T2 - t0, {}
            self.used = [list(free) for _ in range(3)]

        def square(self, k, marks):
            self.sq[k] = A.op(ae.activation, TMP[k % 3][:, 0:self.n], X[:, k, self.t0:T2], ACT.Square,
                              after=marks + self.used[k % 3])

        def sum(self, k):
            if k == 0:
                if self.n == 528:
                    self.p, after = pair()
                    self.view = self.p[1]
                    self.outs = [(self.view[:, 0, :], 0, 264), (self.view[:, 1, :], 264, 528)]
                else:
                    self.p, after = bank()
                    self.view = self.p.ap[:, 0:self.n]
                    self.outs = [(self.view, 0, self.n)]
                T.wait(after)
            T.wait([self.sq[k]])
            for o, a, b in self.outs:
                ins = te.matmul(o, con("ones"), TMP[k % 3][:, a:b], start=(k == 0), stop=(k == KT - 1))
            ins.then_inc(T.sem, 1)
            T.n += 1
            self.used[k % 3] = [(T.sem, T.n)]

        def done(self, mark):
            if self.n == 528:
                free_pair(self.p, [mark])
            else:
                self.p.free = [mark]

    def rms(wcols, shift, t0, xmarks, free, dst=None, st=None):
        n = T2 - t0
        x = X
        if st is None:
            st = Stats(t0, free)
            for k in range(KT):
                st.square(k, xmarks[k])
                if k:
                    st.sum(k - 1)
        st.sum(KT - 1)
        used = st.used
        rv = two(RSTD[:, 0:n]) if n == 528 else RSTD[:, 0:n]
        r1 = A.op(ae.activation, rv, st.view, ACT.Sqrt, bias=EPSC[:, 0:1], scale=1.0 / D,
                  after=[(T.sem, T.n), epc] + free)
        st.done(r1)
        r2 = V.op(ve.reciprocal, RSTD[:, 0:n], RSTD[:, 0:n], after=[r1])
        res = []
        for k in range(KT):
            if dst is not None:
                res.append([V.op(ve.scalar_tensor_tensor, dst[:, k, t0:T2], x[:, k, t0:T2], wcols[:, k:k + 1],
                                 RSTD[:, 0:n], ALU.mult, ALU.mult, after=[r2] + xmarks[k])])
                continue
            h = V.op(ve.scalar_tensor_tensor, TMP[k % 3][:, 0:n], x[:, k, t0:T2], wcols[:, k:k + 1], RSTD[:, 0:n],
                     ALU.mult, ALU.mult, after=[r2] + used[k % 3])
            if shift is None:
                hi = A.op(ae.activation, HH[:, k, t0:T2], TMP[k % 3][:, 0:n], ACT.Copy, after=[h])
                lo = V.op(ve.tensor_tensor, HL[:, k, t0:T2], TMP[k % 3][:, 0:n], HH[:, k, t0:T2].bitcast(f32),
                          ALU.subtract, after=[hi])
            else:
                hi = A.op(ae.activation, HH[:, k, t0:T2], TMP[k % 3][:, 0:n], ACT.Identity,
                          bias=shift[:, k:k + 1], after=[h])
                lo = V.op(ve.scalar_tensor_tensor, HL[:, k, t0:T2], TMP[k % 3][:, 0:n], shift[:, k:k + 1],
                          HH[:, k, t0:T2].bitcast(f32), ALU.add, ALU.subtract, after=[hi])
            used[k % 3] = [lo]
            res.append([hi, lo])
        return res

    def flat(marks):
        return [x for m in marks for x in m]

    def ffn(name, hm, t0, finish, s0):
        st = ExitStack()
        n = T2 - t0
        IH = sbuf("IH" + name, [128, FT, n], f32r, st)
        IL = sbuf("IL" + name, [128, FT, n], f32r, st)
        halves = H2 if t0 == 0 else H1
        im = []
        used = [[], [], []]
        for j in range(FT):
            ps = []
            for w in "gu":
                if t0 == 0:
                    p, after = pair()
                    d = gemm(name + w, j, p[1], after, HH, HL, KT, halves, hm)
                    ps.append((p, p[1], d))
                else:
                    p, after = bank()
                    d = gemm(name + w, j, p.ap, after, HH, HL, KT, halves, hm)
                    ps.append((p, p.ap, d))
            (pg, g, dg), (pu, u, du) = ps
            b = j % 3
            tv = two(TMP[b][:, 0:n]) if t0 == 0 else TMP[b][:, 0:n]
            a = A.op(ae.activation, tv, g, ACT.Silu, after=[dg] + used[b])
            m = V.op(ve.tensor_tensor, tv, tv, u, ALU.mult, after=[a, du])
            if t0 == 0:
                free_pair(pg, [a])
                free_pair(pu, [m])
            else:
                pg.free, pu.free = [a], [m]
            hi = A.op(ae.activation, IH[:, j, :], TMP[b][:, 0:n], ACT.Copy, after=[m])
            lo = V.op(ve.tensor_tensor, IL[:, j, :], TMP[b][:, 0:n], IH[:, j, :].bitcast(f32), ALU.subtract,
                      after=[hi])
            used[b] = [lo]
            im.append([hi, lo])
        out_marks = []
        stats = Stats(s0, [im[-1][1]])
        hv = [(0, 0, n)] if t0 else H2
        for m in range(8):
            if t0 == 0:
                p, after = pair()
                ps = p[1]
            else:
                p, after = bank()
                ps = p.ap
            for t in range(3):
                nk = 8 if t < 2 else 6
                d = gemm(name + "d", 3 * m + t, ps, after, IH, IL, nk, hv, im if m == 0 else [],
                         first=(t == 0), last=(t == 2), k0=8 * t)
                after = []
            mk = finish(m, ps, d)
            if t0 == 0:
                free_pair(p, [mk])
            else:
                p.free = [mk]
            out_marks.append([mk])
            if m:
                stats.sum(m - 1)
            stats.square(m, [mk])
        st.close()
        return out_marks, d, stats

    se.dma_start(KC[0][:, :], consts[:, 0:NCON[0]]).then_inc(s_in, 16)
    se.dma_start(X[:, :, 0:NM], metaT.rearrange("(k p) t -> p k t", p=128)).then_inc(s_in, 16)
    s_x = sem("s_x")
    for _ in range(NR):
        load_next()
    se.dma_start(X[:, :, NM:T2], xT.rearrange("(k p) t -> p k t", p=128)).then_inc(s_x, 16)

    ca = A.op(ae.activation, CA[:, :], CV[:, COLS["c"]:COLS["c"] + 8], ACT.Silu, after=loaded)
    EPSC = sbuf("EPSC", [128, 1])
    epc = G.op(ge.memset, EPSC[:, :], EPS)
    c2 = A.op(ae.activation, ONER[:, :], con("ones"), ACT.Copy)

    ada_bank = [None]

    def ada(j, j0, after):
        i = slab("ada", j)
        r = i % NR
        b = ada_bank[0]
        T.wait([loads[i], ca] + after)
        for k in range(KT):
            ins = te.matmul(b.ap[:, j - j0:j - j0 + 1], RAW[r][:, k * 128:k * 128 + 128], CA[:, k:k + 1],
                            start=(k == 0), stop=(k == KT - 1))
        ins.then_inc(T.sem, 1)
        T.n += 1
        raw_used[r] = [(T.sem, T.n)]
        load_next()
        return (T.sem, T.n)

    ada_bank[0], after = bank()
    for j in range(16):
        d = ada(j, 0, after)
    mod1 = V.op(ve.tensor_tensor, MOD[:, 0:16], ada_bank[0].ap[:, 0:16], CV[:, COLS["b_ada"]:COLS["b_ada"] + 16],
                ALU.add, after=[d] + loaded)
    ada_bank[0].free = [mod1]
    sc1 = V.op(ve.scalar_tensor_tensor, SC[:, 0:8], MOD[:, 8:16], 1.0, CV[:, COLS["norm1"]:COLS["norm1"] + 8],
               ALU.add, ALU.mult, after=[mod1])
    A.wait([sc1])
    T.wait(loaded + [c2])
    V.wait(loaded)
    G.wait(loaded)
    A.wait(loaded)
    hm = rms(SC[:, 0:8], MOD[:, 0:8], NM, [[(s_x, 16)]] * KT, [sc1])

    mx = ExitStack()
    KC[1] = sbuf("KC1", [128, NCON[1]], st=mx)
    s_k1 = sem("s_k1")
    S.wait([(V.sem, V.n)])
    se.dma_start(KC[1][:, :], consts[:, NCON[0]:NCON[0] + NCON[1]]).then_inc(s_k1, 16)
    k1 = [(s_k1, 32)]
    a1 = NCON[0] + NCON[1] + CON["reset1"][1]
    QKV = sbuf("QKV", [128, 12, 512], st=mx)
    Z = sbuf("Z", [128, 4, 512], st=mx)
    YS = sbuf("YS", [128, 4, 512], st=mx)
    se.dma_start(YS[:, 0, :], consts[:, a1:a1 + 512]).then_inc(s_k1, 16)
    ROW = sbuf("ROW", [64, 512], st=mx)
    NEA = sbuf("NEA", [4, 1], st=mx)
    STG = [sbuf(f"STG{i}", [128, 3 + 512], st=mx) for i in range(2)]
    RT = [TMP[i][0:64, 0:512] for i in range(2)]
    free_x = [(V.sem, V.n)]
    A.wait(free_x)
    G.wait(free_x)
    z0 = G.op(ge.memset, STG[0][:, 0:3], 0.0)
    z1 = G.op(ge.memset, STG[1][:, 0:3], 0.0)
    z2 = G.op(ge.memset, ROW[:, :], 0.0)
    hall = flat(hm)

    ada_bank[0] = Bank(None)
    ada_b, ada_after = bank()
    ada_bank[0] = ada_b
    ada_next = [16]

    def more_ada():
        if ada_next[0] < 48:
            d = ada(ada_next[0], 16, ada_after)
            ada_next[0] += 1
            return d

    p, after = bank()
    d = gemm("ab", 0, p.ap, after, HH, HL, KT, H1, hm, m=64)
    tx = V.op(ve.tensor_scalar, RT[0][0:4, :], p.ap[0:4, :], col("dtb", 0, 0, 4), None, ALU.add, after=[d])
    rb = A.op(ae.activation, ROW[32:36, :], p.ap[32:36, :], ACT.Sigmoid, after=[d, z2])
    p.free = [tx, rb]
    ab = A.op(ae.activation, RT[1][0:4, :], RT[0][0:4, :], ACT.Abs, after=[tx])
    ex = A.op(ae.activation, RT[1][0:4, :], RT[1][0:4, :], ACT.Exp, scale=-1.0, after=[ab])
    ln = A.op(ae.activation, RT[1][0:4, :], RT[1][0:4, :], ACT.Ln, bias=1.0, after=[ex])
    nea = A.op(ae.activation, NEA[:, :], col("alog", 0, 0, 4), ACT.Exp)
    sp = V.op(ve.scalar_tensor_tensor, RT[0][0:4, :], RT[0][0:4, :], 0.0, RT[1][0:4, :], ALU.max, ALU.add, after=[ln])
    gg = V.op(ve.tensor_scalar, RT[0][0:4, :], RT[0][0:4, :], NEA[:, 0:1], -1.0, ALU.mult, ALU.mult, after=[sp, nea])
    rg = V.op(ve.tensor_tensor_scan, ROW[0:4, :], YS[0:4, 0, :], RT[0][0:4, :], 0.0, ALU.mult, ALU.add,
              after=[gg, z2] + k1)
    rows = [rb, rg]

    used = [[z0], [z1]]
    tused = [[rg], [sp], []]
    qkv = []
    for j in range(12):
        p, after = bank()
        d = gemm("w_in", j, p.ap, after, HH, HL, KT, H1, hm)
        more_ada()
        s = STG[j % 2]
        ev = A.op(ae.activation, s[:, 3:515], p.ap, ACT.Copy, after=[d] + used[j % 2])
        p.free = [ev]
        a = TMP[j % 3][:, 0:512]
        m = V.op(ve.tensor_scalar, a, s[:, 0:512], col("convq", j), None, ALU.mult, after=[ev] + tused[j % 3] + used[j % 2])
        for t in range(1, 4):
            m = V.op(ve.scalar_tensor_tensor, a, s[:, t:t + 512], col("convq", 12 * t + j), a, ALU.mult, ALU.add,
                     after=[m])
        si = A.op(ae.activation, QKV[:, j, :], a, ACT.Silu, after=[m])
        used[j % 2] = [m]
        tused[j % 3] = [si]
        qkv.append(si)
    zm, cat = [None] * 4, [None] * 8
    rest = {}

    def project_rest():
        for j in range(4):
            p, after = bank()
            d = yield from gemm_steps("w_in", 12 + j, p.ap, after, HH, HL, KT, H1, hm)
            more_ada()
            yield
            zm[j] = A.op(ae.activation, Z[:, j, :], p.ap, ACT.Copy, after=[d])
            p.free = [zm[j]]
        ys = []
        for j in range(4):
            s = STG[j % 2]
            p, after = bank()
            d = yield from gemm_steps("w_in", 16 + 3 * j, p.ap, after, HH, HL, KT, H1, hm)
            more_ada()
            yield
            y = YS[:, j, :]
            ev = A.op(ae.activation, y, p.ap, ACT.Copy, after=[d, rg])
            p.free = [ev]
            p, after = bank()
            d = yield from gemm_steps("w_in", 17 + 3 * j, p.ap, after, HH, HL, KT, H1, hm)
            more_ada()
            yield
            m = V.op(ve.tensor_tensor, s[:, 3:515], y, p.ap, ALU.mult, after=[d, ev] + used[j % 2])
            p.free = [m]
            m = V.op(ve.tensor_scalar, y, s[:, 1:513], col("convs", j), None, ALU.mult, after=[m])
            for t in (1, 2):
                m = V.op(ve.scalar_tensor_tensor, y, s[:, 1 + t:513 + t], col("convs", 4 * t + j), y, ALU.mult,
                         ALU.add, after=[m])
            used[j % 2] = [m]
            p, after = bank()
            d = yield from gemm_steps("w_in", 18 + 3 * j, p.ap, after, HH, HL, KT, H1, hm)
            more_ada()
            yield
            m = V.op(ve.tensor_tensor, y, y, p.ap, ALU.mult, after=[d, m])
            p.free = [m]
            ys.append(m)
        rest["done"] = d
        while ada_next[0] < 48:
            d = more_ada()
            yield
        mod2 = V.op(ve.tensor_tensor, MOD[:, 16:48], ada_b.ap[:, 0:32], CV[:, COLS["b_ada"] + 16:COLS["b_ada"] + 48],
                    ALU.add, after=[d])
        ada_b.free = [mod2]
        rest["mod2"] = mod2
        rest["sc2"] = V.op(ve.scalar_tensor_tensor, SC[:, 8:16], MOD[:, 32:40], 1.0,
                           CV[:, COLS["norm2"]:COLS["norm2"] + 8], ALU.add, ALU.mult, after=[mod2])
        for j in range(4):
            yield
            hi = A.op(ae.activation, HH[:, 4 + j, NM:T2], YS[:, j, :], ACT.Copy, after=[ys[j], rest["done"]])
            lo = V.op(ve.tensor_tensor, HL[:, 4 + j, NM:T2], YS[:, j, :], HH[:, 4 + j, NM:T2].bitcast(f32),
                      ALU.subtract, after=[hi, rest["done"]])
            cat[4 + j] = [hi, lo]

    def bc(ap, n):
        return ap.unsqueeze(1).broadcast_to([ap.shape[0], n, ap.shape[1]])

    class Inverse:
        def __init__(self, st, name):
            t = [sbuf(f"{name}{x}", [64, 8, 64], st=st) for x in ("L", "UD", "LD", "U2", "L2", "XA", "XB")]
            self.L, self.UD, self.LD, self.U2, self.L2, self.XA, self.XB = t
            self.done = []

    def products(lhs, rhs, marks, transpose=False):
        p, after = bank()
        T.wait(after + marks)
        o = p.ap[0:64, :].rearrange("p (u t) -> p u t", u=8)
        for u in range(8):
            if transpose:
                ins = te.transpose(o[:, u, :], lhs[:, u, :], con("ident")[0:64, 0:64])
            else:
                ins = te.matmul(o[:, u, :], lhs[:, u, :], rhs[:, u, :], start=True, stop=True)
        ins.then_inc(T.sem, 1)
        T.n += 1
        return p, o, (T.sem, T.n)

    def copied(dst, lhs, rhs, marks, e, transpose=False):
        p, o, d = products(lhs, rhs, marks, transpose)
        if e is A:
            m = A.op(ae.activation, dst, o, ACT.Copy, after=[d])
        else:
            m = V.op(ve.tensor_copy, dst, o, after=[d])
        p.free = [m]
        return m

    def added(dst, base, lhs, rhs, marks):
        p, o, d = products(lhs, rhs, marks)
        m = V.op(ve.tensor_tensor, dst, o, base, ALU.add, after=[d])
        p.free = [m]
        return m

    def invert(w, U, um, X, free):
        i64 = con("ident", 64)[:, 0:64]
        L, UD, LD, U2, L2, XA, XB = w.L, w.UD, w.LD, w.U2, w.L2, w.XA, w.XB
        U4, L4 = UD, LD
        ud = V.op(ve.tensor_tensor, UD[:, :, :], U, bc(con("b16", 64), 8), ALU.mult, after=um + w.done)
        l = copied(L[:, :, :], U, None, um + w.done, A, transpose=True)
        yield
        ld = V.op(ve.tensor_tensor, LD[:, :, :], L[:, :, :], bc(con("b16", 64), 8), ALU.mult, after=[l])
        xa = V.op(ve.tensor_tensor, XA[:, :, :], UD[:, :, :], bc(i64, 8), ALU.add, after=[ud])
        l2 = copied(L2[:, :, :], UD, LD, [ud, ld], A)
        yield
        u2 = copied(U2[:, :, :], LD, UD, [], V)
        yield
        xb = added(XB[:, :, :], XA[:, :, :], L2, XA, [l2, xa])
        yield
        l4 = copied(L4[:, :, :], U2, L2, [u2, l2], A)
        yield
        u4 = copied(U4[:, :, :], L2, U2, [], V)
        yield
        xa = added(XA[:, :, :], XB[:, :, :], L4, XB, [l4, xb])
        yield
        l8 = copied(L2[:, :, :], U4, L4, [u4, l4], A)
        yield
        xb = added(XB[:, :, :], XA[:, :, :], L2, XA, [l8, xa])
        c1 = V.op(ve.tensor_tensor, LD[:, :, :], L[:, :, :], bc(con("c32", 64), 8), ALU.mult, after=[l8, xa])
        yield
        y = copied(U2[:, :, :], XB, None, [xb, l4], A, transpose=True)
        z = copied(U4[:, :, :], LD, XB, [c1], V)
        yield
        xa = added(XA[:, :, :], XB[:, :, :], U2, U4, [y, z])
        yield
        yy = added(L4[:, :, :], U2[:, :, :], U4, U2, [])
        c2 = V.op(ve.tensor_tensor, XB[:, :, :], L[:, :, :], bc(con("c64", 64), 8), ALU.mult, after=[z, xa])
        yield
        z = copied(U2[:, :, :], XB, XA, [c2, xa, yy], A)
        yield
        p, o, d = products(L4, U2, [z])
        m = V.op(ve.tensor_tensor, X, o, XA[:, :, :], ALU.add, after=[d] + free)
        p.free = [m]
        w.done = [m]
        return m

    COLT = sbuf("COLT", [64, 8, 64], st=mx)
    EGC = sbuf("EGC", [64, 8, 4], st=mx)
    BEG = sbuf("BEG", [64, 8, 4], st=mx)
    inv = Inverse(mx, "iv")
    UU = sbuf("UU", [64, 8, 64], st=mx)
    EG = sbuf("EG", [128, 4, 128], st=mx)
    KB = sbuf("KB", [128, 4, 128], st=mx)
    VN = sbuf("VN", [64, 4, 128], st=mx)
    ST = sbuf("ST", [128, 4, 128], st=mx)
    XF = X[:, :, :].rearrange("p k t -> p (k t)")
    BUF = []
    for i in range(2):
        b = {"AT": sbuf(f"AT{i}", [64, 8, 64], st=mx), "XX": sbuf(f"XX{i}", [64, 8, 64], st=mx),
             "VBT": sbuf(f"VBT{i}", [64, 8, 128], st=mx), "WT": sbuf(f"WT{i}", [128, 8, 64], st=mx),
             "QD": sbuf(f"QD{i}", [128, 4, 128], st=mx),
             "GL": sbuf(f"GL{i}", [128, 2, 4], st=mx), "EGL": sbuf(f"EGL{i}", [128, 2, 4], st=mx),
             "KDC": sbuf(f"KDC{i}", [64, 2, 4], st=mx),
             "DC": sbuf(f"DC{i}", [64, 2, 4, 64], st=mx),
             "KBT": XF[0:64, 2048 * i:2048 * i + 1024].rearrange("p (u t) -> p u t", u=8),
             "KDT": XF[0:64, 2048 * i + 1024:2048 * i + 2048].rearrange("p (u t) -> p u t", u=8),
             "done": []}
        BUF.append(b)
    OG = QKV
    p, after = bank()
    T.wait(after + rows)
    o = p.ap[0:64, :].rearrange("p (u t) -> p u t", u=8)
    for n in range(8):
        ins = te.transpose(o[:, n, :], ROW[:, 64 * n:64 * n + 64], con("ident")[0:64, 0:64])
    ins.then_inc(T.sem, 1)
    T.n += 1
    ct = V.op(ve.tensor_copy, COLT[:, :, :], o, after=[(T.sem, T.n)])
    p.free = [ct]
    eg = A.op(ae.activation, EGC[:, :, :], COLT[:, :, 0:4], ACT.Exp, after=[ct])
    bg = V.op(ve.tensor_tensor, BEG[:, :, :], EGC[:, :, :], COLT[:, :, 32:36], ALU.mult, after=[eg])

    def l2_norm():
        for j in (4, 0, 5, 1, 6, 2, 7, 3):
            t = TMP[j % 3][:, 0:512]
            sq = A.op(ae.activation, t, QKV[:, j, :], ACT.Square, after=[qkv[j]] + tused[j % 3])
            p, after = bank()
            mm = T.op(te.matmul, p.ap, con("ones"), t, start=True, stop=True, after=after + [sq])
            yield
            r = A.op(ae.activation, t, p.ap, ACT.Sqrt, bias=EPSC[:, 0:1], after=[mm])
            p.free = [r]
            r = V.op(ve.reciprocal, t, t, after=[r])
            qkv[j] = V.op(ve.scalar_tensor_tensor, QKV[:, j, :], QKV[:, j, :], 128.0 ** -0.5 if j < 4 else 1.0, t,
                          ALU.mult, ALU.mult, after=[r])
            tused[j % 3] = [qkv[j]]
            yield

    sm = [G.op(ge.memset, ST[:, :, :], 0.0)]
    cb = lambda ap: ap.unsqueeze(2).broadcast_to([64, 4, 128])
    v8 = lambda ap: ap[0:64, :].rearrange("p (u t) -> p u t", u=8)
    h4 = lambda ap: ap.rearrange("p (h t) -> p h t", h=4)
    shared = {"kb": [], "eg": [], "uu": []}

    def prepare(b):
        B = BUF[b % 2]
        old = B["done"]
        ts = slice(128 * b, 128 * b + 128)
        p, after = bank()
        T.wait(after + rows + k1)
        for h in range(4):
            ins = te.matmul(p.ap[:, 128 * h:128 * h + 128], con("sel", 64)[:, 128 * h:128 * h + 128], ROW[:, ts],
                            start=True, stop=True)
        ins.then_inc(T.sem, 1)
        T.n += 1
        d = (T.sem, T.n)
        p2, after = bank()
        T.wait(after)
        for h in range(4):
            ins = te.matmul(p2.ap[:, 128 * h:128 * h + 128], con("sel", 64)[:, 128 * (4 + h):128 * (4 + h) + 128],
                            ROW[:, ts], start=True, stop=True)
        ins.then_inc(T.sem, 1)
        T.n += 1
        d2 = (T.sem, T.n)
        yield
        g4 = p.ap.rearrange("p (h c t) -> p h c t", h=4, c=2)
        m1 = [V.op(ve.tensor_tensor, B["DC"][:, :, h, :], g4[0:64, h],
                   COLT[:, 2 * b:2 * b + 2, h:h + 1].broadcast_to([64, 2, 64]), ALU.subtract, after=[d, ct] + old)
              for h in range(4)]
        gl = V.op(ve.tensor_copy, B["GL"][:, :, :].rearrange("p c h -> p h c"), g4[:, :, :, 63], after=[d] + old)
        e = A.op(ae.activation, EG[:, :, :], h4(p.ap), ACT.Exp, after=[m1[-1], gl] + shared["eg"])
        p.free = [e]
        yield
        dv = B["DC"][:, :, :, :].rearrange("p c h t -> p (c h) t")
        m2 = V.op(ve.tensor_tensor, dv, dv, bc(con("madd", 64), 8), ALU.add, after=m1)
        dm = A.op(ae.activation, dv, dv, ACT.Exp, after=[m2])
        kb = V.op(ve.tensor_tensor, KB[:, :, :], QKV[:, 4:8, ts], h4(p2.ap), ALU.mult,
                  after=[d2] + qkv[4:8] + shared["kb"])
        p2.free = [kb]
        qd = V.op(ve.tensor_tensor, B["QD"][:, :, :], QKV[:, 0:4, ts], EG[:, :, :], ALU.mult,
                  after=[e] + qkv[0:4] + old)
        shared["eg"] = [qd]
        B["egl"] = A.op(ae.activation, B["EGL"][:, :, :], B["GL"][:, :, :], ACT.Exp, after=[gl])
        kd0 = V.op(ve.tensor_tensor, B["KDC"][:, :, :], B["GL"][0:64, :, :], COLT[:, 2 * b:2 * b + 2, 0:4],
                   ALU.subtract, after=[gl])
        kdc = A.op(ae.activation, B["KDC"][:, :, :], B["KDC"][:, :, :], ACT.Exp, after=[kd0])
        yield
        pk, after1 = bank()
        pq, after2 = bank()
        T.wait(after1 + after2 + qkv[0:8] + [kb])
        for u in range(8):
            c, h = divmod(u, 4)
            t0 = 64 * (2 * b + c)
            te.matmul(pk.ap[0:64, 64 * u:64 * u + 64], QKV[:, 4 + h, t0:t0 + 64], KB[:, h, 64 * c:64 * c + 64],
                      start=True, stop=True)
            ins = te.matmul(pq.ap[0:64, 64 * u:64 * u + 64], QKV[:, 4 + h, t0:t0 + 64], QKV[:, h, t0:t0 + 64],
                            start=True, stop=True)
        ins.then_inc(T.sem, 1)
        T.n += 1
        d = (T.sem, T.n)
        shared["kb"] = [d]
        u1 = V.op(ve.tensor_tensor, UU[:, :, :], v8(pk.ap), dv, ALU.mult, after=[d, dm] + shared["uu"])
        um = V.op(ve.tensor_tensor, UU[:, :, :], UU[:, :, :], bc(con("nstrict", 64), 8), ALU.mult, after=[u1])
        B["at"] = V.op(ve.tensor_tensor, B["AT"][:, :, :], v8(pq.ap), dv, ALU.mult, after=[d])
        pk.free, pq.free = [u1], [B["at"]]
        yield
        tk = []
        for c in range(2):
            n = 2 * b + c
            pk, after1 = bank()
            pv, after2 = bank()
            T.wait(after1 + after2 + qkv[8:12])
            for h in range(4):
                te.transpose(pk.ap[0:64, 128 * h:128 * h + 128], QKV[:, 4 + h, 64 * n:64 * n + 64], con("ident"))
                ins = te.transpose(pv.ap[0:64, 128 * h:128 * h + 128], QKV[:, 8 + h, 64 * n:64 * n + 64], con("ident"))
            ins.then_inc(T.sem, 1)
            T.n += 1
            d = (T.sem, T.n)
            k4, v4 = h4(pk.ap[0:64, :]), h4(pv.ap[0:64, :])
            q = slice(4 * c, 4 * c + 4)
            m1 = V.op(ve.tensor_tensor, B["KBT"][:, q, :], k4, cb(BEG[:, n, :]), ALU.mult, after=[d, bg] + old + free_x)
            m2 = V.op(ve.tensor_tensor, B["KDT"][:, q, :], k4, cb(B["KDC"][:, c, :]), ALU.mult, after=[d, kdc] + old)
            m3 = V.op(ve.tensor_tensor, B["VBT"][:, q, :], v4, cb(COLT[:, n, 32:36]), ALU.mult, after=[d] + old)
            pk.free, pv.free = [m2], [m3]
            tk += [m1, m2, m3]
            yield
        xm = yield from invert(inv, UU[:, :, :], [um], B["XX"][:, :, :], old)
        shared["uu"] = [xm]
        B["u"] = []
        for c in range(2):
            p, after = bank()
            T.wait(after + tk + [xm])
            for h in range(4):
                ins = te.matmul(p.ap[0:64, 128 * h:128 * h + 128], B["XX"][:, 4 * c + h, :], B["VBT"][:, 4 * c + h, :],
                                start=True, stop=True)
            ins.then_inc(T.sem, 1)
            T.n += 1
            B["u"].append(A.op(ae.activation, B["VBT"][:, 4 * c:4 * c + 4, :], h4(p.ap[0:64, :]), ACT.Copy,
                               after=[(T.sem, T.n)]))
            p.free = [B["u"][-1]]
            yield
        p, after = bank()
        T.wait(after)
        for u in range(8):
            ins = te.matmul(p.ap[:, 64 * u:64 * u + 64], B["KBT"][:, u, :], B["XX"][:, u, :], start=True, stop=True)
        ins.then_inc(T.sem, 1)
        T.n += 1
        B["wt"] = V.op(ve.tensor_copy, B["WT"][:, :, :], p.ap.rearrange("p (u t) -> p u t", u=8), after=[(T.sem, T.n)])
        p.free = [B["wt"]]
        B["ready"] = tk + [qd]

    og = []
    last = {"sd": [], "sm": sm}

    def scan1(b):
        B = BUF[b % 2]
        for c in range(2):
            n = 2 * b + c
            p, after = bank()
            T.wait(after + [B["wt"]] + last["sm"])
            for h in range(4):
                ins = te.matmul(p.ap[0:64, 128 * h:128 * h + 128], B["WT"][:, 4 * c + h, :], ST[:, h, :], start=True,
                                stop=True)
            ins.then_inc(T.sem, 1)
            T.n += 1
            vn = V.op(ve.tensor_tensor, VN[:, :, :], B["VBT"][:, 4 * c:4 * c + 4, :], h4(p.ap[0:64, :]), ALU.subtract,
                      after=[(T.sem, T.n), B["u"][c]] + last["sd"])
            p.free = [vn]
            yield
            p, after = bank()
            p2, after2 = bank()
            T.wait(after + after2 + [B["at"], vn] + B["ready"])
            for h in range(4):
                ins = te.matmul(p2.ap[:, 128 * h:128 * h + 128], B["KDT"][:, 4 * c + h, :], VN[:, h, :], start=True,
                                stop=True)
            ins.then_inc(T.sem, 1)
            T.n += 1
            sd = (T.sem, T.n)
            for h in range(4):
                te.matmul(p.ap[:, 64 * h:64 * h + 64], ST[:, h, :], B["QD"][:, h, 64 * c:64 * c + 64], start=True,
                          stop=False)
                ins = te.matmul(p.ap[:, 64 * h:64 * h + 64], VN[:, h, :], B["AT"][:, 4 * c + h, :], start=False,
                                stop=True)
            ins.then_inc(T.sem, 1)
            T.n += 1
            od = (T.sem, T.n)
            om = A.op(ae.activation, OG[:, 0:4, 64 * n:64 * n + 64], h4(p.ap[:, 0:256]), ACT.Copy, after=[od])
            p.free = [om]
            og.append(om)
            last["sm"] = [V.op(ve.scalar_tensor_tensor, ST[:, h, :], ST[:, h, :], B["EGL"][:, c, h:h + 1],
                               p2.ap[:, 128 * h:128 * h + 128], ALU.mult, ALU.add, after=[sd, od, B["egl"]])
                          for h in range(4)]
            p2.free = [last["sm"][-1]]
            last["sd"] = [od]
            yield
        B["done"] = [od, last["sm"][-1]]

    def delta_rule():
        yield from l2_norm()
        yield from prepare(0)
        for b in range(4):
            g = [scan1(b)] + ([prepare(b + 1)] if b < 3 else [])
            while g:
                for x in list(g):
                    if next(x, run) is run:
                        g.remove(x)
                    else:
                        yield

    run(project_rest(), delta_rule())
    proj_done, mod2, sc2 = rest["done"], rest["mod2"], rest["sc2"]
    S.wait([(T.sem, T.n), (V.sem, V.n)])
    se.dma_start(X[:, :, NM:T2], xT.rearrange("(k p) t -> p k t", p=128)).then_inc(s_x, 16)
    se.dma_start(X[:, :, 0:NM], metaT.rearrange("(k p) t -> p k t", p=128)).then_inc(s_x, 16)
    xback = [(s_x, 48)]
    zs = [A.op(ae.activation, Z[:, h, :], Z[:, h, :], ACT.Silu, after=[zm[h]]) for h in range(4)]
    for h in range(4):
        t = TMP[h % 3][:, 0:512]
        sq = A.op(ae.activation, t, OG[:, h, :], ACT.Square, after=[og[-1]] + tused[h % 3])
        p, after = bank()
        mm = T.op(te.matmul, p.ap, con("ones"), t, start=True, stop=True, after=after + [sq])
        r = A.op(ae.activation, t, p.ap, ACT.Sqrt, bias=EPSC[:, 0:1], scale=1.0 / 128, after=[mm])
        p.free = [r]
        r = V.op(ve.reciprocal, t, t, after=[r])
        y = V.op(ve.scalar_tensor_tensor, t, OG[:, h, :], col("gdn"), t, ALU.mult, ALU.mult, after=[r])
        y = V.op(ve.tensor_tensor, t, t, Z[:, h, :], ALU.mult, after=[y, zs[h]])
        hi = A.op(ae.activation, HH[:, h, NM:T2], t, ACT.Copy, after=[y, proj_done])
        lo = V.op(ve.tensor_tensor, HL[:, h, NM:T2], t, HH[:, h, NM:T2].bitcast(f32), ALU.subtract, after=[hi])
        tused[h % 3] = [lo]
        cat[h] = [hi, lo]
    xm = []
    for m in range(8):
        p, after = bank()
        d = gemm("w_out", m, p.ap, after, HH, HL, KT, H1, cat)
        xm.append([V.op(ve.scalar_tensor_tensor, X[:, m, NM:T2], p.ap, MOD[:, 16 + m:17 + m], X[:, m, NM:T2], ALU.mult,
                        ALU.add, after=[d, mod2] + xback)])
        p.free = [xm[-1][0]]
        if m == 0:
            stats = Stats(NM, flat(tused))
        else:
            stats.sum(m - 1)
        stats.square(m, xm[-1])
    mx.close()

    hm = rms(SC[:, 8:16], MOD[:, 24:32], NM, xm, [sc2, d] + flat(cat), st=stats)

    def fin1(m, ps, d):
        return V.op(ve.scalar_tensor_tensor, X[:, m, NM:T2], ps, MOD[:, 40 + m:41 + m], X[:, m, NM:T2],
                    ALU.mult, ALU.add, after=[d])

    xm, d, stats = ffn("f0", hm, NM, fin1, NM)
    xm = rms(CV[:, COLS["normf"]:COLS["normf"] + 8], None, NM, xm, [d], dst=X, st=stats)

    xm = [m + loaded for m in xm]

    def fin2(t0):
        def f(m, ps, d):
            n = T2 - t0
            xv = two(X[:, m, 0:n]) if t0 == 0 else X[:, m, t0:T2]
            return V.op(ve.scalar_tensor_tensor, xv, ps, 0.5, xv, ALU.mult, ALU.add, after=[d])
        return f

    hm = rms(CV[:, COLS["ffn1"]:COLS["ffn1"] + 8], None, 0, xm, [d])
    xm, d, stats = ffn("f1", hm, 0, fin2(0), 0)
    hm = rms(CV[:, COLS["mix"]:COLS["mix"] + 8], None, 0, xm, [d], st=stats)
    hall = flat(hm)

    rw = ExitStack()
    XSAVE = nc.dram_tensor("xsave", (128, KT * T1), f32, kind="Internal").ap()
    BSAVE = nc.dram_tensor("bsave", (128, 4 * T1), f32, kind="Internal").ap()
    s_xs = sem("s_xs")
    s_bs = sem("s_bs")
    S.wait([hm[-1][1]])
    se.dma_start(XSAVE.rearrange("p (k t) -> p k t", k=KT), X[:, :, NM:T2]).then_inc(s_xs, 16)
    xsaved = [(s_xs, 16)]
    KC[2] = sbuf("KC2", [128, 256], st=rw)
    QA = sbuf("QA", [128, 4, 512], st=rw)
    KA = sbuf("KA", [128, 4, 640], st=rw)
    VT = sbuf("VT", [128, 5, 512], st=rw)
    PM = sbuf("PM", [128, 1], st=rw)
    GUP = sbuf("GUP", [96, 512], st=rw)
    XG = sbuf("XG", [96, T2], st=rw)
    VB = sbuf("VB", [128, 4, 64 + TP], st=rw)
    AR = sbuf("AR", [128, 4, NCH, 2, 64], st=rw)
    BK = sbuf("BK", [128, 4, NCH, 2, 64], st=rw)
    WCC = sbuf("WCC", [128, 4, NCH], st=rw)
    KAM = sbuf("KAM", [128, 4], st=rw)
    el = ExitStack()
    LUP = sbuf("LUP", [64, 512], st=el)
    RES = sbuf("RES", [128, TP], st=el)
    LX = sbuf("LX", [64, T2], st=el)
    SG = [sbuf(f"SG{i}", [128, 1 + TP], st=el) for i in range(2)]
    VS = sbuf("VS", [128, 640], st=el)
    R1, K1, SW, SA, CS, KK, EX = (XF[:, TP * i:TP * i + TP] for i in range(7))
    s_k2 = sem("s_k2")
    S.wait(flat(hm))
    a2 = NCON[0] + NCON[1]
    se.dma_start(KC[2][:, :], consts[:, a2 + CON["tri"][1]:a2 + CON["tri"][1] + 256]).then_inc(s_k2, 16)
    CON["tri"], CON["m4"] = (2, 0, 128), (2, 128, 128)
    a2 += CON["reset2"][1]
    se.dma_start(RES[:, :], consts[:, a2:a2 + TP]).then_inc(s_k2, 16)
    se.dma_start(LUP[:, :], lup).then_inc(s_k2, 16)
    se.dma_start(GUP[:, :], gup).then_inc(s_k2, 16)
    k2 = [(s_k2, 64)]
    zr = [G.op(ge.memset, t[:, 0:PAD + 1], 0.0, after=hm[-1]) for t in SG]
    zr.append(G.op(ge.memset, VB[:, :, 0:64], 0.0))
    zr.append(G.op(ge.memset, KA[:, :, 0:112], 0.0))
    zr.append(G.op(ge.memset, VS[:, 0:112], 0.0))
    zr += [G.op(ge.memset, t[:, 0:PAD], 0.0, after=xsaved) for t in (SW, SA)]
    pm0 = G.op(ge.memset, PM[:, :], 1.0)
    pmk = G.op(ge.affine_select, out=PM[:, :], in_=PM[:, :], pattern=[[0, 1]], compare_op=ALU.is_ge, fill=0.0,
               base=-112, channel_multiplier=1, after=[pm0])
    V.wait(zr)
    A.wait(zr)
    c1 = A.op(ae.activation, TRIR[:, :], con("tri"), ACT.Copy, after=k2)
    kam = V.op(ve.tensor_scalar, KAM[:, :], CV[:, COLS["ka"]:COLS["ka"] + 4], -1.0, 1.0, ALU.mult, ALU.add)

    sgused = [[], []]
    nst = [0]

    def shifted(which, j, dst, mucol, rows, dused):
        b = nst[0] % 2
        nst[0] += 1
        s = SG[b]
        p, after = pair()
        d = gemm(which, j, p[1], after, HH, HL, KT, H2, hm)
        ev = A.op(ae.activation, two(s[:, 1 + PAD:1 + TP]), p[1], ACT.Copy, after=[d] + sgused[b])
        free_pair(p, [ev])
        df = V.op(ve.tensor_tensor, dst[0:rows], s[0:rows, 0:TP], s[0:rows, 1:1 + TP], ALU.subtract,
                  after=[ev] + dused)
        m = V.op(ve.scalar_tensor_tensor, dst[0:rows], dst[0:rows], col("mu", mucol, 0, rows), s[0:rows, 1:1 + TP],
                 ALU.mult, ALU.add, after=[df])
        sgused[b] = [m]
        return m

    m = shifted("lora", 0, R1, 12, 64, [])
    lx1 = A.op(ae.activation, LX[0:32, :], R1[0:32, PAD:TP], ACT.Tanh, after=[m])
    lx2 = A.op(ae.activation, LX[32:64, :], R1[32:64, PAD:TP], ACT.Copy, after=[m])
    m = shifted("lora", 1, K1, 13, 96, [])
    xg = A.op(ae.activation, XG[:, :], K1[0:96, PAD:TP], ACT.Sigmoid, after=[m])
    used = {x: [] for x in ("R1", "K1", "SW", "SA", "CS", "KK", "EX")}
    used["R1"], used["K1"] = [lx1, lx2], [xg]
    feats, vmarks, bonm, wcm = [], [], [], []
    qm, km, vtm, vsu = [], [], [], []

    def ch(ap):
        return ap.rearrange("p (n t) -> p n t", t=64)

    def features(i, r1, k1m, vm):
        for dst, r0, bias, nm in ((SW, 0, "w0", "SW"), (SA, 32, "a0", "SA")):
            p, after = pair()
            T.wait(after + [lx1, lx2] + k2)
            for q in range(2):
                ins = te.matmul(p[1][:, q, :], LUP[r0:r0 + 32, 128 * i:128 * i + 128],
                                LX[r0:r0 + 32, 264 * q:264 * q + 264], start=True, stop=True)
            ins.then_inc(T.sem, 1)
            T.n += 1
            sg = A.op(ae.activation, two(dst[:, PAD:TP]), p[1], ACT.Sigmoid, bias=col(bias, i),
                      after=[(T.sem, T.n)] + used[nm])
            free_pair(p, [sg])
            if nm == "SW":
                sw = sg
            else:
                sa = sg
        yield
        cs = V.op(ve.tensor_tensor_scan, CS, RES[:, :], SW, 0.0, ALU.mult, ALU.add, after=[sw] + k2 + used["CS"])
        kk = V.op(ve.tensor_scalar, KK, K1, col("kk", i), None, ALU.mult, after=[k1m] + used["KK"])
        sq = A.op(ae.activation, EX, KK, ACT.Square, after=[kk] + used["EX"])
        p, after = pair()
        T.wait(after + [sq])
        pv = PS[:, p[0]:p[0] + 2, 0:288]
        for q in range(2):
            ins = te.matmul(pv[:, q, :], con("bones"), EX[:, 288 * q:288 * q + 288], start=True, stop=True)
        ins.then_inc(T.sem, 1)
        T.n += 1
        yield
        dcs = V.op(ve.tensor_tensor, SW, CS, SW, ALU.subtract, after=[cs])
        mxm = V.op(ve.tensor_scalar, two(EX), pv, 1e-24, None, ALU.max, after=[(T.sem, T.n)])
        free_pair(p, [mxm])
        sr = A.op(ae.activation, EX, EX, ACT.Sqrt, after=[mxm])
        rc = V.op(ve.reciprocal, EX, EX, after=[sr])
        yield
        kn = V.op(ve.tensor_tensor, KK, KK, EX, ALU.mult, after=[rc])
        e1 = A.op(ae.activation, EX, CS, ACT.Exp, scale=-KAPPA, after=[cs, kn])
        e1p = A.op(ae.activation, SW, SW, ACT.Exp, scale=-KAPPA, after=[dcs])
        f1 = V.op(ve.tensor_tensor, AR[:, i, :, 1, :], ch(R1), ch(EX), ALU.mult, after=[e1, r1])
        wc = V.op(ve.tensor_copy, WCC[:, i, :], ch(EX)[:, :, 63], after=[e1])
        wcm.append(wc)
        yield
        e2 = A.op(ae.activation, EX, CS, ACT.Exp, scale=KAPPA, after=[f1, wc])
        f2 = V.op(ve.scalar_tensor_tensor, AR[:, i, :, 0, :], ch(KK), -1.0, ch(SW), ALU.mult, ALU.mult,
                  after=[kn, e1p])
        bm = V.op(ve.tensor_tensor, KK, KK, SA, ALU.mult, after=[f2, sa])
        yield
        f3 = V.op(ve.tensor_tensor, BK[:, i, :, 0, :], ch(KK), ch(EX), ALU.mult, after=[bm, e2])
        tm = V.op(ve.tensor_scalar, SA, SA, col("ka", i), KAM[:, i:i + 1], ALU.mult, ALU.add, after=[bm, kam])
        kf = V.op(ve.tensor_tensor, K1, K1, SA, ALU.mult, after=[tm, kk])
        yield
        f4 = V.op(ve.tensor_tensor, BK[:, i, :, 1, :], ch(K1), ch(EX), ALU.mult, after=[kf, e2])
        bo = V.op(ve.scalar_tensor_tensor, K1[:, 64:TP], R1[:, 64:TP], col("rk", i), K1[:, 64:TP], ALU.mult,
                  ALU.mult, after=[kf, r1, f4])
        p, after = bank()
        mm = T.op(te.matmul, p.ap, con("bones"), K1[:, 64:TP], start=True, stop=True, after=after + [bo])
        yield
        t = TMP[i % 3][:, 0:512]
        bn = V.op(ve.tensor_tensor, t, VB[:, i, 128:64 + TP], p.ap, ALU.mult, after=[mm, vm] +
                  ([(s_bs, 16)] if i == 3 else []))
        p.free = [bn]
        S.wait([bn])
        se.dma_start(BSAVE[:, 512 * i:512 * i + 512], t).then_inc(s_bs, 16)
        bonm.append(bn)
        used.update({"R1": [f1, bo], "K1": [f4, mm], "SW": [f2], "SA": [kf], "CS": [e2, dcs], "KK": [f3], "EX": [f4]})
        feats.append([f1, f2, f3, f4])

    def attention_inputs(i):
        p, after = pair()
        d = yield from gemm_steps("w_in2", 12 + i, p[1], after, HH, HL, KT, H2, hm)
        A.op(ae.activation, QA[:, i, 0:248], p[1][:, 0, 16:264], ACT.Copy, scale=0.125, after=[d])
        m2 = A.op(ae.activation, QA[:, i, 248:512], p[1][:, 1, :], ACT.Copy, scale=0.125)
        free_pair(p, [m2])
        qm.append(m2)
        p, after = pair()
        d = yield from gemm_steps("w_in2", 16 + i, p[1], after, HH, HL, KT, H2, hm)
        m = A.op(ae.activation, two(KA[:, i, 112:640]), p[1], ACT.Copy, after=[d])
        free_pair(p, [m])
        km.append(m)
        p, after = pair()
        d = yield from gemm_steps("w_in2", 20 + i, p[1], after, HH, HL, KT, H2, hm)
        m = A.op(ae.activation, two(VS[:, 112:640]), p[1], ACT.Copy, after=[d] + vsu[-1:])
        free_pair(p, [m])
        yield
        p, after = bank()
        q, after2 = bank()
        T.wait(after + after2 + [m])
        for j in range(5):
            o = p.ap[:, 128 * j:128 * j + 128] if j < 4 else q.ap[:, 0:128]
            ins = te.transpose(o, VS[:, 128 * j:128 * j + 128], con("ident"))
        ins.then_inc(T.sem, 1)
        T.n += 1
        d = (T.sem, T.n)
        vsu.append(d)
        m1 = A.op(ae.activation, VT[:, 0:4, 128 * i:128 * i + 128], p.ap.rearrange("p (j t) -> p j t", j=4), ACT.Copy,
                  after=[d])
        m2 = A.op(ae.activation, VT[:, 4, 128 * i:128 * i + 128], q.ap[:, 0:128], ACT.Copy)
        p.free, q.free = [m1], [m2]
        vtm.extend([m1, m2])

    for i in range(4):
        r1 = shifted("w_in2", 3 * i, R1, i, 128, used["R1"])
        k1m = shifted("w_in2", 3 * i + 1, K1, 4 + i, 128, used["K1"])
        vm = shifted("w_in2", 3 * i + 2, VB[:, i, 64:64 + TP], 8 + i, 128, [])
        vmarks.append(vm)
        run(features(i, r1, k1m, vm), attention_inputs(i))
    proj_done = (T.sem, T.n)
    el.close()

    ck = ExitStack()
    ae.preload_act_table_set("natural_log_exp_and_others")
    inv = Inverse(ck, "rv")
    V0 = sbuf("V0", [128, 8, 64], st=ck)
    SB = sbuf("SB", [128, 4, 2, 64], st=ck)
    RH = RAWS[0:64, 3584:4096].rearrange("p (u t) -> p u t", u=8)
    ATT = [RAWS[:, 1792 * i:1792 * i + 1792] for i in range(2)]
    BUF = []
    for i in range(2):
        o = 2112 * i
        BUF.append({"MM": XF[:, o:o + 1024].rearrange("p (h t) -> p h t", h=8),
                    "SV": XF[:, o + 1024:o + 1536].rearrange("p (h t) -> p h t", h=8),
                    "BKT": XF[:, o + 1536:o + 2048].rearrange("p (h t) -> p h t", h=8),
                    "XX": sbuf(f"RX{i}", [64, 8, 64], st=ck), "done": []})
    fall = flat(feats) + bonm + [(T.sem, T.n)]
    z1 = G.op(ge.memset, V0[0:64, :, :], 0.0, after=fall)
    z2 = G.op(ge.memset, SB[:, :, :, :], 0.0)
    rws = {"sm": [z2], "v0": []}
    y_marks = []
    A.wait(fall)
    V.wait([z1])

    def rw_prepare(n):
        B = BUF[n % 2]
        MM, SV, BKT = B["MM"], B["SV"], B["BKT"]
        old = B["done"]
        b0, after0 = bank()
        b1, after1 = bank()
        T.wait(after0 + after1 + flat(feats) + [z1])
        for h in range(8):
            i, par = divmod(h, 2)
            pb = 64 * par
            ins = te.matmul((b0, b1)[par].ap[:, 128 * i:128 * i + 128],
                            BK[pb:pb + 64, i, n, :, :].rearrange("p a t -> p (a t)"),
                            AR[pb:pb + 64, i, n, :, :].rearrange("p a t -> p (a t)"), start=True, stop=True)
        ins.then_inc(T.sem, 1)
        T.n += 1
        d = (T.sem, T.n)
        M2 = MM.rearrange("p (i a) t -> p i a t", a=2)
        mms = []
        for par in range(2):
            p = (b0, b1)[par]
            m = V.op(ve.tensor_tensor, M2[:, :, par, :], p.ap.rearrange("p (i t) -> p i t", i=4),
                     con("m4").unsqueeze(1).broadcast_to([128, 4, 128]), ALU.mult, after=[d] + old)
            p.free = [m]
            mms.append(m)
        B["mm"] = mms
        yield
        pk, after1 = bank()
        pv, after2 = bank()
        T.wait(after1 + after2 + vmarks)
        for i in range(4):
            te.transpose(pk.ap[:, 128 * i:128 * i + 128], BK[:, i, n, :, :].rearrange("p a t -> p (a t)"),
                         con("ident"))
            ins = te.transpose(pv.ap[:, 128 * i:128 * i + 128], VB[:, i, 64 * n:64 * n + 128], con("ident"))
        ins.then_inc(T.sem, 1)
        T.n += 1
        d = (T.sem, T.n)
        bt = A.op(ae.activation, BKT, pk.ap.rearrange("p (h t) -> p h t", h=8), ACT.Copy, after=[d] + old)
        v1 = A.op(ae.activation, SV[64:128], pv.ap[64:128, :].rearrange("p (h t) -> p h t", h=8), ACT.Copy, after=old)
        pk.free, pv.free = [bt], [v1]
        B["tok"] = [bt, v1]
        yield
        B["x"] = yield from invert(inv, MM[0:64, :, 0:64], mms, B["XX"][:, :, :], old)

    def rw_scan(n):
        B = BUF[n % 2]
        MM, SV, BKT = B["MM"], B["SV"], B["BKT"]
        v0 = G.op(ge.tensor_copy, V0[64:128, :, :], SV[64:128], after=B["tok"] + rws["v0"] + [(G.sem, G.n)])
        p, after = bank()
        T.wait(after + rws["sm"] + [v0] + B["mm"])
        for i in range(4):
            te.matmul(p.ap[0:64, 128 * i:128 * i + 128], AR[:, i, n, 0, :],
                      SB[:, i, :, :].rearrange("p a t -> p (a t)"), start=True, stop=True)
            for par in range(2):
                h = 2 * i + par
                ins = te.matmul(p.ap[0:64, 64 * h:64 * h + 64], MM[:, h, 0:64], V0[:, h, :], start=False,
                                stop=True, skip_group_check=True)
        ins.then_inc(T.sem, 1)
        T.n += 1
        d = (T.sem, T.n)
        rws["v0"] = [d]
        rh = V.op(ve.tensor_copy, RH, p.ap[0:64, :].rearrange("p (h t) -> p h t", h=8), after=[d])
        p.free = [rh]
        yield
        p, o, d = products(B["XX"], RH, [rh, B["x"]])
        sv = V.op(ve.tensor_copy, SV[0:64], o, after=[d])
        p.free = [sv]
        yield
        p, after = bank()
        T.wait(after + B["tok"] + [sv])
        for h in range(8):
            i, par = divmod(h, 2)
            ins = te.matmul(p.ap[64 * par:64 * par + 64, 64 * i:64 * i + 64], BKT[:, h, :], SV[:, h, :],
                            start=True, stop=True)
        ins.then_inc(T.sem, 1)
        T.n += 1
        sd = (T.sem, T.n)
        yd = sd
        if n:
            p2, after = bank()
            T.wait(after)
            for i in range(4):
                te.matmul(p2.ap[:, 64 * i:64 * i + 64], SB[:, i, :, :].rearrange("p a t -> p (a t)"),
                          AR[:, i, n, 1, :], start=True, stop=True)
                for par in range(2):
                    h = 2 * i + par
                    ins = te.matmul(p2.ap[64 * par:64 * par + 64, 64 * i:64 * i + 64], SV[:, h, :], MM[:, h, 64:128],
                                    start=False, stop=True, skip_group_check=True)
            ins.then_inc(T.sem, 1)
            T.n += 1
            yd = (T.sem, T.n)
            ym = A.op(ae.activation, AR[:, :, n, 1, :], p2.ap[:, 0:256].rearrange("p (i t) -> p i t", i=4),
                      ACT.Copy, after=[yd])
            p2.free = [ym]
            y_marks.append(ym)
        sm = []
        for par in range(2):
            q = slice(64 * par, 64 * par + 64)
            pp = p.ap[q, 0:256].rearrange("p (i t) -> p i t", i=4)
            s1 = V.op(ve.tensor_tensor, SB[q, :, par, :], pp, SB[q, :, par, :], ALU.add, after=[sd, yd])
            sm.append(V.op(ve.tensor_tensor, SB[q, :, par, :], SB[q, :, par, :],
                           WCC[q, :, n:n + 1].broadcast_to([64, 4, 64]), ALU.mult, after=[s1] + wcm))
        p.free = [s1]
        rws["sm"] = sm
        B["done"] = [yd, v0]
        yield

    def rwkv():
        yield from rw_prepare(0)
        for n in range(NCH):
            g = [rw_scan(n)] + ([rw_prepare(n + 1)] if n + 1 < NCH else [])
            while g:
                for x in list(g):
                    if next(x, run) is run:
                        g.remove(x)
                    else:
                        yield

    OFF = [0, 512, 1024, 1408, 1664]
    LEN = [512, 512, 384, 256, 128]
    flatr = lambda t, a: t[:, a:a + 4, :].rearrange("p k t -> p (k t)")
    KHI = [flatr(HH, 0), flatr(HH, 4)]
    KLO = [flatr(HL, 0), flatr(HL, 4)]
    TT = [[TMP[0], TMP[1]], [TMP[2], RSTD]]
    ttu = [[[(s_bs, 64)], [(s_bs, 64)]], [[(s_bs, 64)], [(s_bs, 64)]]]
    khu = [[proj_done], [proj_done]]
    atu = [[], []]
    sbm = [None] * 8

    def heads(b):
        nt = 0
        for i in range(4):
            h = 2 * i + b
            pb = 64 * b
            am = []
            for j in (4, 3, 2, 1, 0):
                n = LEN[j]
                p, after = bank()
                T.wait(after + qm + km)
                z = T.op(te.matmul, p.ap[:, 0:n], KA[pb:pb + 64, i, 128 * j:128 * j + 128],
                         QA[pb:pb + 64, i, 512 - n:512], start=True, stop=True)
                t = TT[b][nt % 2]
                a1 = A.op(ae.activation, t[:, 0:n], p.ap[:, 0:n], ACT.Abs, after=[z] + ttu[b][nt % 2])
                a2 = A.op(ae.activation, t[:, 0:n], t[:, 0:n], ACT.Exp, scale=-1.0, after=[a1])
                a3 = A.op(ae.activation, t[:, 0:n], t[:, 0:n], ACT.Ln, bias=1.0, after=[a2])
                yield
                m = V.op(ve.scalar_tensor_tensor, t[:, 0:n], p.ap[:, 0:n], 0.0, t[:, 0:n], ALU.max, ALU.add,
                         after=[a3])
                if j:
                    m = G.op(ge.affine_select, out=t[:, 0:128], in_=t[:, 0:128], pattern=[[1, 128]],
                             compare_op=ALU.is_gt, fill=0.0, base=0, channel_multiplier=-1,
                             after=[m, (G.sem, G.n)])
                else:
                    m = V.op(ve.tensor_scalar, t[:, 0:n], t[:, 0:n], PM[:, 0:1], None, ALU.mult, after=[m, pmk])
                yield
                o = slice(OFF[j], OFF[j] + n)
                hi = A.op(ae.activation, KHI[b][:, o], t[:, 0:n], ACT.Copy, scale=-1.0, after=[m] + khu[b])
                lo = V.op(ve.scalar_tensor_tensor, KLO[b][:, o], t[:, 0:n], -1.0, KHI[b][:, o].bitcast(f32), ALU.mult,
                          ALU.subtract, after=[hi, m] + khu[b])
                ttu[b][nt % 2] = [lo, hi]
                nt += 1
                yield
                T.wait([hi, lo])
                for q in range(4, j - 1, -1):
                    w = TRIR if q == j else ONER
                    for part in (KHI[b], KLO[b]):
                        ins = te.matmul(p.ap[:, n - LEN[q]:n], w[:, :], part[:, OFF[q]:OFF[q] + LEN[q]], start=False,
                                        stop=True, skip_group_check=True)
                ins.then_inc(T.sem, 1)
                T.n += 1
                d = (T.sem, T.n)
                yield
                e = A.op(ae.activation, ATT[b][:, o], p.ap[:, 0:n], ACT.Exp, after=[d] + atu[b])
                p.free = [e]
                if j:
                    e = G.op(ge.affine_select, out=ATT[b][:, OFF[j]:OFF[j] + 128], in_=ATT[b][:, OFF[j]:OFF[j] + 128],
                             pattern=[[1, 128]], compare_op=ALU.is_gt, fill=0.0, base=0, channel_multiplier=-1,
                             after=[e, (G.sem, G.n)])
                am.append(e)
                yield
            khu[b] = [d]
            p, after = bank()
            T.wait(after + am + vtm)
            for j in range(5):
                ins = te.matmul(p.ap[pb:pb + 64, 512 - LEN[j]:512], VT[:, j, 64 * h:64 * h + 64],
                                ATT[b][:, OFF[j]:OFF[j] + LEN[j]], start=(j == 0), stop=(j == 4))
            ins.then_inc(T.sem, 1)
            T.n += 1
            d = (T.sem, T.n)
            atu[b] = [d]
            sbm[h] = A.op(ae.activation, QA[pb:pb + 64, i, :], p.ap[pb:pb + 64, :], ACT.Copy, after=[d])
            p.free = [sbm[h]]
            yield

    run(rwkv(), heads(0), heads(1))
    ck.close()

    resume()
    alldone = [(e.sem, e.n) for e in (V, A, G, T)]
    S.wait(alldone)
    se.dma_start(X[:, :, NM:T2], XSAVE.rearrange("p (k t) -> p k t", k=KT)).then_inc(s_xs, 16)
    xback = [(s_xs, 32)]
    BON = sbuf("BON", [128, 4, 512], st=rw)
    se.dma_start(BON[:, :, :].rearrange("p k t -> p (k t)"), BSAVE).then_inc(s_bs, 16)
    bback = [(s_bs, 80)]
    EPL = sbuf("EPL", [128, 1], st=rw)
    TL = [sbuf(f"TL{i}", [128, 512], st=rw) for i in range(4)]
    epl = G.op(ge.memset, EPL[:, :], 64e-5, after=alldone)
    A.wait(alldone)
    V.wait(alldone)
    cat = [None] * 8
    for j in range(4):
        hi = A.op(ae.activation, HH[:, j, NM:T2], QA[:, j, :], ACT.Copy)
        lo = V.op(ve.tensor_tensor, HL[:, j, NM:T2], QA[:, j, :], HH[:, j, NM:T2].bitcast(f32), ALU.subtract,
                  after=[hi])
        cat[j] = [hi, lo]
    tlu = [[], []]

    def group_norm(i):
        y3 = AR[:, i, 1:NCH, 1, :]
        pp, after = bank()
        T.wait(after + y_marks)
        mm = T.op(te.matmul, pp.ap, con("bones"), y3, start=True, stop=True)
        yield
        t, sq = TL[2 * (i % 2)], TL[2 * (i % 2) + 1]
        c = V.op(ve.scalar_tensor_tensor, ch(t[:, :]), ch(pp.ap), -1.0 / 64, y3, ALU.mult, ALU.add,
                 after=[mm] + tlu[i % 2])
        pp.free = [c]
        s2 = A.op(ae.activation, sq[:, :], t[:, :], ACT.Square, after=[c])
        yield
        pp, after = bank()
        mm = T.op(te.matmul, pp.ap, con("bones"), sq[:, :], start=True, stop=True, after=after + [s2])
        yield
        r = A.op(ae.activation, sq[:, :], pp.ap, ACT.Sqrt, bias=EPL[:, 0:1], scale=1.0 / 64, after=[mm, epl])
        pp.free = [r]
        yield
        r = V.op(ve.reciprocal, sq[:, :], sq[:, :], after=[r])
        m = V.op(ve.tensor_tensor, t[:, :], t[:, :], sq[:, :], ALU.mult, after=[r])
        m = V.op(ve.tensor_scalar, t[:, :], t[:, :], col("lnw", i), col("lnb", i), ALU.mult, ALU.add, after=[m])
        m = V.op(ve.tensor_tensor, t[:, :], BON[:, i, :], t[:, :], ALU.add, after=[m] + bback)
        yield
        pp, after = bank()
        mm = T.op(te.matmul, pp.ap, GUP[0:96, 128 * i:128 * i + 128], XG[0:96, NM:T2], start=True, stop=True,
                  after=after + [xg])
        m = V.op(ve.tensor_tensor, t[:, :], t[:, :], pp.ap, ALU.mult, after=[mm, m])
        pp.free = [m]
        hi = A.op(ae.activation, HH[:, 4 + i, NM:T2], t[:, :], ACT.Copy, after=[m])
        lo = V.op(ve.tensor_tensor, HL[:, 4 + i, NM:T2], t[:, :], HH[:, 4 + i, NM:T2].bitcast(f32),
                  ALU.subtract, after=[hi])
        tlu[i % 2] = [lo]
        cat[4 + i] = [hi, lo]

    run(group_norm(0), group_norm(1))
    run(group_norm(2), group_norm(3))
    xn = []
    for m in range(8):
        p, after = bank()
        d = gemm("w_out2", m, p.ap, after, HH, HL, KT, H1, cat)
        xn.append([V.op(ve.tensor_tensor, X[:, m, NM:T2], p.ap, X[:, m, NM:T2], ALU.add, after=[d] + xback)])
        p.free = [xn[-1][0]]
        if m == 0:
            stats = Stats(NM, alldone)
        else:
            stats.sum(m - 1)
        stats.square(m, xn[-1])
    rw.close()
    hm = rms(CV[:, COLS["ffn2"]:COLS["ffn2"] + 8], None, NM, xn, [d] + flat(cat), st=stats)
    xm, d, stats = ffn("f2", hm, NM, fin2(NM), NM)
    xm = rms(CV[:, COLS["final"]:COLS["final"] + 8], None, NM, xm, [d], dst=X, st=stats)

    s_out = sem("s_out")
    S.wait(flat(xm))
    se.dma_start(out.rearrange("(k p) t -> p k t", p=128), X[:, :, NM:T2]).then_inc(s_out, 16)
    se.wait_ge(s_out, 16)
    top.close()


def host(inputs):
    import numpy as np
    g = {k: np.asarray(v) for k, v in inputs.items()}
    z = lambda *s: np.zeros(s, np.float32)

    def cv(v):
        v = v.reshape(-1)
        n = -(-v.size // 128)
        o = z(n * 128)
        o[:v.size] = v
        return o.reshape(n, 128).T

    mu = g["rwkv_mu_2"][0]
    cat = [g["c"], g["b_ada"], g["norm1_w"], g["conv_qkv_w"], g["conv_short_w"], g["gdn_norm_w"], g["norm2_w"],
           g["norm_f_w"], g["ffn1_norm_2"], g["mix_norm_2"], (mu[:1536], mu[1536:1600], mu[1600:]), g["rwkv_w0_2"],
           g["rwkv_a0_2"], g["rwkv_k_k_2"], g["rwkv_k_a_2"], g["rwkv_r_k_2"], g["rwkv_lnx_w_2"], g["rwkv_lnx_b_2"],
           g["ffn2_norm_2"], g["final_norm_2"], g["A_log"], g["dt_bias"]]
    cols = np.concatenate([np.concatenate([cv(x) for x in v], 1) if isinstance(v, tuple) else cv(v) for v in cat], 1)
    assert cols.shape[1] == NCOL, cols.shape

    con = z(128, sum(NCON))

    def put(n, v):
        g_, a, k = CON[n]
        a += sum(NCON[:g_])
        con[:v.shape[0], a:a + k] = v

    i = np.arange(128)
    s, t = i[:, None], i[None, :]
    put("ident", (s == t) * np.float32(1))
    put("ones", np.ones((128, 128), np.float32))
    put("bones", (s // 64 == t // 64) * np.float32(1))
    put("tri", (s >= t) * np.float32(1))
    put("m4", np.where(t < 64, s % 64 < t % 64, s % 64 <= t % 64) * np.float32(1))
    s, t = s[:64], t[:, :64]
    put("b16", (s // 16 == t // 16) * np.float32(1))
    c32 = ((s // 32 == t // 32) & (s // 16 != t // 16)) * np.float32(1)
    c64 = (s // 32 != t // 32) * np.float32(1)
    put("c32", c32)
    put("c64", c64)
    put("madd", np.where(s <= t, 0, -1e30).astype(np.float32))
    put("nstrict", np.where(s < t, -1, 0).astype(np.float32))
    put("reset1", np.broadcast_to((np.arange(512) % 64 != 0) * np.float32(1), (128, 512)))
    put("reset2", np.broadcast_to((np.arange(TP) % 64 != 0) * np.float32(1), (128, TP)))
    sel = z(64, 8, 128)
    for h in range(4):
        sel[h, h] = 1
        sel[32 + h, 4 + h] = 1
    put("sel", sel.reshape(64, 1024))

    def tiles(w):
        K, M = w.shape
        return np.ascontiguousarray(w.reshape(K // 128, 128, M // 128, 128).transpose(2, 1, 0, 3)).reshape(M // 128, 128, -1)

    def down(w):
        o = z(24, 128, 1024)
        a = tiles(w)
        for m in range(8):
            o[3 * m] = a[m][:, :1024]
            o[3 * m + 1] = a[m][:, 1024:2048]
            o[3 * m + 2, :, :768] = a[m][:, 2048:]
        return o

    w_in = g["w_in"][0]
    ab = z(1024, 64)
    ab[:, 0:4] = w_in[:, 2048:2052]
    ab[:, 32:36] = w_in[:, 2052:2056]
    sb, sc, sh = (tiles(w_in[:, 2056 + 512 * i:2568 + 512 * i]) for i in range(3))
    w = {"ada": tiles(g["w_ada"][0]),
         "ab": np.ascontiguousarray(ab.reshape(8, 128, 64).transpose(1, 0, 2)).reshape(1, 128, 512),
         "w_in": np.concatenate([tiles(w_in[:, :2048]), np.stack([sc, sh, sb], 1).reshape(12, 128, 1024)], 0),
         "w_out": tiles(g["w_out"][0])}
    v = g["w_in_2"][0]
    lo = z(1024, 256)
    lo[:, 0:64] = v[:, 3072:3136]
    lo[:, 128:224] = v[:, 3136:3232]
    r, k, vv = (tiles(v[:, 1536 + 512 * i:2048 + 512 * i]) for i in range(3))
    w["lora"] = tiles(lo)
    w["w_in2"] = np.concatenate([np.stack([r, k, vv], 1).reshape(12, 128, 1024), tiles(v[:, :1536])], 0)
    w["w_out2"] = tiles(g["w_out_2"][0])
    for f, pre in (("f0", ""), ("f1", "ffn1_"), ("f2", "ffn2_")):
        post = "_2" if pre else ""
        w[f + "g"] = tiles(g[pre + "w_gate" + post][0])
        w[f + "u"] = tiles(g[pre + "w_up" + post][0])
        w[f + "d"] = down(g[pre + "w_down" + post][0])
    arrays = {"xT": np.ascontiguousarray(g["x"][0].T), "metaT": np.ascontiguousarray(g["meta_tokens_2"].T),
              "cols": np.ascontiguousarray(cols), "consts": con}
    arrays["lup"] = np.ascontiguousarray(np.concatenate([g["rwkv_w_up_2"][0], g["rwkv_a_up_2"][0]], 0))
    arrays["gup"] = np.ascontiguousarray(g["rwkv_g_up_2"][0])
    for n, a in w.items():
        arrays["w_" + n] = a
    return arrays


def kernel(**inputs):
    import numpy as _np
    import concourse.bacc as _bacc
    from concourse import mybir as _mybir
    from concourse.bass_utils import run_bass_kernel_spmd as _run

    arrays = host(inputs)
    nc = _bacc.Bacc("TRN2", target_bir_lowering=False, num_devices=1)
    f32 = _mybir.dt.float32
    ap = {n: nc.dram_tensor(n, a.shape, f32, kind="ExternalInput").ap() for n, a in arrays.items()}
    out = nc.dram_tensor("out", (D, T1), f32, kind="ExternalOutput").ap()
    slabs = {n[2:]: a for n, a in ap.items() if n.startswith("w_")}
    program(nc, ap["xT"], ap["metaT"], ap["cols"], ap["consts"], slabs, ap["lup"], ap["gup"], out)
    r = _run(nc, [arrays], core_ids=[0])
    return _np.ascontiguousarray(r.results[0]["out"].T)[None]
```

```python
import concourse.bass as bass
from concourse import mybir
from contextlib import ExitStack

D = 1024
T1 = 512
NM = 16
T2 = T1 + NM
KT = 8
FT = 22
SLAB = 1024
EPS = 1e-6
KAPPA = 0.6065306597126334
PAD = 48
TP = T2 + PAD
NCH = 9

COLS = {}
_at = 0
for _n, _k in (("c", 8), ("b_ada", 48), ("norm1", 8), ("convq", 48), ("convs", 12), ("gdn", 1), ("norm2", 8),
               ("normf", 8), ("ffn1", 8), ("mix", 8), ("mu", 14), ("w0", 4), ("a0", 4), ("kk", 4), ("ka", 4),
               ("rk", 4), ("lnw", 4), ("lnb", 4), ("ffn2", 8), ("final", 8), ("alog", 1), ("dtb", 1)):
    COLS[_n] = _at
    _at += _k
NCOL = _at

CON = {}
NCON = [0, 0, 0]
for _g, _n, _k in ((0, "ident", 128), (0, "ones", 128), (0, "bones", 128), (0, "b16", 64), (0, "c32", 64), (0, "c64", 64), (0, "i2", 64),
                   (1, "madd", 64), (1, "nstrict", 64), (1, "sel", 1024), (2, "reset1", 512),
                   (2, "tri", 128), (2, "m4", 128), (2, "reset2", TP)):
    CON[_n] = (_g, NCON[_g], _k)
    NCON[_g] += _k



class Engine:

    def __init__(self, eng, sem):
        self.eng, self.sem, self.n, self.seen = eng, sem, 0, {}

    def wait(self, marks):
        for sem, n in marks:
            if self.seen.get(sem.name, 0) < n:
                self.eng.wait_ge(sem, n)
                self.seen[sem.name] = n

    def op(self, f, *a, after=(), **k):
        self.wait(after)
        f(*a, **k).then_inc(self.sem, 1)
        self.n += 1
        return (self.sem, self.n)

    def quiet(self, f, *a, after=(), **k):
        self.wait(after)
        f(*a, **k)


class Bank:
    def __init__(self, ap):
        self.ap, self.free = ap, []


def program(nc, xT, metaT, cols, consts, slabs, lup, gup, out):
    f32, f32r = mybir.dt.float32, mybir.dt.float32r
    ALU, ACT = mybir.AluOpType, mybir.ActivationFunctionType
    ve, ae, ge, te, se = nc.vector, nc.scalar, nc.gpsimd, nc.tensor, nc.sync
    top = ExitStack()

    def sem(name):
        return top.enter_context(nc.semaphore(name))

    def sbuf(name, shape, dt=f32, st=top):
        return st.enter_context(nc.sbuf_tensor(name, shape, dt))

    V, A, G, T = Engine(ve, sem("s_v")), Engine(ae, sem("s_a")), Engine(ge, sem("s_g")), Engine(te, sem("s_t"))
    S = Engine(se, sem("s_s"))
    PS = top.enter_context(nc.psum_tensor("PS", [128, 8, 512], f32))
    banks = [Bank(PS[:, i, :]) for i in range(8)]
    pairs = [Bank(PS[:, 2 * i:2 * i + 2, 0:264]) for i in range(4)]
    turn = [0]

    def bank():
        for _ in range(8):
            b = banks[turn[0] % 8]
            turn[0] += 1
            if b.free is not None:
                break
        after = b.free
        b.free = None
        assert after is not None
        return b, after

    def pair():
        turn[0] += turn[0] % 2
        for _ in range(4):
            i = turn[0] % 8
            turn[0] += 2
            if banks[i].free is not None and banks[i + 1].free is not None:
                break
        after = banks[i].free + banks[i + 1].free
        banks[i].free = banks[i + 1].free = None
        return (i, pairs[i // 2].ap), after

    def free_pair(p, marks):
        banks[p[0]].free = list(marks)
        banks[p[0] + 1].free = list(marks)

    X = sbuf("X", [128, KT, T2])
    HH = sbuf("HH", [128, KT, T2], f32r)
    HL = sbuf("HL", [128, KT, T2], f32r)
    CV = sbuf("CV", [128, NCOL])
    NCV = sbuf("NCV", [128, 8])
    KC = [sbuf("KC", [128, NCON[0]]), None, None]
    MOD = sbuf("MOD", [128, 48])
    SC = sbuf("SC", [128, 16])
    CA = sbuf("CA", [128, 8])
    TRIR = sbuf("TRIR", [128, 128], f32r)
    ONER = sbuf("ONER", [128, 128], f32r)
    RSTD = sbuf("RSTD", [128, T2])
    TMP = [sbuf(f"TMP{i}", [128, T2]) for i in range(3)]

    def col(name, i=0, p0=0, p1=128):
        return CV[p0:p1, COLS[name] + i:COLS[name] + i + 1]

    def con(name, p1=128):
        g, a, k = CON[name]
        return KC[g][0:p1, a:a + k]

    s_in = sem("s_in")
    se.dma_start(CV[:, :], cols).then_inc(s_in, 16)
    loaded = [(s_in, 48)]

    NR, NS = 4, 3
    RAWS = sbuf("RAWS", [128, NR * SLAB])
    RAW = [RAWS[:, SLAB * i:SLAB * i + SLAB] for i in range(NR)]
    WH = [sbuf(f"WH{i}", [128, SLAB], f32r) for i in range(NS)]
    WL = [sbuf(f"WL{i}", [128, SLAB], f32r) for i in range(NS)]
    s_raw = [sem(f"s_raw{i}") for i in range(NR)]
    order = []

    def whole(which, n):
        order.extend((which, i, SLAB, which != "ada") for i in range(n))

    later = [("ada", i, SLAB, False) for i in range(16, 48)]
    order.append(("ab", 0, 512, True))
    for i in range(28):
        order.append(("w_in", i, SLAB, True))
        later and order.append(later.pop(0))
    order += later
    whole("w_out", 8)
    for w in ("f0", "f1", "f2"):
        if w == "f2":
            order.append(("lora", 0, SLAB, True))
            order.append(("lora", 1, SLAB, True))
            for i in range(4):
                order.extend(("w_in2", t, SLAB, True) for t in (3 * i, 3 * i + 1, 3 * i + 2, 12 + i, 16 + i, 20 + i))
            order.append(("pause", 0, 0, False))
            whole("w_out2", 8)
        for j in range(FT):
            order.append((w + "g", j, SLAB, True))
            order.append((w + "u", j, SLAB, True))
        for m in range(8):
            for t in range(3):
                order.append((w + "d", 3 * m + t, SLAB if t < 2 else 768, True))
    raw_used = [[] for _ in range(NR)]
    split_used = [[] for _ in range(NS)]
    at = {"load": 0, "split": 0, "use": 0, "nsplit": 0}
    loads = {}
    splits = {}

    def load_next():
        i = at["load"]
        if i >= len(order) or raw_used[i % NR] is None:
            return
        which, j, n, _ = order[i]
        if which == "pause":
            return
        r = i % NR
        S.wait(raw_used[r])
        raw_used[r] = None
        se.dma_start(RAW[r][:, 0:n], slabs[which][j, :, 0:n]).then_inc(s_raw[r], 16)
        loads[i] = (s_raw[r], 16 * (i // NR + 1))
        at["load"] += 1

    def split_next():
        i = at["split"]
        if i >= len(order):
            return
        which, j, n, cut = order[i]
        r = i % NR
        at["split"] += 1
        if not cut:
            return
        s = at["nsplit"] % NS
        at["nsplit"] += 1
        used = split_used[s]
        assert used is not None
        split_used[s] = None
        hi = A.op(ae.activation, WH[s][:, 0:n], RAW[r][:, 0:n], ACT.Copy, after=[loads[i]] + used)
        lo = G.op(ge.tensor_tensor, WL[s][:, 0:n], RAW[r][:, 0:n], WH[s][:, 0:n].bitcast(f32), ALU.subtract,
                  after=[loads[i], hi] + used)
        splits[i] = (s, [hi, lo])
        raw_used[r] = [hi, lo]
        load_next()

    def slab(which, j):
        i = at["use"]
        assert order[i][:2] == (which, j), (order[i], which, j)
        at["use"] += 1
        while (at["split"] < min(i + 3, at["load"]) and at["nsplit"] - cut_before(i) < NS and
               split_used[at["nsplit"] % NS] is not None):
            split_next()
        return i

    def resume():
        i = at["load"]
        assert order[i][0] == "pause" and at["use"] == i
        del order[i]
        del cuts[i]
        marks = [(e.sem, e.n) for e in (V, A, G, T)]
        for r in range(NR):
            assert raw_used[r] is not None
            raw_used[r] = raw_used[r] + marks
        for _ in range(NR):
            load_next()

    cuts = [0]
    for o in order:
        cuts.append(cuts[-1] + o[3])

    def cut_before(i):
        return cuts[i]

    def run(*gens):
        live = list(gens)
        while live:
            for g in list(live):
                if next(g, run) is run:
                    live.remove(g)

    def gemm(*a, **k):
        g = gemm_steps(*a, **k)
        while True:
            try:
                next(g)
            except StopIteration as e:
                return e.value

    def gemm_steps(which, j, ps, after, xh, xl, nk, halves, xmarks, m=128, first=True, last=True, k0=0):
        i = slab(which, j)
        s, marks = splits[i]
        T.wait(list(after) + marks)
        for k in range(nk):
            if k:
                yield
            T.wait(xmarks[k0 + k] if xmarks else [])
            for w, x, e in ((WH[s], xh, 0), (WH[s], xl, 1), (WL[s], xh, 2)):
                for q, (o, a, b) in enumerate(halves):
                    stop = last and k == nk - 1 and e == 2
                    ins = te.matmul(ps[0:m, q, o:o + b - a] if len(halves) > 1 else ps[0:m, o:o + b - a],
                                    w[:, k * m:k * m + m], x[:, k0 + k, a:b],
                                    start=first and k == 0 and e == 0, stop=stop)
        ins.then_inc(T.sem, 1)
        T.n += 1
        done = (T.sem, T.n)
        split_used[s] = [done]
        return done

    def gemms(jobs, xh, xl, halves, xmarks, m=128):
        return together([gemm_steps(w, j, ps, after, xh, xl, KT, halves, xmarks, m=k or 128)
                         for w, j, ps, after, k in jobs])

    def together(gens):
        marks = [None] * len(gens)
        while None in marks:
            for i, g in enumerate(gens):
                if marks[i] is None:
                    try:
                        next(g)
                    except StopIteration as e:
                        marks[i] = e.value
        return marks

    H1 = [(0, NM, T2)]
    H2 = [(0, 0, 264), (0, 264, T2)]

    def two(ap):
        return ap.rearrange("p (a b) -> p a b", a=2)

    class Stats:

        def __init__(self, t0, free):
            self.t0, self.n, self.sq = t0, T2 - t0, {}
            self.used = [list(free) for _ in range(3)]

        def square(self, k, marks):
            self.sq[k] = A.op(ae.activation, TMP[k % 3][:, 0:self.n], X[:, k, self.t0:T2], ACT.Square,
                              after=marks + self.used[k % 3])

        def sum(self, k):
            if k == 0:
                if self.n == 528:
                    self.p, after = pair()
                    self.view = self.p[1]
                    self.outs = [(self.view[:, 0, :], 0, 264), (self.view[:, 1, :], 264, 528)]
                else:
                    self.p, after = bank()
                    self.view = self.p.ap[:, 0:self.n]
                    self.outs = [(self.view, 0, self.n)]
                T.wait(after)
            T.wait([self.sq[k]])
            for o, a, b in self.outs:
                ins = te.matmul(o, con("ones"), TMP[k % 3][:, a:b], start=(k == 0), stop=(k == KT - 1))
            ins.then_inc(T.sem, 1)
            T.n += 1
            self.used[k % 3] = [(T.sem, T.n)]

        def done(self, mark):
            if self.n == 528:
                free_pair(self.p, [mark])
            else:
                self.p.free = [mark]

    def log_and_exp():
        ae.preload_act_table_set("natural_log_exp_and_others")

    def rsqrt(dst, src, scale=1.0, bias=0.0, after=()):
        r1 = A.op(ae.activation, dst, src, ACT.Ln, bias=bias, scale=scale, after=after)
        return r1, A.op(ae.activation, dst, dst, ACT.Exp, scale=-0.5, after=[r1])

    def rstd(st, n, free):
        st.sum(KT - 1)
        rv = two(RSTD[:, 0:n]) if n == 528 else RSTD[:, 0:n]
        log_and_exp()
        r1, r2 = rsqrt(rv, st.view, 1.0 / D, EPSC[:, 0:1], [(T.sem, T.n), epc] + free)
        st.done(r1)
        return r2

    def rms(wcols, shift, t0, xmarks, free, dst=None, st=None, r2=None):
        n = T2 - t0
        x = X
        if st is None:
            st = Stats(t0, free)
            for k in range(KT):
                st.square(k, xmarks[k])
                if k:
                    st.sum(k - 1)
        if r2 is None:
            r2 = rstd(st, n, free)
        used = st.used
        if dst is not None:
            return [[V.op(ve.scalar_tensor_tensor, dst[:, k, t0:T2], x[:, k, t0:T2], wcols[:, k:k + 1], RSTD[:, 0:n],
                          ALU.mult, ALU.mult, after=[r2] + xmarks[k])] for k in range(KT)]
        his, res = [], []

        def low(k):
            if shift is None:
                lo = V.op(ve.tensor_tensor, HL[:, k, t0:T2], TMP[k % 3][:, 0:n], HH[:, k, t0:T2].bitcast(f32),
                          ALU.subtract, after=[his[k]])
            else:
                lo = V.op(ve.scalar_tensor_tensor, HL[:, k, t0:T2], TMP[k % 3][:, 0:n], shift[:, k:k + 1],
                          HH[:, k, t0:T2].bitcast(f32), ALU.add, ALU.subtract, after=[his[k]])
            used[k % 3] = [lo]
            res.append([his[k], lo])

        for k in range(KT):
            h = V.op(ve.scalar_tensor_tensor, TMP[k % 3][:, 0:n], x[:, k, t0:T2], wcols[:, k:k + 1], RSTD[:, 0:n],
                     ALU.mult, ALU.mult, after=[r2] + xmarks[k] + used[k % 3])
            if shift is None:
                his.append(A.op(ae.activation, HH[:, k, t0:T2], TMP[k % 3][:, 0:n], ACT.Copy, after=[h]))
            else:
                his.append(A.op(ae.activation, HH[:, k, t0:T2], TMP[k % 3][:, 0:n], ACT.Identity,
                                bias=shift[:, k:k + 1], after=[h]))
            if k:
                low(k - 1)
        low(KT - 1)
        return res

    def flat(marks):
        return [x for m in marks for x in m]

    def ffn(name, hm, t0, finish, s0):
        st = ExitStack()
        n = T2 - t0
        IH = sbuf("IH" + name, [128, FT, n], f32r, st)
        IL = sbuf("IL" + name, [128, FT, n], f32r, st)
        halves = H2 if t0 == 0 else H1
        im = []
        used = [[], [], []]
        ahead = []
        for w, j in (("g", 0), ("u", 0)):
            p, after = pair() if t0 == 0 else bank()
            ahead.append((p, p[1] if t0 == 0 else p.ap, (name + w, j), after))
        marks = gemms([(w[0], w[1], v, after, None) for p, v, w, after in ahead], HH, HL, halves, hm)
        ahead = [(p, v, d) for (p, v, w, after), d in zip(ahead, marks)]
        for j in range(FT):
            ps = []
            for w in "gu":
                if ahead:
                    ps.append(ahead.pop(0))
                    continue
                p, after = pair() if t0 == 0 else bank()
                v = p[1] if t0 == 0 else p.ap
                ps.append((p, v, gemm(name + w, j, v, after, HH, HL, KT, halves, hm)))
            (pg, g, dg), (pu, u, du) = ps
            b = j % 3
            tv = two(TMP[b][:, 0:n]) if t0 == 0 else TMP[b][:, 0:n]
            a = A.op(ae.activation, tv, g, ACT.Silu, after=[dg] + used[b])
            m = V.op(ve.tensor_tensor, tv, tv, u, ALU.mult, after=[a, du])
            if t0 == 0:
                free_pair(pg, [a])
                free_pair(pu, [m])
            else:
                pg.free, pu.free = [a], [m]
            hi = A.op(ae.activation, IH[:, j, :], TMP[b][:, 0:n], ACT.Copy, after=[m])
            lo = V.op(ve.tensor_tensor, IL[:, j, :], TMP[b][:, 0:n], IH[:, j, :].bitcast(f32), ALU.subtract,
                      after=[hi])
            used[b] = [lo]
            im.append([hi, lo])
        out_marks = []
        stats = Stats(s0, [im[-1][1]])
        hv = [(0, 0, n)] if t0 else H2
        for m in range(8):
            if t0 == 0:
                p, after = pair()
                ps = p[1]
            else:
                p, after = bank()
                ps = p.ap
            for t in range(3):
                nk = 8 if t < 2 else 6
                d = gemm(name + "d", 3 * m + t, ps, after, IH, IL, nk, hv, im if m == 0 else [],
                         first=(t == 0), last=(t == 2), k0=8 * t)
                after = []
            mk = finish(m, ps, d)
            if t0 == 0:
                free_pair(p, [mk])
            else:
                p.free = [mk]
            out_marks.append([mk])
            if m:
                stats.sum(m - 1)
            stats.square(m, [mk])
        st.close()
        return out_marks, d, stats

    se.dma_start(KC[0][:, :], consts[:, 0:NCON[0]]).then_inc(s_in, 16)
    se.dma_start(X[:, :, 0:NM], metaT.rearrange("(k p) t -> p k t", p=128)).then_inc(s_in, 16)
    s_x = sem("s_x")
    EPSC = sbuf("EPSC", [128, 1])
    acs = ExitStack()
    ACC = [sbuf(f"ACC{i}", [128, SLAB], st=acs) for i in range(2)]
    a0 = ExitStack()
    ADA = sbuf("ADA", [128, 16, SLAB], st=a0)
    s_ad = [sem(f"s_ad{i}") for i in range(4)]
    for i in range(4):
        se.dma_start(ADA[:, 4 * i:4 * i + 4, :], slabs["ada"][4 * i:4 * i + 4].rearrange("j p t -> p j t")).then_inc(
            s_ad[i], 16)
        if i == 1:
            se.dma_start(X[:, :, NM:T2], xT.rearrange("(k p) t -> p k t", p=128)).then_inc(s_x, 16)
    for _ in range(NR):
        load_next()

    ca = A.op(ae.activation, CA[:, :], CV[:, COLS["c"]:COLS["c"] + 8], ACT.Silu, after=loaded)
    
    epc = G.op(ge.memset, EPSC[:, :], EPS)
    c2 = A.op(ae.activation, ONER[:, :], con("ones"), ACT.Copy)
    T.wait(loaded + [c2])
    V.wait(loaded)
    G.wait(loaded)
    A.wait(loaded)

    acc_used = [[], []]
    ada_acc = {}

    def weigh(j, w, marks):
        v, k = divmod(j, 8)
        a = ACC[v % 2]
        if k == 0:
            ada_acc[v] = V.op(ve.tensor_scalar, a[:, :], w, CA[:, 0:1], None, ALU.mult, after=marks + acc_used[v % 2])
        else:
            ada_acc[v] = V.op(ve.scalar_tensor_tensor, a[:, :], w, CA[:, k:k + 1], a[:, :], ALU.mult, ALU.add,
                              after=marks + [ada_acc[v]])
        return ada_acc[v]

    def column(v):
        p, after = bank()
        T.wait(after + [ada_acc[v]])
        for m in range(8):
            ins = te.matmul(p.ap[:, m:m + 1], ACC[v % 2][:, 128 * m:128 * m + 128], con("ones")[:, 0:1], start=True,
                            stop=True)
        ins.then_inc(T.sem, 1)
        T.n += 1
        acc_used[v % 2] = [(T.sem, T.n)]
        a = COLS["b_ada"] + 8 * v
        mod = V.op(ve.tensor_tensor, MOD[:, 8 * v:8 * v + 8], p.ap[:, 0:8], CV[:, a:a + 8], ALU.add,
                   after=[(T.sem, T.n)])
        p.free = [mod]
        return mod

    def ada(j):
        i = slab("ada", j)
        r = i % NR
        raw_used[r] = [weigh(j, RAW[r][:, :], [loads[i], ca])]
        load_next()
        if j % 8 == 7:
            return column(j // 8)

    st = Stats(NM, [])
    for j in range(16):
        weigh(j, ADA[:, j, :], [(s_ad[j // 4], 16), ca])
        if j == 7:
            mod1 = column(0)
            for k in range(KT):
                st.square(k, [(s_x, 16)])
                if k:
                    st.sum(k - 1)
    r2 = rstd(st, T1, [])
    mod1 = column(1)
    sc1 = V.op(ve.scalar_tensor_tensor, SC[:, 0:8], MOD[:, 8:16], 1.0, CV[:, COLS["norm1"]:COLS["norm1"] + 8],
               ALU.add, ALU.mult, after=[mod1])
    A.wait([sc1])
    V.wait([sc1])
    a0.close()
    hm = rms(SC[:, 0:8], MOD[:, 0:8], NM, [[(s_x, 16)]] * KT, [sc1], st=st, r2=r2)

    mx = ExitStack()
    KC[1] = sbuf("KC1", [128, NCON[1]], st=mx)
    s_k1 = sem("s_k1")
    S.wait([(V.sem, V.n)])
    se.dma_start(KC[1][:, :], consts[:, NCON[0]:NCON[0] + NCON[1]]).then_inc(s_k1, 16)
    k1 = [(s_k1, 32)]
    a1 = NCON[0] + NCON[1] + CON["reset1"][1]
    QKV = sbuf("QKV", [128, 12, 512], st=mx)
    Z = sbuf("Z", [128, 4, 512], st=mx)
    YS = sbuf("YS", [128, 4, 512], st=mx)
    se.dma_start(YS[:, 0, :], consts[:, a1:a1 + 512]).then_inc(s_k1, 16)
    ROW = sbuf("ROW", [64, 512], st=mx)
    NEA = sbuf("NEA", [4, 1], st=mx)
    STG = [sbuf(f"STG{i}", [128, 3 + 512], st=mx) for i in range(2)]
    RT = [TMP[i][0:64, 0:512] for i in range(2)]
    free_x = [(V.sem, V.n)]
    A.wait(free_x)
    G.wait(free_x)
    z0 = G.op(ge.memset, STG[0][:, 0:3], 0.0)
    z1 = G.op(ge.memset, STG[1][:, 0:3], 0.0)
    z2 = G.op(ge.memset, ROW[:, :], 0.0)
    hall = flat(hm)

    ada_next = [16]
    mod2_last = [None]

    def more_ada():
        if ada_next[0] < 48:
            mod2_last[0] = ada(ada_next[0]) or mod2_last[0]
            ada_next[0] += 1

    p, after = bank()
    p1, after1 = bank()
    d, d1 = gemms([("ab", 0, p.ap, after, 64), ("w_in", 0, p1.ap, after1, None)], HH, HL, H1, hm)
    pab, dab = p, d
    used = [[z0], [z1]]
    qkv = []

    def convolve(j, p, d):
        s = STG[j % 2]
        ev = A.op(ae.activation, s[:, 3:515], p.ap, ACT.Copy, after=[d] + used[j % 2])
        p.free = [ev]
        a = TMP[j % 3][:, 0:512]
        m = V.op(ve.tensor_scalar, a, s[:, 0:512], col("convq", j), None, ALU.mult,
                 after=[ev] + tused[j % 3] + used[j % 2])
        for t in range(1, 4):
            m = V.op(ve.scalar_tensor_tensor, a, s[:, t:t + 512], col("convq", 12 * t + j), a, ALU.mult, ALU.add,
                     after=[m])
        si = A.op(ae.activation, QKV[:, j, :], a, ACT.Silu, after=[m])
        used[j % 2] = [m]
        tused[j % 3] = [si]
        qkv.append(si)

    done = [(0, p1, d1)]
    for j in range(1, 12):
        more_ada()
        p, after = bank()
        d = gemm("w_in", j, p.ap, after, HH, HL, KT, H1, hm)
        if j == 1:
            tx = V.op(ve.tensor_scalar, RT[0][0:4, :], pab.ap[0:4, :], col("dtb", 0, 0, 4), None, ALU.add, after=[dab])
            rb = A.op(ae.activation, ROW[32:36, :], pab.ap[32:36, :], ACT.Sigmoid, after=[dab, z2])
            pab.free = [tx, rb]
            log_and_exp()
            ab = A.op(ae.activation, RT[1][0:4, :], RT[0][0:4, :], ACT.Abs, after=[tx])
            ex = A.op(ae.activation, RT[1][0:4, :], RT[1][0:4, :], ACT.Exp, scale=-1.0, after=[ab])
            ln = A.op(ae.activation, RT[1][0:4, :], RT[1][0:4, :], ACT.Ln, bias=1.0, after=[ex])
            nea = A.op(ae.activation, NEA[:, :], col("alog", 0, 0, 4), ACT.Exp)
            sp = V.op(ve.scalar_tensor_tensor, RT[0][0:4, :], RT[0][0:4, :], 0.0, RT[1][0:4, :], ALU.max, ALU.add,
                      after=[ln])
            gg = V.op(ve.tensor_scalar, RT[0][0:4, :], RT[0][0:4, :], NEA[:, 0:1], -1.0, ALU.mult, ALU.mult,
                      after=[sp, nea])
            rg = V.op(ve.tensor_tensor_scan, ROW[0:4, :], YS[0:4, 0, :], RT[0][0:4, :], 0.0, ALU.mult, ALU.add,
                      after=[gg, z2] + k1)
            rows = [rb, rg]
            tused = [[rg], [sp], []]
        convolve(*done.pop())
        done.append((j, p, d))
    more_ada()
    convolve(*done.pop())
    zm, cat = [None] * 4, [None] * 8
    rest = {}

    def project_rest():
        for j in range(4):
            p, after = bank()
            d = yield from gemm_steps("w_in", 12 + j, p.ap, after, HH, HL, KT, H1, hm)
            more_ada()
            yield
            zm[j] = A.op(ae.activation, Z[:, j, :], p.ap, ACT.Copy, after=[d])
            p.free = [zm[j]]
        ys = []
        for j in range(4):
            s = STG[j % 2]
            p, after = bank()
            d = yield from gemm_steps("w_in", 16 + 3 * j, p.ap, after, HH, HL, KT, H1, hm)
            more_ada()
            yield
            y = YS[:, j, :]
            ev = A.op(ae.activation, y, p.ap, ACT.Copy, after=[d, rg])
            p.free = [ev]
            p, after = bank()
            d = yield from gemm_steps("w_in", 17 + 3 * j, p.ap, after, HH, HL, KT, H1, hm)
            more_ada()
            yield
            m = V.op(ve.tensor_tensor, s[:, 3:515], y, p.ap, ALU.mult, after=[d, ev] + used[j % 2])
            p.free = [m]
            m = V.op(ve.tensor_scalar, y, s[:, 1:513], col("convs", j), None, ALU.mult, after=[m])
            for t in (1, 2):
                m = V.op(ve.scalar_tensor_tensor, y, s[:, 1 + t:513 + t], col("convs", 4 * t + j), y, ALU.mult,
                         ALU.add, after=[m])
            used[j % 2] = [m]
            p, after = bank()
            d = yield from gemm_steps("w_in", 18 + 3 * j, p.ap, after, HH, HL, KT, H1, hm)
            more_ada()
            yield
            m = V.op(ve.tensor_tensor, y, y, p.ap, ALU.mult, after=[d, m])
            p.free = [m]
            ys.append(m)
        rest["done"] = d
        while ada_next[0] < 48:
            more_ada()
            yield
        mod2 = mod2_last[0]
        rest["mod2"] = mod2
        rest["sc2"] = V.op(ve.scalar_tensor_tensor, SC[:, 8:16], MOD[:, 32:40], 1.0,
                           CV[:, COLS["norm2"]:COLS["norm2"] + 8], ALU.add, ALU.mult, after=[mod2])
        for j in range(4):
            yield
            hi = A.op(ae.activation, HH[:, 4 + j, NM:T2], YS[:, j, :], ACT.Copy, after=[ys[j], rest["done"]])
            lo = V.op(ve.tensor_tensor, HL[:, 4 + j, NM:T2], YS[:, j, :], HH[:, 4 + j, NM:T2].bitcast(f32),
                      ALU.subtract, after=[hi, rest["done"]])
            cat[4 + j] = [hi, lo]

    def bc(ap, n):
        return ap.unsqueeze(1).broadcast_to([ap.shape[0], n, ap.shape[1]])

    HALF = (slice(0, 64), slice(64, 128))

    class Inverse:
        def __init__(self, st, name):
            t = {x: sbuf(f"{name}{x}", [128, 4, 64], st=st)[:, :, :] for x in ("L", "UD", "LD", "L2", "XB", "C1", "C2")}
            self.XU = sbuf(f"{name}XU", [128, 4, 128], st=st)
            t["XA"], t["U2"] = self.XU[:, :, 0:64], self.XU[:, :, 64:128]
            self.t = [t[x] for x in ("L", "UD", "LD", "U2", "L2", "XA", "XB", "C1", "C2")]
            self.done = []

    def products(lhs, rhs, marks):
        p, after = bank()
        T.wait(after + marks)
        o = p.ap[:, 0:256].rearrange("p (u t) -> p u t", u=4)
        for u in range(4):
            for q in HALF:
                ins = te.matmul(o[q, u, :], lhs[q, u, :], con("ident")[q, q] if rhs is None else rhs[q, u, :],
                                start=True, stop=True)
        ins.then_inc(T.sem, 1)
        T.n += 1
        return p, o, (T.sem, T.n)

    def copied(dst, lhs, rhs, marks, e):
        p, o, d = products(lhs, rhs, marks)
        if e is A:
            m = A.op(ae.activation, dst, o, ACT.Copy, after=[d])
        else:
            m = V.op(ve.tensor_copy, dst, o, after=[d])
        p.free = [m]
        return m

    def added(dst, base, lhs, rhs, marks):
        p, o, d = products(lhs, rhs, marks)
        m = V.op(ve.tensor_tensor, dst, o, base, ALU.add, after=[d])
        p.free = [m]
        return m

    def invert(w, U, um, X, free):
        L, UD, LD, U2, L2, XA, XB, C1, C2 = w.t
        U4, L4 = UD, LD
        ud = V.op(ve.tensor_tensor, UD, U, bc(con("b16"), 4), ALU.mult, after=um + w.done)
        p, o, d = products(U, None, um + w.done)
        yield
        ld = V.op(ve.tensor_tensor, LD, o, bc(con("b16"), 4), ALU.mult, after=[d])
        lp = V.op(ve.tensor_copy, L, o, after=[d])
        p.free = [lp]
        xa = V.op(ve.tensor_tensor, XA, UD, bc(con("i2"), 4), ALU.add, after=[ud])
        c1 = G.op(ge.tensor_tensor, C1, L, bc(con("c32"), 4), ALU.mult, after=[lp] + w.done)
        c2 = G.op(ge.tensor_tensor, C2, L, bc(con("c64"), 4), ALU.mult, after=[lp] + w.done)
        l2 = copied(L2, UD, LD, [ud, ld], A)
        yield
        u2 = copied(U2, LD, UD, [], A)
        yield
        p, after = bank()
        T.wait(after + [l2, xa, u2])
        o = p.ap.rearrange("p (u t) -> p u t", u=4)
        for u in range(4):
            for q in HALF:
                ins = te.matmul(o[q, u, :], L2[q, u, :], w.XU[q, u, :], start=True, stop=True)
        ins.then_inc(T.sem, 1)
        T.n += 1
        xb = V.op(ve.tensor_tensor, XB, o[:, :, 0:64], XA, ALU.add, after=[(T.sem, T.n)])
        u4 = V.op(ve.tensor_copy, U4, o[:, :, 64:128], after=[(T.sem, T.n)])
        p.free = [u4]
        yield
        l4 = copied(L4, U2, L2, [u2, l2], A)
        yield
        xa = added(XA, XB, L4, XB, [l4, xb])
        yield
        l8 = copied(L2, U4, L4, [u4, l4], A)
        yield
        xb = added(XB, XA, L2, XA, [l8, xa])
        yield
        y = copied(U2, XB, None, [xb, l4], A)
        z = copied(U4, C1, XB, [c1], V)
        yield
        xa = added(XA, XB, U2, U4, [y, z])
        yield
        yy = added(L4, U2, U4, U2, [])
        z = copied(L2, C2, XA, [c2, xa], A)
        yield
        p, o, d = products(L4, L2, [z, yy])
        m = V.op(ve.tensor_tensor, X, o, XA, ALU.add, after=[d] + free)
        p.free = [m]
        w.done = [m]
        return m

    def pipeline(n, prepare, scan):
        ready, scanned = set(), set()

        def preparer(i0):
            for i in range(i0, n, 2):
                while i >= 2 and i - 2 not in scanned:
                    yield
                yield from prepare(i)
                ready.add(i)

        def scanner():
            for i in range(n):
                while i not in ready:
                    yield
                yield from scan(i)
                scanned.add(i)

        live = [scanner(), preparer(0), preparer(1)]
        while live:
            for g in list(live):
                if next(g, run) is run:
                    live.remove(g)
                yield

    COLT = sbuf("COLT", [128, 4, 64], st=mx)
    EGC = sbuf("EGC", [128, 4, 4], st=mx)
    BEG = sbuf("BEG", [128, 4, 4], st=mx)
    inv = [Inverse(mx, f"iv{i}") for i in range(2)]
    UU2 = [sbuf(f"UU{i}", [128, 4, 64], st=mx) for i in range(2)]
    VN = sbuf("VN", [128, 4, 128], st=mx)
    ST = sbuf("ST", [128, 4, 128], st=mx)
    XF = X[:, :, :].rearrange("p k t -> p (k t)")
    EG2, KB2 = ([XF[:, o + 512 * i:o + 512 * i + 512].rearrange("p (h t) -> p h t", h=4) for i in range(2)]
                for o in (2048, 3072))
    BUF = []
    for i in range(2):
        b = {"AT": sbuf(f"AT{i}", [128, 4, 64], st=mx), "XX": sbuf(f"XX{i}", [128, 4, 64], st=mx),
             "VBT": sbuf(f"VBT{i}", [128, 4, 128], st=mx), "WT": sbuf(f"WT{i}", [128, 8, 64], st=mx),
             "QD": sbuf(f"QD{i}", [128, 4, 128], st=mx),
             "GL": sbuf(f"GL{i}", [128, 2, 4], st=mx), "EGL": sbuf(f"EGL{i}", [128, 2, 4], st=mx),
             "KDC": sbuf(f"KDC{i}", [128, 4], st=mx),
             "DC": sbuf(f"DC{i}", [128, 4, 64], st=mx),
             "KBT": XF[:, 1024 * i:1024 * i + 512].rearrange("p (u t) -> p u t", u=4),
             "KDT": XF[:, 1024 * i + 512:1024 * i + 1024].rearrange("p (u t) -> p u t", u=4),
             "done": []}
        BUF.append(b)
    OG = QKV
    p, after = bank()
    T.wait(after + rows)
    o = p.ap[:, 0:256].rearrange("p (u t) -> p u t", u=4)
    for n in range(4):
        ins = te.transpose(o[:, n, :], ROW[:, 128 * n:128 * n + 128], con("ident")[0:64, 0:64])
    ins.then_inc(T.sem, 1)
    T.n += 1
    ct = V.op(ve.tensor_copy, COLT[:, :, :], o, after=[(T.sem, T.n)])
    p.free = [ct]
    eg = A.op(ae.activation, EGC[:, :, :], COLT[:, :, 0:4], ACT.Exp, after=[ct])
    bg = V.op(ve.tensor_tensor, BEG[:, :, :], EGC[:, :, :], COLT[:, :, 32:36], ALU.mult, after=[eg])

    def l2_norm():
        for j in (4, 0, 5, 1, 6, 2, 7, 3):
            t = TMP[j % 3][:, 0:512]
            sq = A.op(ae.activation, t, QKV[:, j, :], ACT.Square, after=[qkv[j]] + tused[j % 3])
            p, after = bank()
            mm = T.op(te.matmul, p.ap, con("ones"), t, start=True, stop=True, after=after + [sq])
            yield
            r = A.op(ae.activation, t, p.ap, ACT.Sqrt, bias=EPSC[:, 0:1], after=[mm])
            p.free = [r]
            r = V.op(ve.reciprocal, t, t, after=[r])
            qkv[j] = V.op(ve.scalar_tensor_tensor, QKV[:, j, :], QKV[:, j, :], 128.0 ** -0.5 if j < 4 else 1.0, t,
                          ALU.mult, ALU.mult, after=[r])
            tused[j % 3] = [qkv[j]]
            yield

    sm = [G.op(ge.memset, ST[:, :, :], 0.0)]
    cb = lambda ap: ap.unsqueeze(2).broadcast_to([128, 4, 128])
    h4 = lambda ap: ap.rearrange("p (h t) -> p h t", h=4)
    shared = [{"kb": [], "eg": free_x, "uu": []} for _ in range(2)]

    def prepare(b):
        B = BUF[b % 2]
        EG, KB, UU = EG2[b % 2], KB2[b % 2], UU2[b % 2]
        old = B["done"]
        ts = slice(128 * b, 128 * b + 128)
        p, after = bank()
        T.wait(after + rows + k1)
        for h in range(4):
            ins = te.matmul(p.ap[:, 128 * h:128 * h + 128], con("sel", 64)[:, 128 * h:128 * h + 128], ROW[:, ts],
                            start=True, stop=True)
        ins.then_inc(T.sem, 1)
        T.n += 1
        d = (T.sem, T.n)
        p2, after = bank()
        T.wait(after)
        for h in range(4):
            ins = te.matmul(p2.ap[:, 128 * h:128 * h + 128], con("sel", 64)[:, 128 * (4 + h):128 * (4 + h) + 128],
                            ROW[:, ts], start=True, stop=True)
        ins.then_inc(T.sem, 1)
        T.n += 1
        d2 = (T.sem, T.n)
        yield
        g4 = p.ap.rearrange("p (h c t) -> p h c t", h=4, c=2)
        m1 = [V.op(ve.tensor_tensor, B["DC"][q, :, :], g4[q, :, c, :],
                   COLT[q, b, 0:4].unsqueeze(2).broadcast_to([64, 4, 64]), ALU.subtract, after=[d, ct] + old)
              for c, q in enumerate(HALF)]
        gl = V.op(ve.tensor_copy, B["GL"][:, :, :].rearrange("p c h -> p h c"), g4[:, :, :, 63], after=[d] + old)
        e = A.op(ae.activation, EG[:, :, :], h4(p.ap), ACT.Exp, after=[m1[-1], gl] + shared[b % 2]["eg"])
        p.free = [e]
        yield
        dv = B["DC"][:, :, :]
        m2 = V.op(ve.tensor_tensor, dv, dv, bc(con("madd"), 4), ALU.add, after=m1)
        dm = A.op(ae.activation, dv, dv, ACT.Exp, after=[m2])
        kb = V.op(ve.tensor_tensor, KB[:, :, :], QKV[:, 4:8, ts], h4(p2.ap), ALU.mult,
                  after=[d2] + qkv[4:8] + shared[b % 2]["kb"])
        p2.free = [kb]
        qd = V.op(ve.tensor_tensor, B["QD"][:, :, :], QKV[:, 0:4, ts], EG[:, :, :], ALU.mult,
                  after=[e] + qkv[0:4] + old)
        shared[b % 2]["eg"] = [qd]
        B["egl"] = A.op(ae.activation, B["EGL"][:, :, :], B["GL"][:, :, :], ACT.Exp, after=[gl])
        for c, q in enumerate(HALF):
            kd0 = V.op(ve.tensor_tensor, B["KDC"][q, :], B["GL"][q, c, :], COLT[q, b, 0:4], ALU.subtract, after=[gl])
        kdc = A.op(ae.activation, B["KDC"][:, :], B["KDC"][:, :], ACT.Exp, after=[kd0])
        yield
        pk, after1 = bank()
        pq, after2 = bank()
        T.wait(after1 + after2 + qkv[0:8] + [kb])
        for c, q in enumerate(HALF):
            for h in range(4):
                t0 = 64 * (2 * b + c)
                te.matmul(pk.ap[q, 64 * h:64 * h + 64], QKV[:, 4 + h, t0:t0 + 64], KB[:, h, 64 * c:64 * c + 64],
                          start=True, stop=True)
                ins = te.matmul(pq.ap[q, 64 * h:64 * h + 64], QKV[:, 4 + h, t0:t0 + 64], QKV[:, h, t0:t0 + 64],
                                start=True, stop=True)
        ins.then_inc(T.sem, 1)
        T.n += 1
        d = (T.sem, T.n)
        shared[b % 2]["kb"] = [d]
        u1 = V.op(ve.tensor_tensor, UU[:, :, :], h4(pk.ap[:, 0:256]), dv, ALU.mult, after=[d, dm] + shared[b % 2]["uu"])
        um = V.op(ve.tensor_tensor, UU[:, :, :], UU[:, :, :], bc(con("nstrict"), 4), ALU.mult, after=[u1])
        B["at"] = V.op(ve.tensor_tensor, B["AT"][:, :, :], h4(pq.ap[:, 0:256]), dv, ALU.mult, after=[d])
        pk.free, pq.free = [u1], [B["at"]]
        yield
        pk, after1 = bank()
        pv, after2 = bank()
        T.wait(after1 + after2 + qkv[8:12])
        for h in range(4):
            te.transpose(pk.ap[:, 128 * h:128 * h + 128], QKV[:, 4 + h, ts], con("ident"))
            ins = te.transpose(pv.ap[:, 128 * h:128 * h + 128], QKV[:, 8 + h, ts], con("ident"))
        ins.then_inc(T.sem, 1)
        T.n += 1
        d = (T.sem, T.n)
        k4, v4 = h4(pk.ap), h4(pv.ap)
        m1 = V.op(ve.tensor_tensor, B["KBT"], k4, cb(BEG[:, b, :]), ALU.mult, after=[d, bg] + old + free_x)
        m2 = V.op(ve.tensor_tensor, B["KDT"], k4, cb(B["KDC"][:, :]), ALU.mult, after=[d, kdc] + old)
        m3 = V.op(ve.tensor_tensor, B["VBT"][:, :, :], v4, cb(COLT[:, b, 32:36]), ALU.mult, after=[d] + old)
        pk.free, pv.free = [m2], [m3]
        tk = [m1, m2, m3]
        yield
        xm = yield from invert(inv[b % 2], UU[:, :, :], [um], B["XX"][:, :, :], old)
        shared[b % 2]["uu"] = [xm]
        p, after = bank()
        T.wait(after + tk + [xm])
        for q in HALF:
            for h in range(4):
                ins = te.matmul(p.ap[q, 128 * h:128 * h + 128], B["XX"][q, h, :], B["VBT"][q, h, :], start=True,
                                stop=True)
        ins.then_inc(T.sem, 1)
        T.n += 1
        B["u"] = A.op(ae.activation, B["VBT"][:, :, :], h4(p.ap), ACT.Copy, after=[(T.sem, T.n)])
        p.free = [B["u"]]
        yield
        p, after = bank()
        p2, after2 = bank()
        T.wait(after + after2)
        for h in range(4):
            for q, o in zip(HALF, (p, p2)):
                ins = te.matmul(o.ap[:, 64 * h:64 * h + 64], B["KBT"][q, h, :], B["XX"][q, h, :], start=True, stop=True)
        ins.then_inc(T.sem, 1)
        T.n += 1
        w1 = A.op(ae.activation, B["WT"][:, 0:4, :], h4(p.ap[:, 0:256]), ACT.Copy, after=[(T.sem, T.n)] + old)
        w2 = V.op(ve.tensor_copy, B["WT"][:, 4:8, :], h4(p2.ap[:, 0:256]), after=[(T.sem, T.n)] + old)
        p.free, p2.free = [w1], [w2]
        B["wt"] = [w1, w2]
        B["ready"] = tk + [qd]

    og = []
    last = {"sd": [], "sm": sm}

    def scan1(b):
        B = BUF[b % 2]
        for c, q in enumerate(HALF):
            n = 2 * b + c
            p, after = bank()
            T.wait(after + B["wt"] + last["sm"])
            for h in range(4):
                ins = te.matmul(p.ap[q, 128 * h:128 * h + 128], B["WT"][:, 4 * c + h, :], ST[:, h, :], start=True,
                                stop=True)
            ins.then_inc(T.sem, 1)
            T.n += 1
            vn = V.op(ve.tensor_tensor, VN[q, :, :], B["VBT"][q, :, :], h4(p.ap[q, :]), ALU.subtract,
                      after=[(T.sem, T.n), B["u"]] + last["sd"])
            p.free = [vn]
            yield
            p, after = bank()
            p2, after2 = bank()
            T.wait(after + after2 + [B["at"], vn] + B["ready"])
            for h in range(4):
                ins = te.matmul(p2.ap[:, 128 * h:128 * h + 128], B["KDT"][q, h, :], VN[q, h, :], start=True,
                                stop=True)
            ins.then_inc(T.sem, 1)
            T.n += 1
            sd = (T.sem, T.n)
            for h in range(4):
                te.matmul(p.ap[:, 64 * h:64 * h + 64], ST[:, h, :], B["QD"][:, h, 64 * c:64 * c + 64], start=True,
                          stop=False)
                ins = te.matmul(p.ap[:, 64 * h:64 * h + 64], VN[q, h, :], B["AT"][q, h, :], start=False,
                                stop=True)
            ins.then_inc(T.sem, 1)
            T.n += 1
            od = (T.sem, T.n)
            om = A.op(ae.activation, OG[:, 0:4, 64 * n:64 * n + 64], h4(p.ap[:, 0:256]), ACT.Copy, after=[od])
            p.free = [om]
            og.append(om)
            last["sm"] = [V.op(ve.scalar_tensor_tensor, ST[:, h, :], ST[:, h, :], B["EGL"][:, c, h:h + 1],
                               p2.ap[:, 128 * h:128 * h + 128], ALU.mult, ALU.add, after=[sd, od, B["egl"]])
                          for h in range(4)]
            p2.free = [last["sm"][-1]]
            last["sd"] = [od]
            yield
        B["done"] = [od, last["sm"][-1]]

    def delta_rule():
        yield from l2_norm()
        yield from pipeline(4, prepare, scan1)

    pr, dr = project_rest(), delta_rule()
    run(*[pr, dr] * 4, dr)
    proj_done, mod2, sc2 = rest["done"], rest["mod2"], rest["sc2"]
    S.wait([(T.sem, T.n), (V.sem, V.n)])
    se.dma_start(X[:, :, NM:T2], xT.rearrange("(k p) t -> p k t", p=128)).then_inc(s_x, 16)
    se.dma_start(X[:, :, 0:NM], metaT.rearrange("(k p) t -> p k t", p=128)).then_inc(s_x, 16)
    xback = [(s_x, 48)]
    zs = [A.op(ae.activation, Z[:, h, :], Z[:, h, :], ACT.Silu, after=[zm[h]]) for h in range(4)]
    log_and_exp()
    buf = TMP + [RSTD]
    before = flat(tused) + [(V.sem, V.n)]

    def gate(h):
        t = buf[h][:, 0:512]
        sq = A.op(ae.activation, t, OG[:, h, :], ACT.Square, after=[og[-1]] + before)
        p, after = bank()
        mm = T.op(te.matmul, p.ap, con("ones"), t, start=True, stop=True, after=after + [sq])
        yield
        r1, r = rsqrt(t, p.ap, 1.0 / 128, EPSC[:, 0:1], [mm])
        p.free = [r1]
        yield
        y = V.op(ve.scalar_tensor_tensor, t, OG[:, h, :], col("gdn"), t, ALU.mult, ALU.mult, after=[r])
        y = V.op(ve.tensor_tensor, t, t, Z[:, h, :], ALU.mult, after=[y, zs[h]])
        yield
        hi = A.op(ae.activation, HH[:, h, NM:T2], t, ACT.Copy, after=[y, proj_done])
        yield
        lo = V.op(ve.tensor_tensor, HL[:, h, NM:T2], t, HH[:, h, NM:T2].bitcast(f32), ALU.subtract, after=[hi])
        tused[h % 3] = [lo]
        cat[h] = [hi, lo]

    run(*(gate(h) for h in range(4)))
    xm = []
    for m in range(8):
        if m == 0:
            ps = [bank() for _ in range(2)]
            ds = gemms([("w_out", i, p.ap, after, None) for i, (p, after) in enumerate(ps)], HH, HL, H1, cat)
        if m < 2:
            p, d = ps[m][0], ds[m]
        else:
            p, after = bank()
            d = gemm("w_out", m, p.ap, after, HH, HL, KT, H1, cat)
        xm.append([V.op(ve.scalar_tensor_tensor, X[:, m, NM:T2], p.ap, MOD[:, 16 + m:17 + m], X[:, m, NM:T2], ALU.mult,
                        ALU.add, after=[d, mod2] + xback)])
        p.free = [xm[-1][0]]
        if m == 0:
            stats = Stats(NM, flat(tused))
        else:
            stats.sum(m - 1)
        stats.square(m, xm[-1])
    mx.close()
    acs.close()

    hm = rms(SC[:, 8:16], MOD[:, 24:32], NM, xm, [sc2, d] + flat(cat), st=stats)

    def fin1(m, ps, d):
        return V.op(ve.scalar_tensor_tensor, X[:, m, NM:T2], ps, MOD[:, 40 + m:41 + m], X[:, m, NM:T2],
                    ALU.mult, ALU.add, after=[d])

    xm, d, stats = ffn("f0", hm, NM, fin1, NM)
    xm = rms(CV[:, COLS["normf"]:COLS["normf"] + 8], None, NM, xm, [d], dst=X, st=stats)

    xm = [m + loaded for m in xm]

    def fin2(t0):
        def f(m, ps, d):
            n = T2 - t0
            xv = two(X[:, m, 0:n]) if t0 == 0 else X[:, m, t0:T2]
            return V.op(ve.scalar_tensor_tensor, xv, ps, 0.5, xv, ALU.mult, ALU.add, after=[d])
        return f

    hm = rms(CV[:, COLS["ffn1"]:COLS["ffn1"] + 8], None, 0, xm, [d])
    xm, d, stats = ffn("f1", hm, 0, fin2(0), 0)
    hm = rms(CV[:, COLS["mix"]:COLS["mix"] + 8], None, 0, xm, [d], st=stats)
    hall = flat(hm)

    rw = ExitStack()
    XSAVE = nc.dram_tensor("xsave", (128, KT * T1), f32, kind="Internal").ap()
    BSAVE = nc.dram_tensor("bsave", (128, 4 * T1), f32, kind="Internal").ap()
    s_xs = sem("s_xs")
    s_bs = sem("s_bs")
    S.wait([hm[-1][1]])
    se.dma_start(XSAVE.rearrange("p (k t) -> p k t", k=KT), X[:, :, NM:T2]).then_inc(s_xs, 16)
    xsaved = [(s_xs, 16)]
    KC[2] = sbuf("KC2", [128, 256], st=rw)
    QA = sbuf("QA", [128, 4, 512], st=rw)
    KA = sbuf("KA", [128, 4, 640], st=rw)
    VT = sbuf("VT", [128, 5, 512], st=rw)
    PM = sbuf("PM", [128, 1], st=rw)
    GUP = sbuf("GUP", [96, 512], st=rw)
    XG = sbuf("XG", [96, T2], st=rw)
    VB = sbuf("VB", [128, 4, 64 + TP], st=rw)
    AR = sbuf("AR", [128, 4, NCH, 2, 64], st=rw)
    BK = sbuf("BK", [128, 4, NCH, 2, 64], st=rw)
    WCC = sbuf("WCC", [128, 4, NCH], st=rw)
    KAM = sbuf("KAM", [128, 4], st=rw)
    el = ExitStack()
    LUP = sbuf("LUP", [64, 512], st=el)
    RES = sbuf("RES", [128, TP], st=el)
    LX = sbuf("LX", [64, T2], st=el)
    SG = [sbuf(f"SG{i}", [128, 1 + TP], st=el) for i in range(2)]
    VS = sbuf("VS", [128, 640], st=el)
    R1, K1, SW, SA, CS, KK, EX = (XF[:, TP * i:TP * i + TP] for i in range(7))
    s_k2 = sem("s_k2")
    S.wait(flat(hm))
    a2 = NCON[0] + NCON[1]
    se.dma_start(KC[2][:, :], consts[:, a2 + CON["tri"][1]:a2 + CON["tri"][1] + 256]).then_inc(s_k2, 16)
    CON["tri"], CON["m4"] = (2, 0, 128), (2, 128, 128)
    a2 += CON["reset2"][1]
    se.dma_start(RES[:, :], consts[:, a2:a2 + TP]).then_inc(s_k2, 16)
    se.dma_start(LUP[:, :], lup).then_inc(s_k2, 16)
    se.dma_start(GUP[:, :], gup).then_inc(s_k2, 16)
    k2 = [(s_k2, 64)]
    zr = [G.op(ge.memset, t[:, 0:PAD + 1], 0.0, after=hm[-1]) for t in SG]
    zr.append(G.op(ge.memset, VB[:, :, 0:64], 0.0))
    zr.append(G.op(ge.memset, KA[:, :, 0:112], 0.0))
    zr.append(G.op(ge.memset, VS[:, 0:112], 0.0))
    zr += [G.op(ge.memset, t[:, 0:PAD], 0.0, after=xsaved) for t in (SW, SA)]
    pm0 = G.op(ge.memset, PM[:, :], 1.0)
    pmk = G.op(ge.affine_select, out=PM[:, :], in_=PM[:, :], pattern=[[0, 1]], compare_op=ALU.is_ge, fill=0.0,
               base=-112, channel_multiplier=1, after=[pm0])
    V.wait(zr)
    A.wait(zr)
    c1 = A.op(ae.activation, TRIR[:, :], con("tri"), ACT.Copy, after=k2)
    kam = V.op(ve.tensor_scalar, KAM[:, :], CV[:, COLS["ka"]:COLS["ka"] + 4], -1.0, 1.0, ALU.mult, ALU.add)

    sgused = [[], []]
    nst = [0]

    def shifted(which, j, dst, mucol, rows, dused):
        b = nst[0] % 2
        nst[0] += 1
        s = SG[b]
        p, after = pair()
        d = gemm(which, j, p[1], after, HH, HL, KT, H2, hm)
        ev = A.op(ae.activation, two(s[:, 1 + PAD:1 + TP]), p[1], ACT.Copy, after=[d] + sgused[b])
        free_pair(p, [ev])
        df = V.op(ve.tensor_tensor, dst[0:rows], s[0:rows, 0:TP], s[0:rows, 1:1 + TP], ALU.subtract,
                  after=[ev] + dused)
        m = V.op(ve.scalar_tensor_tensor, dst[0:rows], dst[0:rows], col("mu", mucol, 0, rows), s[0:rows, 1:1 + TP],
                 ALU.mult, ALU.add, after=[df])
        sgused[b] = [m]
        return m

    m = shifted("lora", 0, R1, 12, 64, [])
    lx1 = A.op(ae.activation, LX[0:32, :], R1[0:32, PAD:TP], ACT.Tanh, after=[m])
    lx2 = A.op(ae.activation, LX[32:64, :], R1[32:64, PAD:TP], ACT.Copy, after=[m])
    m = shifted("lora", 1, K1, 13, 96, [])
    xg = A.op(ae.activation, XG[:, :], K1[0:96, PAD:TP], ACT.Sigmoid, after=[m])
    used = {x: [] for x in ("R1", "K1", "SW", "SA", "CS", "KK", "EX")}
    used["R1"], used["K1"] = [lx1, lx2], [xg]
    feats, vmarks, bonm, wcm = [], [], [], []
    qm, km, vtm, vsu = [], [], [], []

    def ch(ap):
        return ap.rearrange("p (n t) -> p n t", t=64)

    def features(i, r1, k1m, vm):
        for dst, r0, bias, nm in ((SW, 0, "w0", "SW"), (SA, 32, "a0", "SA")):
            p, after = pair()
            T.wait(after + [lx1, lx2] + k2)
            for q in range(2):
                ins = te.matmul(p[1][:, q, :], LUP[r0:r0 + 32, 128 * i:128 * i + 128],
                                LX[r0:r0 + 32, 264 * q:264 * q + 264], start=True, stop=True)
            ins.then_inc(T.sem, 1)
            T.n += 1
            sg = A.op(ae.activation, two(dst[:, PAD:TP]), p[1], ACT.Sigmoid, bias=col(bias, i),
                      after=[(T.sem, T.n)] + used[nm])
            free_pair(p, [sg])
            if nm == "SW":
                sw = sg
            else:
                sa = sg
        yield
        cs = V.op(ve.tensor_tensor_scan, CS, RES[:, :], SW, 0.0, ALU.mult, ALU.add, after=[sw] + k2 + used["CS"])
        kk = V.op(ve.tensor_scalar, KK, K1, col("kk", i), None, ALU.mult, after=[k1m] + used["KK"])
        sq = A.op(ae.activation, EX, KK, ACT.Square, after=[kk] + used["EX"])
        p, after = pair()
        T.wait(after + [sq])
        pv = PS[:, p[0]:p[0] + 2, 0:288]
        for q in range(2):
            ins = te.matmul(pv[:, q, :], con("bones"), EX[:, 288 * q:288 * q + 288], start=True, stop=True)
        ins.then_inc(T.sem, 1)
        T.n += 1
        yield
        dcs = V.op(ve.tensor_tensor, SW, CS, SW, ALU.subtract, after=[cs])
        mxm = V.op(ve.tensor_scalar, two(EX), pv, 1e-24, None, ALU.max, after=[(T.sem, T.n)])
        free_pair(p, [mxm])
        sr = A.op(ae.activation, EX, EX, ACT.Sqrt, after=[mxm])
        rc = V.op(ve.reciprocal, EX, EX, after=[sr])
        yield
        kn = V.op(ve.tensor_tensor, KK, KK, EX, ALU.mult, after=[rc])
        e1 = A.op(ae.activation, EX, CS, ACT.Exp, scale=-KAPPA, after=[cs, kn])
        e1p = A.op(ae.activation, SW, SW, ACT.Exp, scale=-KAPPA, after=[dcs])
        f1 = V.op(ve.tensor_tensor, AR[:, i, :, 1, :], ch(R1), ch(EX), ALU.mult, after=[e1, r1])
        wc = V.op(ve.tensor_copy, WCC[:, i, :], ch(EX)[:, :, 63], after=[e1])
        wcm.append(wc)
        yield
        e2 = A.op(ae.activation, EX, CS, ACT.Exp, scale=KAPPA, after=[f1, wc])
        f2 = V.op(ve.scalar_tensor_tensor, AR[:, i, :, 0, :], ch(KK), -1.0, ch(SW), ALU.mult, ALU.mult,
                  after=[kn, e1p])
        bm = V.op(ve.tensor_tensor, KK, KK, SA, ALU.mult, after=[f2, sa])
        yield
        f3 = V.op(ve.tensor_tensor, BK[:, i, :, 0, :], ch(KK), ch(EX), ALU.mult, after=[bm, e2])
        tm = V.op(ve.tensor_scalar, SA, SA, col("ka", i), KAM[:, i:i + 1], ALU.mult, ALU.add, after=[bm, kam])
        kf = V.op(ve.tensor_tensor, K1, K1, SA, ALU.mult, after=[tm, kk])
        yield
        f4 = V.op(ve.tensor_tensor, BK[:, i, :, 1, :], ch(K1), ch(EX), ALU.mult, after=[kf, e2])
        bo = V.op(ve.scalar_tensor_tensor, K1[:, 64:TP], R1[:, 64:TP], col("rk", i), K1[:, 64:TP], ALU.mult,
                  ALU.mult, after=[kf, r1, f4])
        p, after = bank()
        mm = T.op(te.matmul, p.ap, con("bones"), K1[:, 64:TP], start=True, stop=True, after=after + [bo])
        yield
        t = TMP[i % 3][:, 0:512]
        bn = V.op(ve.tensor_tensor, t, VB[:, i, 128:64 + TP], p.ap, ALU.mult, after=[mm, vm] +
                  ([(s_bs, 16)] if i == 3 else []))
        p.free = [bn]
        S.wait([bn])
        se.dma_start(BSAVE[:, 512 * i:512 * i + 512], t).then_inc(s_bs, 16)
        bonm.append(bn)
        used.update({"R1": [f1, bo], "K1": [f4, mm], "SW": [f2], "SA": [kf], "CS": [e2, dcs], "KK": [f3], "EX": [f4]})
        feats.append([f1, f2, f3, f4])

    def attention_inputs(i):
        p, after = pair()
        d = yield from gemm_steps("w_in2", 12 + i, p[1], after, HH, HL, KT, H2, hm)
        A.op(ae.activation, QA[:, i, 0:248], p[1][:, 0, 16:264], ACT.Copy, scale=0.125, after=[d])
        m2 = A.op(ae.activation, QA[:, i, 248:512], p[1][:, 1, :], ACT.Copy, scale=0.125)
        free_pair(p, [m2])
        qm.append(m2)
        p, after = pair()
        d = yield from gemm_steps("w_in2", 16 + i, p[1], after, HH, HL, KT, H2, hm)
        m = A.op(ae.activation, two(KA[:, i, 112:640]), p[1], ACT.Copy, after=[d])
        free_pair(p, [m])
        km.append(m)
        p, after = pair()
        d = yield from gemm_steps("w_in2", 20 + i, p[1], after, HH, HL, KT, H2, hm)
        m = A.op(ae.activation, two(VS[:, 112:640]), p[1], ACT.Copy, after=[d] + vsu[-1:])
        free_pair(p, [m])
        yield
        p, after = bank()
        q, after2 = bank()
        T.wait(after + after2 + [m])
        for j in range(5):
            o = p.ap[:, 128 * j:128 * j + 128] if j < 4 else q.ap[:, 0:128]
            ins = te.transpose(o, VS[:, 128 * j:128 * j + 128], con("ident"))
        ins.then_inc(T.sem, 1)
        T.n += 1
        d = (T.sem, T.n)
        vsu.append(d)
        m1 = A.op(ae.activation, VT[:, 0:4, 128 * i:128 * i + 128], p.ap.rearrange("p (j t) -> p j t", j=4), ACT.Copy,
                  after=[d])
        m2 = A.op(ae.activation, VT[:, 4, 128 * i:128 * i + 128], q.ap[:, 0:128], ACT.Copy)
        p.free, q.free = [m1], [m2]
        vtm.extend([m1, m2])

    for i in range(4):
        r1 = shifted("w_in2", 3 * i, R1, i, 128, used["R1"])
        k1m = shifted("w_in2", 3 * i + 1, K1, 4 + i, 128, used["K1"])
        vm = shifted("w_in2", 3 * i + 2, VB[:, i, 64:64 + TP], 8 + i, 128, [])
        vmarks.append(vm)
        ai = attention_inputs(i)
        run(features(i, r1, k1m, vm), ai, ai, ai)
    proj_done = (T.sem, T.n)
    el.close()

    ck = ExitStack()
    ae.preload_act_table_set("natural_log_exp_and_others")
    V0 = sbuf("V0", [128, 8, 64], st=ck)
    SB = sbuf("SB", [128, 4, 2, 64], st=ck)
    RH = RAWS[:, 3584:3840].rearrange("p (u t) -> p u t", u=4)
    UP2 = [RAWS[:, 3840:4096].rearrange("p (u t) -> p u t", u=4), sbuf("UP", [128, 4, 64], st=ck)[:, :, :]]
    ATT = [RAWS[:, 1792 * i:1792 * i + 1792] for i in range(2)]
    BUF = []
    for i in range(2):
        o = 2112 * i
        BUF.append({"MM": XF[:, o:o + 1024].rearrange("p (h t) -> p h t", h=8),
                    "SV": XF[:, o + 1024:o + 1536].rearrange("p (h t) -> p h t", h=8),
                    "BKT": XF[:, o + 1536:o + 2048].rearrange("p (h t) -> p h t", h=8),
                    "XX": sbuf(f"RX{i}", [128, 4, 64], st=ck), "done": []})
    fall = flat(feats) + bonm + [(T.sem, T.n)]
    z1 = G.op(ge.memset, V0[0:64, :, :], 0.0, after=fall)
    z2 = G.op(ge.memset, SB[:, :, :, :], 0.0)
    inv = [Inverse(ck, f"rv{i}") for i in range(2)]
    rws = {"sm": [z2], "v0": []}
    y_marks = []
    A.wait(fall)
    V.wait([z1])

    def rw_prepare(n):
        B = BUF[n % 2]
        UP = UP2[n % 2]
        MM, SV, BKT = B["MM"], B["SV"], B["BKT"]
        old = B["done"]
        b0, after0 = bank()
        b1, after1 = bank()
        T.wait(after0 + after1 + flat(feats) + [z1])
        for h in range(8):
            i, par = divmod(h, 2)
            pb = 64 * par
            ins = te.matmul((b0, b1)[par].ap[:, 128 * i:128 * i + 128],
                            BK[pb:pb + 64, i, n, :, :].rearrange("p a t -> p (a t)"),
                            AR[pb:pb + 64, i, n, :, :].rearrange("p a t -> p (a t)"), start=True, stop=True)
        ins.then_inc(T.sem, 1)
        T.n += 1
        d = (T.sem, T.n)
        M2 = MM.rearrange("p (i a) t -> p i a t", a=2)
        mms = []
        for par in range(2):
            p = (b0, b1)[par]
            m = V.op(ve.tensor_tensor, M2[:, :, par, :], p.ap.rearrange("p (i t) -> p i t", i=4),
                     con("m4").unsqueeze(1).broadcast_to([128, 4, 128]), ALU.mult, after=[d] + old)
            p.free = [m]
            mms.append(m)
        B["mm"] = mms
        yield
        p, after = bank()
        T.wait(after)
        for par, q in enumerate(HALF):
            for i in range(4):
                ins = te.matmul(p.ap[q, 64 * i:64 * i + 64], BK[q, i, n, 0, :], AR[q, i, n, 0, :], start=True,
                                stop=True)
        ins.then_inc(T.sem, 1)
        T.n += 1
        um = V.op(ve.tensor_tensor, UP, p.ap[:, 0:256].rearrange("p (i t) -> p i t", i=4),
                  bc(con("m4")[:, 0:64], 4), ALU.mult, after=[(T.sem, T.n)] + inv[n % 2].done)
        p.free = [um]
        yield
        pk, after1 = bank()
        pv, after2 = bank()
        T.wait(after1 + after2 + vmarks)
        for i in range(4):
            te.transpose(pk.ap[:, 128 * i:128 * i + 128], BK[:, i, n, :, :].rearrange("p a t -> p (a t)"),
                         con("ident"))
            ins = te.transpose(pv.ap[:, 128 * i:128 * i + 128], VB[:, i, 64 * n:64 * n + 128], con("ident"))
        ins.then_inc(T.sem, 1)
        T.n += 1
        d = (T.sem, T.n)
        bt = A.op(ae.activation, BKT, pk.ap.rearrange("p (h t) -> p h t", h=8), ACT.Copy, after=[d] + old)
        v1 = A.op(ae.activation, SV[64:128], pv.ap[64:128, :].rearrange("p (h t) -> p h t", h=8), ACT.Copy, after=old)
        pk.free, pv.free = [bt], [v1]
        B["tok"] = [bt, v1]
        yield
        B["x"] = yield from invert(inv[n % 2], UP, [um], B["XX"][:, :, :], old)

    def rw_scan(n):
        B = BUF[n % 2]
        MM, SV, BKT = B["MM"], B["SV"], B["BKT"]
        v0 = G.op(ge.tensor_copy, V0[64:128, :, :], SV[64:128], after=B["tok"] + rws["v0"] + [(G.sem, G.n)])
        p, after = bank()
        T.wait(after + rws["sm"] + [v0] + B["mm"])
        for i in range(4):
            for par, q in enumerate(HALF):
                te.matmul(p.ap[q, 64 * i:64 * i + 64], AR[:, i, n, 0, :], SB[:, i, par, :], start=True, stop=False)
                ins = te.matmul(p.ap[q, 64 * i:64 * i + 64], MM[:, 2 * i + par, 0:64], V0[:, 2 * i + par, :],
                                start=False, stop=True)
        ins.then_inc(T.sem, 1)
        T.n += 1
        d = (T.sem, T.n)
        rws["v0"] = [d]
        rh = V.op(ve.tensor_copy, RH, p.ap[:, 0:256].rearrange("p (i t) -> p i t", i=4), after=[d])
        p.free = [rh]
        yield
        p, after = bank()
        p2, after2 = bank()
        T.wait(after + after2 + [rh, B["x"]])
        for i in range(4):
            for q, o in zip(HALF, (p, p2)):
                ins = te.matmul(o.ap[0:64, 64 * i:64 * i + 64], B["XX"][q, i, :], RH[q, i, :], start=True, stop=True)
        ins.then_inc(T.sem, 1)
        T.n += 1
        d = (T.sem, T.n)
        S2 = SV.rearrange("p (i a) t -> p i a t", a=2)
        q4 = lambda o: o.ap[0:64, 0:256].rearrange("p (i t) -> p i t", i=4)
        sa = A.op(ae.activation, S2[0:64, :, 0, :], q4(p), ACT.Copy, after=[d])
        sv = V.op(ve.tensor_copy, S2[0:64, :, 1, :], q4(p2), after=[d])
        p.free, p2.free = [sa], [sv]
        yield
        p, after = bank()
        T.wait(after + B["tok"] + [sa, sv])
        for h in range(8):
            i, par = divmod(h, 2)
            ins = te.matmul(p.ap[64 * par:64 * par + 64, 64 * i:64 * i + 64], BKT[:, h, :], SV[:, h, :],
                            start=True, stop=True)
        ins.then_inc(T.sem, 1)
        T.n += 1
        sd = (T.sem, T.n)
        yd = sd
        if n:
            p2, after = bank()
            T.wait(after)
            for i in range(4):
                te.matmul(p2.ap[:, 64 * i:64 * i + 64], SB[:, i, :, :].rearrange("p a t -> p (a t)"),
                          AR[:, i, n, 1, :], start=True, stop=True)
                for par in range(2):
                    h = 2 * i + par
                    ins = te.matmul(p2.ap[64 * par:64 * par + 64, 64 * i:64 * i + 64], SV[:, h, :], MM[:, h, 64:128],
                                    start=False, stop=True, skip_group_check=True)
            ins.then_inc(T.sem, 1)
            T.n += 1
            yd = (T.sem, T.n)
            ym = A.op(ae.activation, AR[:, :, n, 1, :], p2.ap[:, 0:256].rearrange("p (i t) -> p i t", i=4),
                      ACT.Copy, after=[yd])
            p2.free = [ym]
            y_marks.append(ym)
        sm = []
        for par in range(2):
            q = slice(64 * par, 64 * par + 64)
            pp = p.ap[q, 0:256].rearrange("p (i t) -> p i t", i=4)
            s1 = V.op(ve.tensor_tensor, SB[q, :, par, :], pp, SB[q, :, par, :], ALU.add, after=[sd, yd])
            sm.append(V.op(ve.tensor_tensor, SB[q, :, par, :], SB[q, :, par, :],
                           WCC[q, :, n:n + 1].broadcast_to([64, 4, 64]), ALU.mult, after=[s1] + wcm))
        p.free = [s1]
        rws["sm"] = sm
        B["done"] = [yd, v0]
        yield

    def rwkv():
        yield from pipeline(NCH, rw_prepare, rw_scan)

    OFF = [0, 512, 1024, 1408, 1664]
    LEN = [512, 512, 384, 256, 128]
    flatr = lambda t, a: t[:, a:a + 4, :].rearrange("p k t -> p (k t)")
    KHI = [flatr(HH, 0), flatr(HH, 4)]
    KLO = [flatr(HL, 0), flatr(HL, 4)]
    TT = [[TMP[0], TMP[1]], [TMP[2], RSTD]]
    ttu = [[[(s_bs, 64)], [(s_bs, 64)]], [[(s_bs, 64)], [(s_bs, 64)]]]
    khu = [[proj_done], [proj_done]]
    atu = [[], []]
    sbm = [None] * 8

    def heads(b):
        nt = 0
        for i in range(4):
            h = 2 * i + b
            pb = 64 * b
            am = []
            for j in (4, 3, 2, 1, 0):
                n = LEN[j]
                p, after = bank()
                T.wait(after + qm + km)
                z = T.op(te.matmul, p.ap[:, 0:n], KA[pb:pb + 64, i, 128 * j:128 * j + 128],
                         QA[pb:pb + 64, i, 512 - n:512], start=True, stop=True)
                t = TT[b][nt % 2]
                a1 = A.op(ae.activation, t[:, 0:n], p.ap[:, 0:n], ACT.Abs, after=[z] + ttu[b][nt % 2])
                a2 = A.op(ae.activation, t[:, 0:n], t[:, 0:n], ACT.Exp, scale=-1.0, after=[a1])
                a3 = A.op(ae.activation, t[:, 0:n], t[:, 0:n], ACT.Ln, bias=1.0, after=[a2])
                yield
                m = V.op(ve.scalar_tensor_tensor, t[:, 0:n], p.ap[:, 0:n], 0.0, t[:, 0:n], ALU.max, ALU.add,
                         after=[a3])
                if j:
                    m = G.op(ge.affine_select, out=t[:, 0:128], in_=t[:, 0:128], pattern=[[1, 128]],
                             compare_op=ALU.is_gt, fill=0.0, base=0, channel_multiplier=-1,
                             after=[m, (G.sem, G.n)])
                else:
                    m = V.op(ve.tensor_scalar, t[:, 0:n], t[:, 0:n], PM[:, 0:1], None, ALU.mult, after=[m, pmk])
                yield
                o = slice(OFF[j], OFF[j] + n)
                hi = A.op(ae.activation, KHI[b][:, o], t[:, 0:n], ACT.Copy, scale=-1.0, after=[m] + khu[b])
                lo = V.op(ve.scalar_tensor_tensor, KLO[b][:, o], t[:, 0:n], -1.0, KHI[b][:, o].bitcast(f32), ALU.mult,
                          ALU.subtract, after=[hi, m] + khu[b])
                ttu[b][nt % 2] = [lo, hi]
                nt += 1
                yield
                T.wait([hi, lo])
                for q in range(4, j - 1, -1):
                    w = TRIR if q == j else ONER
                    for part in (KHI[b], KLO[b]):
                        ins = te.matmul(p.ap[:, n - LEN[q]:n], w[:, :], part[:, OFF[q]:OFF[q] + LEN[q]], start=False,
                                        stop=True, skip_group_check=True)
                ins.then_inc(T.sem, 1)
                T.n += 1
                d = (T.sem, T.n)
                yield
                e = A.op(ae.activation, ATT[b][:, o], p.ap[:, 0:n], ACT.Exp, after=[d] + atu[b])
                p.free = [e]
                if j:
                    e = G.op(ge.affine_select, out=ATT[b][:, OFF[j]:OFF[j] + 128], in_=ATT[b][:, OFF[j]:OFF[j] + 128],
                             pattern=[[1, 128]], compare_op=ALU.is_gt, fill=0.0, base=0, channel_multiplier=-1,
                             after=[e, (G.sem, G.n)])
                am.append(e)
                yield
            khu[b] = [d]
            p, after = bank()
            T.wait(after + am + vtm)
            for j in range(5):
                ins = te.matmul(p.ap[pb:pb + 64, 512 - LEN[j]:512], VT[:, j, 64 * h:64 * h + 64],
                                ATT[b][:, OFF[j]:OFF[j] + LEN[j]], start=(j == 0), stop=(j == 4))
            ins.then_inc(T.sem, 1)
            T.n += 1
            d = (T.sem, T.n)
            atu[b] = [d]
            sbm[h] = A.op(ae.activation, QA[pb:pb + 64, i, :], p.ap[pb:pb + 64, :], ACT.Copy, after=[d])
            p.free = [sbm[h]]
            yield

    cat = [None] * 8

    def later_by(n, g):
        for _ in range(n):
            yield
        yield from g

    def attention_parts():
        while sbm[6] is None or sbm[7] is None:
            yield
        for j in range(4):
            hi = A.op(ae.activation, HH[:, j, NM:T2], QA[:, j, :], ACT.Copy, after=[sbm[2 * j], sbm[2 * j + 1]] + khu[0])
            yield
            lo = V.op(ve.tensor_tensor, HL[:, j, NM:T2], QA[:, j, :], HH[:, j, NM:T2].bitcast(f32), ALU.subtract,
                      after=[hi])
            cat[j] = [hi, lo]

    rk = rwkv()
    run(rk, heads(0), rk, later_by(2, heads(1)), attention_parts())
    ck.close()

    resume()
    alldone = [(e.sem, e.n) for e in (V, A, G, T)]
    S.wait(alldone)
    se.dma_start(X[:, :, NM:T2], XSAVE.rearrange("p (k t) -> p k t", k=KT)).then_inc(s_xs, 16)
    xback = [(s_xs, 32)]
    BON = sbuf("BON", [128, 4, 512], st=rw)
    se.dma_start(BON[:, :, :].rearrange("p k t -> p (k t)"), BSAVE).then_inc(s_bs, 16)
    bback = [(s_bs, 80)]
    EPL = sbuf("EPL", [128, 1], st=rw)
    TL = [sbuf(f"TL{i}", [128, 512], st=rw) for i in range(8)]
    epl = G.op(ge.memset, EPL[:, :], 64e-5, after=alldone)
    A.wait(alldone)
    V.wait(alldone)
    def group_norm(i):
        y3 = AR[:, i, 1:NCH, 1, :]
        pp, after = bank()
        T.wait(after + y_marks)
        mm = T.op(te.matmul, pp.ap, con("bones"), y3, start=True, stop=True)
        yield
        t, sq = TL[2 * i], TL[2 * i + 1]
        c = V.op(ve.scalar_tensor_tensor, ch(t[:, :]), ch(pp.ap), -1.0 / 64, y3, ALU.mult, ALU.add,
                 after=[mm])
        pp.free = [c]
        s2 = A.op(ae.activation, sq[:, :], t[:, :], ACT.Square, after=[c])
        yield
        pp, after = bank()
        mm = T.op(te.matmul, pp.ap, con("bones"), sq[:, :], start=True, stop=True, after=after + [s2])
        yield
        r1, r = rsqrt(sq[:, :], pp.ap, 1.0 / 64, EPL[:, 0:1], [mm, epl])
        pp.free = [r1]
        yield
        m = V.op(ve.tensor_tensor, t[:, :], t[:, :], sq[:, :], ALU.mult, after=[r])
        m = V.op(ve.tensor_scalar, t[:, :], t[:, :], col("lnw", i), col("lnb", i), ALU.mult, ALU.add, after=[m])
        m = V.op(ve.tensor_tensor, t[:, :], BON[:, i, :], t[:, :], ALU.add, after=[m] + bback)
        yield
        pp, after = bank()
        mm = T.op(te.matmul, pp.ap, GUP[0:96, 128 * i:128 * i + 128], XG[0:96, NM:T2], start=True, stop=True,
                  after=after + [xg])
        m = V.op(ve.tensor_tensor, t[:, :], t[:, :], pp.ap, ALU.mult, after=[mm, m])
        pp.free = [m]
        hi = A.op(ae.activation, HH[:, 4 + i, NM:T2], t[:, :], ACT.Copy, after=[m])
        lo = V.op(ve.tensor_tensor, HL[:, 4 + i, NM:T2], t[:, :], HH[:, 4 + i, NM:T2].bitcast(f32),
                  ALU.subtract, after=[hi])
        cat[4 + i] = [hi, lo]

    first = [bank() for _ in range(2)]
    gens = [gemm_steps("w_out2", i, p.ap, after, HH, HL, KT, H1, cat) for i, (p, after) in enumerate(first)]

    def attention_half():
        yield
        yield
        for _ in range(4):
            for g in gens:
                next(g)
            yield

    run(*(group_norm(i) for i in range(4)), attention_half())
    xn = []
    for m in range(8):
        if m == 0:
            ps, ds = first, together(gens)
        if m < 2:
            p, d = ps[m][0], ds[m]
        else:
            p, after = bank()
            d = gemm("w_out2", m, p.ap, after, HH, HL, KT, H1, cat)
        xn.append([V.op(ve.tensor_tensor, X[:, m, NM:T2], p.ap, X[:, m, NM:T2], ALU.add, after=[d] + xback)])
        p.free = [xn[-1][0]]
        if m == 0:
            stats = Stats(NM, alldone)
        else:
            stats.sum(m - 1)
        stats.square(m, xn[-1])
    rw.close()
    hm = rms(CV[:, COLS["ffn2"]:COLS["ffn2"] + 8], None, NM, xn, [d] + flat(cat), st=stats)
    xm, d, stats = ffn("f2", hm, NM, fin2(NM), NM)
    xm = rms(CV[:, COLS["final"]:COLS["final"] + 8], None, NM, xm, [d], dst=X, st=stats)

    s_out = sem("s_out")
    S.wait(flat(xm))
    se.dma_start(out.rearrange("(k p) t -> p k t", p=128), X[:, :, NM:T2]).then_inc(s_out, 16)
    se.wait_ge(s_out, 16)
    top.close()


def host(inputs):
    import numpy as np
    g = {k: np.asarray(v) for k, v in inputs.items()}
    z = lambda *s: np.zeros(s, np.float32)

    def cv(v):
        v = v.reshape(-1)
        n = -(-v.size // 128)
        o = z(n * 128)
        o[:v.size] = v
        return o.reshape(n, 128).T

    mu = g["rwkv_mu_2"][0]
    cat = [g["c"], g["b_ada"], g["norm1_w"], g["conv_qkv_w"], g["conv_short_w"], g["gdn_norm_w"], g["norm2_w"],
           g["norm_f_w"], g["ffn1_norm_2"], g["mix_norm_2"], (mu[:1536], mu[1536:1600], mu[1600:]), g["rwkv_w0_2"],
           g["rwkv_a0_2"], g["rwkv_k_k_2"], g["rwkv_k_a_2"], g["rwkv_r_k_2"], g["rwkv_lnx_w_2"], g["rwkv_lnx_b_2"],
           g["ffn2_norm_2"], g["final_norm_2"], g["A_log"], g["dt_bias"]]
    cols = np.concatenate([np.concatenate([cv(x) for x in v], 1) if isinstance(v, tuple) else cv(v) for v in cat], 1)
    assert cols.shape[1] == NCOL, cols.shape

    con = z(128, sum(NCON))

    def put(n, v):
        g_, a, k = CON[n]
        a += sum(NCON[:g_])
        con[:v.shape[0], a:a + k] = v

    i = np.arange(128)
    s, t = i[:, None], i[None, :]
    put("ident", (s == t) * np.float32(1))
    put("ones", np.ones((128, 128), np.float32))
    put("bones", (s // 64 == t // 64) * np.float32(1))
    put("tri", (s >= t) * np.float32(1))
    put("m4", np.where(t < 64, s % 64 < t % 64, s % 64 <= t % 64) * np.float32(1))
    put("i2", (s % 64 == t[:, :64]) * np.float32(1))
    s, t = s % 64, t[:, :64]
    put("b16", (s // 16 == t // 16) * np.float32(1))
    c32 = ((s // 32 == t // 32) & (s // 16 != t // 16)) * np.float32(1)
    c64 = (s // 32 != t // 32) * np.float32(1)
    put("c32", c32)
    put("c64", c64)
    put("madd", np.where(s <= t, 0, -1e30).astype(np.float32))
    put("nstrict", np.where(s < t, -1, 0).astype(np.float32))
    put("reset1", np.broadcast_to((np.arange(512) % 64 != 0) * np.float32(1), (128, 512)))
    put("reset2", np.broadcast_to((np.arange(TP) % 64 != 0) * np.float32(1), (128, TP)))
    sel = z(64, 8, 128)
    for h in range(4):
        sel[h, h] = 1
        sel[32 + h, 4 + h] = 1
    put("sel", sel.reshape(64, 1024))

    def tiles(w):
        K, M = w.shape
        return np.ascontiguousarray(w.reshape(K // 128, 128, M // 128, 128).transpose(2, 1, 0, 3)).reshape(M // 128, 128, -1)

    def down(w):
        o = z(24, 128, 1024)
        a = tiles(w)
        for m in range(8):
            o[3 * m] = a[m][:, :1024]
            o[3 * m + 1] = a[m][:, 1024:2048]
            o[3 * m + 2, :, :768] = a[m][:, 2048:]
        return o

    w_in = g["w_in"][0]
    ab = z(1024, 64)
    ab[:, 0:4] = w_in[:, 2048:2052]
    ab[:, 32:36] = w_in[:, 2052:2056]
    sb, sc, sh = (tiles(w_in[:, 2056 + 512 * i:2568 + 512 * i]) for i in range(3))
    w = {"ada": np.ascontiguousarray(g["w_ada"][0].reshape(8, 128, 6, 1024).transpose(2, 0, 1, 3)).reshape(48, 128, 1024),
         "ab": np.ascontiguousarray(ab.reshape(8, 128, 64).transpose(1, 0, 2)).reshape(1, 128, 512),
         "w_in": np.concatenate([tiles(w_in[:, :2048]), np.stack([sc, sh, sb], 1).reshape(12, 128, 1024)], 0),
         "w_out": tiles(g["w_out"][0])}
    v = g["w_in_2"][0]
    lo = z(1024, 256)
    lo[:, 0:64] = v[:, 3072:3136]
    lo[:, 128:224] = v[:, 3136:3232]
    r, k, vv = (tiles(v[:, 1536 + 512 * i:2048 + 512 * i]) for i in range(3))
    w["lora"] = tiles(lo)
    w["w_in2"] = np.concatenate([np.stack([r, k, vv], 1).reshape(12, 128, 1024), tiles(v[:, :1536])], 0)
    w["w_out2"] = tiles(g["w_out_2"][0])
    for f, pre in (("f0", ""), ("f1", "ffn1_"), ("f2", "ffn2_")):
        post = "_2" if pre else ""
        w[f + "g"] = tiles(g[pre + "w_gate" + post][0])
        w[f + "u"] = tiles(g[pre + "w_up" + post][0])
        w[f + "d"] = down(g[pre + "w_down" + post][0])
    arrays = {"xT": np.ascontiguousarray(g["x"][0].T), "metaT": np.ascontiguousarray(g["meta_tokens_2"].T),
              "cols": np.ascontiguousarray(cols), "consts": con}
    arrays["lup"] = np.ascontiguousarray(np.concatenate([g["rwkv_w_up_2"][0], g["rwkv_a_up_2"][0]], 0))
    arrays["gup"] = np.ascontiguousarray(g["rwkv_g_up_2"][0])
    for n, a in w.items():
        arrays["w_" + n] = a
    return arrays


def kernel(**inputs):
    import numpy as _np
    import concourse.bacc as _bacc
    from concourse import mybir as _mybir
    from concourse.bass_utils import run_bass_kernel_spmd as _run

    arrays = host(inputs)
    nc = _bacc.Bacc("TRN2", target_bir_lowering=False, num_devices=1)
    f32 = _mybir.dt.float32
    ap = {n: nc.dram_tensor(n, a.shape, f32, kind="ExternalInput").ap() for n, a in arrays.items()}
    out = nc.dram_tensor("out", (D, T1), f32, kind="ExternalOutput").ap()
    slabs = {n[2:]: a for n, a in ap.items() if n.startswith("w_")}
    program(nc, ap["xT"], ap["metaT"], ap["cols"], ap["consts"], slabs, ap["lup"], ap["gup"], out)
    r = _run(nc, [arrays], core_ids=[0])
    return _np.ascontiguousarray(r.results[0]["out"].T)[None]
```
